# Optimizing a Trainium2 kernel written in Bass

```python
import functools
import jax
import jax.numpy as jnp
from jax import lax
import numpy as np

D_MODEL = 1024
BATCH = 1
SEQ = 1024
DEPTH = 1
DEC_BATCH = 8
DEC_SEQ = 4
PAST_LEN = 4096
PAGE_SIZE = 128

HEAD_DIM = 64
N_ATTN_HEADS = 8
N_MLSTM_HEADS = 4
N_HGRN_HEADS = 4
ATTN_WIDTH = N_ATTN_HEADS * HEAD_DIM
MLSTM_WIDTH = N_MLSTM_HEADS * HEAD_DIM
HGRN_WIDTH = N_HGRN_HEADS * HEAD_DIM
MIX_WIDTH = ATTN_WIDTH + MLSTM_WIDTH + HGRN_WIDTH
PROJ_SPLITS = (ATTN_WIDTH, ATTN_WIDTH, ATTN_WIDTH,
               MLSTM_WIDTH, MLSTM_WIDTH, MLSTM_WIDTH, MLSTM_WIDTH, N_MLSTM_HEADS, N_MLSTM_HEADS,
               HGRN_WIDTH, HGRN_WIDTH, HGRN_WIDTH, HGRN_WIDTH)
PROJ_WIDTH = 3 * ATTN_WIDTH + 4 * MLSTM_WIDTH + 2 * N_MLSTM_HEADS + 4 * HGRN_WIDTH
DILATED_PATTERNS = ((128, 1), (512, 4), (2048, 16))
MAX_WINDOW = 2048
QBLOCK = 128
N_REL_BUCKETS = 32
REL_MAX_DISTANCE = 2048
CONV_WIDTH = 4
MLSTM_CHUNK = 64
HGRN_CHUNK = 64
D_FF = 4 * D_MODEL
EPS = 1e-6
NEG_BIG = -1e30

kernel_name = 'hymba_dilated_mlstm_hgrn2_step'

def rmsnorm(x, g):
    xf = x.astype(jnp.float32)
    y = xf * lax.rsqrt(jnp.mean(xf * xf, axis=-1, keepdims=True) + EPS)
    return (y * g.astype(jnp.float32)).astype(x.dtype)

def head_rmsnorm(h, g):
    y = h * lax.rsqrt(jnp.mean(h * h, axis=-1, keepdims=True) + EPS)
    return y * g.astype(jnp.float32).reshape(h.shape[-2:])

def t5_causal_bucket(dist):
    n = np.asarray(dist).astype(np.int32)
    max_exact = N_REL_BUCKETS // 2
    scaled = np.log(np.maximum(n, 1) / max_exact) / np.log(REL_MAX_DISTANCE / max_exact)
    large = np.minimum(max_exact + (scaled * (N_REL_BUCKETS - max_exact)).astype(np.int32), N_REL_BUCKETS - 1)
    return np.where(n < max_exact, n, large).astype(np.int32)

def dilated_branch_prompt(q, k, v, rel_bias, window, dilation):
    B, S, H, E = q.shape
    ls = S // dilation
    nsub = window // dilation
    nb = -(-ls // QBLOCK)
    lp = nb * QBLOCK

    def to_blocks(t):
        t = jnp.swapaxes(t.reshape(B, ls, dilation, H, E), 1, 2)
        t = jnp.pad(t, ((0, 0), (0, 0), (0, lp - ls), (0, 0), (0, 0)))
        return t.reshape(B, dilation, nb, QBLOCK, H, E)

    def with_prev(t):
        prev = jnp.pad(t, ((0, 0), (0, 0), (1, 0), (0, 0), (0, 0), (0, 0)))[:, :, :-1]
        return jnp.concatenate([prev, t], axis=3)

    def from_blocks(t):
        t = t.reshape((B, dilation, lp) + t.shape[4:])[:, :, :ls]
        t = jnp.swapaxes(t, 1, 2)
        return t.reshape((B, S) + t.shape[3:])

    qb = to_blocks(q)
    kk = with_prev(to_blocks(k))
    vv = with_prev(to_blocks(v))
    s = jnp.einsum('brnqhe,brnkhe->brnhqk', qb, kk, preferred_element_type=jnp.float32) * E ** -0.5
    a = np.arange(QBLOCK)[:, None]
    b = np.arange(2 * QBLOCK)[None, :]
    rel = QBLOCK + a - b
    band = (rel >= 0) & (rel <= nsub)
    bias = jnp.transpose(rel_bias.astype(jnp.float32)[t5_causal_bucket(np.clip(rel, 0, None) * dilation)], (2, 0, 1))
    first = (np.arange(nb) == 0)[:, None, None]
    valid = band[None] & ~(first & (b < QBLOCK)[None])
    s = jnp.where(valid[None, None, :, None], s + bias, NEG_BIG)
    m = jnp.max(s, axis=-1, keepdims=True)
    p = jnp.exp(s - m)
    l = jnp.sum(p, axis=-1, keepdims=True)
    o = jnp.einsum('brnhqk,brnkhe->brnqhe', p, vv.astype(jnp.float32)) / jnp.transpose(l, (0, 1, 2, 4, 3, 5))
    lse = jnp.transpose((m + jnp.log(l))[..., 0], (0, 1, 2, 4, 3))
    return from_blocks(o), from_blocks(lse)

def dilated_branch_sample(q, k_all, v_all, rel_bias, window, dilation, n_past):
    T, E = q.shape[1], q.shape[3]
    j = np.arange(window // dilation + 1)
    idx = n_past + np.arange(T)[:, None] - dilation * j[None, :]
    valid = idx >= 0
    idx = np.maximum(idx, 0)
    kg = k_all[:, idx]
    vg = v_all[:, idx]
    s = jnp.einsum('bthe,btjhe->bhtj', q, kg, preferred_element_type=jnp.float32) * E ** -0.5
    bias = rel_bias.astype(jnp.float32)[t5_causal_bucket(dilation * j)].T
    s = jnp.where(valid[None, None], s + bias[:, None, :], NEG_BIG)
    m = jnp.max(s, axis=-1, keepdims=True)
    p = jnp.exp(s - m)
    l = jnp.sum(p, axis=-1, keepdims=True)
    o = jnp.einsum('bhtj,btjhe->bthe', p, vg.astype(jnp.float32)) / jnp.swapaxes(l, 1, 2)
    lse = jnp.swapaxes((m + jnp.log(l))[..., 0], 1, 2)
    return o, lse

def dilated_mixture(branches):
    outs = jnp.stack([o for o, _ in branches])
    w = jax.nn.softmax(jnp.stack([lse for _, lse in branches]), axis=0)
    return jnp.sum(w[..., None] * outs, axis=0)

def attn_prompt(q, k, v, rel_bias):
    return dilated_mixture([dilated_branch_prompt(q, k, v, rel_bias, w, d) for w, d in DILATED_PATTERNS])

def attn_sample(q, k, v, rel_bias, k_buf, v_buf):
    n_past = k_buf.shape[1]
    k_all = jnp.concatenate([k_buf.astype(k.dtype), k], axis=1)
    v_all = jnp.concatenate([v_buf.astype(v.dtype), v], axis=1)
    return dilated_mixture([dilated_branch_sample(q, k_all, v_all, rel_bias, w, d, n_past) for w, d in DILATED_PATTERNS])

def causal_conv(x, buf, w):
    S = x.shape[1]
    xp = jnp.concatenate([buf.astype(x.dtype), x], axis=1)
    y = xp[:, :S] * w[0]
    for j in range(1, CONV_WIDTH):
        y = y + xp[:, j:j + S] * w[j]
    return y, xp[:, S:]

def _chunk_len(S, C):
    return C if S % C == 0 else S

def _to_chunks(t, L):
    B, S = t.shape[:2]
    t = t.reshape((B, S // L, L) + t.shape[2:])
    return jnp.moveaxis(jnp.moveaxis(t, 1, 0), 3, 2)

def _from_chunks(t):
    nc, B, H, L, E = t.shape
    return jnp.transpose(t, (1, 0, 3, 2, 4)).reshape(B, nc * L, H, E)

def mlstm_chunked(q, k, v, ig, lf, C0, n0, m0):
    S = q.shape[1]
    L = _chunk_len(S, MLSTM_CHUNK)
    causal = np.tril(np.ones((L, L), dtype=bool))

    def step(carry, xs):
        C, n, m = carry
        qc, kc, vc, ic, fc = xs
        b = jnp.cumsum(fc, axis=-1)
        D = jnp.where(causal, b[..., :, None] - b[..., None, :] + ic[..., None, :], NEG_BIG)
        inter = b + m[..., None]
        mt = jnp.maximum(jnp.max(D, axis=-1), inter)
        wts = jnp.exp(D - mt[..., None]) * jnp.einsum('bhte,bhse->bhts', qc, kc)
        g = jnp.exp(inter - mt)
        num = jnp.einsum('bhts,bhse->bhte', wts, vc) + g[..., None] * jnp.einsum('bhte,bhef->bhtf', qc, C)
        den = jnp.sum(wts, axis=-1) + g * jnp.einsum('bhte,bhe->bht', qc, n)
        h = num / jnp.maximum(jnp.abs(den), jnp.exp(-mt))[..., None]
        mL = mt[..., -1]
        decay = jnp.exp(b[..., -1:] - b + ic - mL[..., None])
        gL = g[..., -1]
        C = gL[..., None, None] * C + jnp.einsum('bhs,bhse,bhsf->bhef', decay, kc, vc)
        n = gL[..., None] * n + jnp.einsum('bhs,bhse->bhe', decay, kc)
        return (C, n, mL), h

    xs = (_to_chunks(q, L), _to_chunks(k, L), _to_chunks(v, L), _to_chunks(ig, L), _to_chunks(lf, L))
    (C, n, m), h = lax.scan(step, (C0, n0, m0), xs)
    return _from_chunks(h), C, n, m

def hgrn2_chunked(q, k, log_f, i, S0):
    S = q.shape[1]
    L = _chunk_len(S, HGRN_CHUNK)
    causal = np.tril(np.ones((L, L), dtype=bool))

    def step(St, xs):
        qc, kc, fc, ic = xs
        b = jnp.cumsum(fc, axis=2)
        diff = b[:, :, :, None, :] - b[:, :, None, :, :]
        dec = jnp.exp(jnp.where(causal[:, :, None], diff, NEG_BIG))
        A = jnp.einsum('bhtk,bhsk,bhtsk->bhts', qc, kc, dec)
        o = jnp.einsum('bhts,bhsv->bhtv', A, ic) + jnp.einsum('bhtk,bhkv->bhtv', qc * jnp.exp(b), St)
        bL = b[:, :, -1:, :]
        St = jnp.exp(bL[:, :, 0])[..., None] * St + jnp.einsum('bhsk,bhsv->bhkv', kc * jnp.exp(bL - b), ic)
        return St, o

    xs = (_to_chunks(q, L), _to_chunks(k, L), _to_chunks(log_f, L), _to_chunks(i, L))
    St, o = lax.scan(step, S0, xs)
    return _from_chunks(o), St

def trunk_layer(x, attn_fn, conv_buf, C0, n0, m0, S0,
                g_mix, w_in, gate_b, conv_w, mlstm_g, lb, hgrn_g, w_out, g_ffn, w_up, w_down):
    f32 = jnp.float32
    B, S, _ = x.shape

    def heads(t):
        return t.reshape(B, S, -1, HEAD_DIM)

    z = rmsnorm(x, g_mix) @ w_in
    cuts = [int(c) for c in np.cumsum(PROJ_SPLITS)[:-1]]
    (aq, ak, av, mq, mk, mv, mo, mi, mf, hq, hf, hi, hg) = jnp.split(z, cuts, axis=-1)
    ak, av = heads(ak), heads(av)
    attn_out = attn_fn(heads(aq), ak, av)
    qk, conv_new = causal_conv(jnp.concatenate([mq, mk], axis=-1), conv_buf, conv_w)
    qk = jax.nn.silu(qk.astype(f32))
    ig = mi.astype(f32) + gate_b[0].astype(f32)
    lf = jax.nn.log_sigmoid(mf.astype(f32) + gate_b[1].astype(f32))
    h_m, C, n, m = mlstm_chunked(heads(qk[..., :MLSTM_WIDTH]), heads(qk[..., MLSTM_WIDTH:]) * HEAD_DIM ** -0.5,
                                 heads(mv).astype(f32), ig, lf, C0.astype(f32), n0.astype(f32), m0.astype(f32))
    mlstm_out = jax.nn.sigmoid(heads(mo).astype(f32)) * head_rmsnorm(h_m, mlstm_g)
    lbh = lb.reshape(N_HGRN_HEADS, HEAD_DIM)
    fpre = heads(hf).astype(f32)
    f_gate = lbh + (1.0 - lbh) * jax.nn.sigmoid(fpre)
    log_f = jnp.log(f_gate)
    k_h = 1.0 - f_gate
    h_h, S_new = hgrn2_chunked(jax.nn.silu(heads(hq).astype(f32)), k_h, log_f, heads(hi).astype(f32), S0.astype(f32))
    hgrn_out = jax.nn.sigmoid(heads(hg).astype(f32)) * head_rmsnorm(h_h, hgrn_g)
    mix = jnp.concatenate([attn_out.reshape(B, S, ATTN_WIDTH), mlstm_out.reshape(B, S, MLSTM_WIDTH),
                           hgrn_out.reshape(B, S, HGRN_WIDTH)], axis=-1)
    x = x + mix.astype(x.dtype) @ w_out
    u = rmsnorm(x, g_ffn) @ w_up
    x = x + jnp.square(jax.nn.relu(u)) @ w_down
    return x, (ak, av, conv_new, C, n, m, S_new)

def setup_inputs(seed: int = 0) -> dict:
    key = jax.random.key(seed)
    ks = jax.random.split(key, 24)
    f32 = jnp.float32

    def nrm(k, shape, scale):
        return scale * jax.random.normal(k, shape, f32)

    n_buf = min(MAX_WINDOW, PAST_LEN)
    f_bias = jnp.linspace(3.0, 6.0, N_MLSTM_HEADS, dtype=f32)
    mlstm_gate_b = jnp.stack([nrm(ks[10], (DEPTH, N_MLSTM_HEADS), 0.1),
                              f_bias + nrm(ks[11], (DEPTH, N_MLSTM_HEADS), 0.1)], axis=1)
    return {
        'x_prompt': nrm(ks[0], (BATCH, SEQ, D_MODEL), 1.0),
        'x_sample': nrm(ks[1], (DEC_BATCH, DEC_SEQ, D_MODEL), 1.0),
        'cache_attn_k': nrm(ks[2], (DEPTH, DEC_BATCH, n_buf, N_ATTN_HEADS, HEAD_DIM), 1.0),
        'cache_attn_v': nrm(ks[3], (DEPTH, DEC_BATCH, n_buf, N_ATTN_HEADS, HEAD_DIM), 1.0),
        'state_mlstm_conv': nrm(ks[4], (DEPTH, DEC_BATCH, CONV_WIDTH - 1, 2 * MLSTM_WIDTH), 1.0),
        'state_mlstm_C': nrm(ks[5], (DEPTH, DEC_BATCH, N_MLSTM_HEADS, HEAD_DIM, HEAD_DIM), 0.3),
        'state_mlstm_n': nrm(ks[6], (DEPTH, DEC_BATCH, N_MLSTM_HEADS, HEAD_DIM), 0.3),
        'state_mlstm_m': nrm(ks[7], (DEPTH, DEC_BATCH, N_MLSTM_HEADS), 1.0),
        'state_hgrn_S': nrm(ks[8], (DEPTH, DEC_BATCH, N_HGRN_HEADS, HEAD_DIM, HEAD_DIM), 1.0),
        'rel_bias': nrm(ks[9], (N_REL_BUCKETS, N_ATTN_HEADS), 0.5),
        'g_mix': 1.0 + nrm(ks[12], (DEPTH, D_MODEL), 0.05),
        'w_in': nrm(ks[13], (DEPTH, D_MODEL, PROJ_WIDTH), D_MODEL ** -0.5),
        'mlstm_gate_b': mlstm_gate_b,
        'mlstm_conv_w': nrm(ks[14], (DEPTH, CONV_WIDTH, 2 * MLSTM_WIDTH), CONV_WIDTH ** -0.5),
        'mlstm_norm_g': 1.0 + nrm(ks[15], (DEPTH, MLSTM_WIDTH), 0.05),
        'hgrn_lb_raw': nrm(ks[16], (DEPTH, HGRN_WIDTH), 0.5),
        'hgrn_norm_g': 1.0 + nrm(ks[17], (DEPTH, HGRN_WIDTH), 0.05),
        'w_out': nrm(ks[18], (DEPTH, MIX_WIDTH, D_MODEL), MIX_WIDTH ** -0.5),
        'g_ffn': 1.0 + nrm(ks[19], (DEPTH, D_MODEL), 0.05),
        'w_up': nrm(ks[20], (DEPTH, D_MODEL, D_FF), D_MODEL ** -0.5),
        'w_down': nrm(ks[21], (DEPTH, D_FF, D_MODEL), D_FF ** -0.5),
        'g_final': 1.0 + nrm(ks[22], (D_MODEL,), 0.05),
    }

def reference(x_prompt, x_sample, cache_attn_k, cache_attn_v, state_mlstm_conv, state_mlstm_C,
              state_mlstm_n, state_mlstm_m, state_hgrn_S, rel_bias, g_mix, w_in, mlstm_gate_b,
              mlstm_conv_w, mlstm_norm_g, hgrn_lb_raw, hgrn_norm_g, w_out, g_ffn, w_up, w_down, g_final):
    f32 = jnp.float32
    bp, sp = x_prompt.shape[:2]
    n_keep = min(MAX_WINDOW, sp)
    lb_p = jax.nn.softmax(hgrn_lb_raw.astype(f32), axis=0)
    hgrn_lb = jnp.cumsum(lb_p, axis=0) - lb_p[0]
    zeros_conv = jnp.zeros((bp, CONV_WIDTH - 1, 2 * MLSTM_WIDTH), x_prompt.dtype)
    zeros_C = jnp.zeros((bp, N_MLSTM_HEADS, HEAD_DIM, HEAD_DIM), f32)
    zeros_n = jnp.zeros((bp, N_MLSTM_HEADS, HEAD_DIM), f32)
    zeros_m = jnp.zeros((bp, N_MLSTM_HEADS), f32)
    zeros_S = jnp.zeros((bp, N_HGRN_HEADS, HEAD_DIM, HEAD_DIM), f32)
    prompt_attn = functools.partial(attn_prompt, rel_bias=rel_bias)
    hp, hs = x_prompt, x_sample
    p_states, s_states = [], []
    for l in range(DEPTH):
        weights = (g_mix[l], w_in[l], mlstm_gate_b[l], mlstm_conv_w[l], mlstm_norm_g[l], hgrn_lb[l],
                   hgrn_norm_g[l], w_out[l], g_ffn[l], w_up[l], w_down[l])
        hp, (pk, pv, pconv, pC, pn, pm, pS) = trunk_layer(hp, prompt_attn, zeros_conv, zeros_C, zeros_n, zeros_m,
                                                         zeros_S, *weights)
        p_states.append((pk[:, sp - n_keep:], pv[:, sp - n_keep:], pconv, pC, pn, pm, pS))
        sample_attn = functools.partial(attn_sample, rel_bias=rel_bias, k_buf=cache_attn_k[l], v_buf=cache_attn_v[l])
        hs, s_st = trunk_layer(hs, sample_attn, state_mlstm_conv[l], state_mlstm_C[l], state_mlstm_n[l],
                               state_mlstm_m[l], state_hgrn_S[l], *weights)
        s_states.append(s_st)
    y_prompt = rmsnorm(hp, g_final)
    y_sample = rmsnorm(hs, g_final)
    p_attn_k, p_attn_v, p_mlstm_conv, p_mlstm_C, p_mlstm_n, p_mlstm_m, p_hgrn_S = [jnp.stack(a) for a in zip(*p_states)]
    s_attn_k, s_attn_v, s_mlstm_conv, s_mlstm_C, s_mlstm_n, s_mlstm_m, s_hgrn_S = [jnp.stack(a) for a in zip(*s_states)]
    return (y_prompt, y_sample,
            p_attn_k, p_attn_v, p_mlstm_conv, p_mlstm_C, p_mlstm_n, p_mlstm_m, p_hgrn_S,
            s_attn_k, s_attn_v, s_mlstm_conv, s_mlstm_C, s_mlstm_n, s_mlstm_m, s_hgrn_S)


_drawn_inputs = setup_inputs


def setup_inputs(seed=0):
    import zlib

    import numpy as np

    out = dict(_drawn_inputs(seed))
    spreads = {}
    factors = {'mlstm_norm_g': 4.369, 'hgrn_norm_g': 4.428}
    for name, (base, spread) in spreads.items():
        noise = np.random.default_rng([zlib.crc32(name.encode()), seed]).standard_normal(out[name].shape)
        drawn = base * np.exp(spread * noise) if base else spread * noise
        out[name] = jnp.asarray(drawn.astype(out[name].dtype))
    for name, factor in factors.items():
        out[name] = (out[name] * factor).astype(out[name].dtype)
    return out
```

```python
from contextlib import ExitStack

import numpy as np
import concourse.bass as bass
from concourse import mybir

ALU = mybir.AluOpType
ACT = mybir.ActivationFunctionType
AX = mybir.AxisListType
F32 = mybir.dt.float32

P = 128
D = 1024
KD = D // P
S = 1024
NB, NT = 8, 4
NS = NB * NT
NTOK = S + NS
TG = NTOK // 3
H, E = 8, 64
HM = 4
NCH = S // P
NTILE = NCH + 1
WB = 2048
FAR, NFAR = 1536, 96
DFF = 4096
EPS = 1e-6
NEG = -1e30
NLEV = 8
UW = 256
SLOTS = 3
TOE = S + P - 1
FOFF = P
NKEY = 4 * NFAR + 4 * P + NS
FW = 1152

AQ, AK, AV = 0, 512, 1024
MQ, MK, MV, MO, MI, MF = 1536, 1792, 2048, 2304, 2560, 2564
HQ, HF, HI, HG = 2568, 2824, 3080, 3336


def rows(i):
    return P if i < NCH else NS


def tile_tokens(i):
    return slice(i * P, i * P + rows(i))


def _bucket(dist):
    n = np.asarray(dist).astype(np.int32)
    scaled = np.log(np.maximum(n, 1) / 16) / np.log(2048 / 16)
    large = np.minimum(16 + (scaled * 16).astype(np.int32), 31)
    return np.where(n < 16, n, large).astype(np.int32)


def _bias_rows(dist):
    d = np.asarray(dist)
    out = np.zeros((33,) + d.shape, np.float32)
    b = _bucket(np.clip(d, 0, None))
    for n in range(32):
        out[n] = b == n
    c = np.zeros(d.shape, np.int32)
    for window, dil in ((128, 1), (512, 4), (2048, 16)):
        c += (d >= 0) & (d <= window) & (d % dil == 0)
    out[32] = np.where(c > 0, np.log(np.maximum(c, 1).astype(np.float64)), NEG)
    return out


def constants():
    c = {}
    c["c_ident"] = np.eye(P, dtype=np.float32)
    toe = np.full(FW, 1 << 20, np.int64)
    toe[:TOE] = S - 1 - np.arange(TOE)
    c["c_bias_toe"] = _bias_rows(toe)
    idx = np.concatenate([
        np.concatenate([16 * np.arange(NFAR) + j for j in range(4)]),
        np.concatenate([FAR + 4 * np.arange(P) + k for k in range(4)]),
    ])
    dist = np.zeros((NT, NKEY), np.int64)
    for t in range(NT):
        dist[t, :NKEY - NS] = WB + t - idx
        dist[t, NKEY - NS:] = t - np.arange(NS) % NT
    c["c_bias_keys"] = np.ascontiguousarray(_bias_rows(dist))
    other = np.zeros((P, 2, NS), np.float32)
    for p in range(P):
        for g in range(2):
            other[p, g] = np.where(np.arange(NS) // NT == 4 * g + p // 32, 0.0, NEG)
    c["c_other_batch"] = other
    s, t = np.arange(P)[:, None], np.arange(P)[None]
    lev = np.zeros((P, NLEV, P), np.float32)
    for l in range(NLEV - 1):
        m = 64 >> l
        lev[:, l] = (s // (2 * m) == t // (2 * m)) & (s % (2 * m) < m) & (t % (2 * m) >= m)
    lev[:, NLEV - 1] = s == t
    c["c_levels"] = lev
    cm = np.zeros((P, P + NS), np.float32)
    cm[:, :P] = np.where(s <= t, 0.0, NEG)
    s4, t4 = np.arange(NS)[:, None], np.arange(NS)[None]
    cm[:NS, P:] = np.where((s4 // NT == t4 // NT) & (s4 <= t4), 0.0, NEG)
    c["c_causal"] = cm
    seg = np.ones((1, NTOK), np.float32)
    seg[0, 0:S:P] = 0.0
    seg[0, S::NT] = 0.0
    c["c_seg"] = seg
    sel = np.zeros((HM, HM + 2, P), np.float32)
    for h in range(HM):
        sel[h, h] = 1.0
        sel[h, HM + h // 2, 64 * (h % 2):64 * (h % 2) + 64] = 1.0
    c["c_sel"] = sel
    c["c_batch"] = (np.arange(NS)[:, None] // NT == np.arange(NB)[None]).astype(np.float32)
    return c


def program(nc, i_, o_, taps=None, upto=99):
    ctx = ExitStack()
    with ctx:
        def sb(name, shape):
            return ctx.enter_context(nc.sbuf_tensor(name, shape, F32))

        def sem(name):
            return ctx.enter_context(nc.semaphore(name))

        PS = ctx.enter_context(nc.psum_tensor("PS", [P, 8, 512], F32))

        R_xn = sb("R_xn", [P, 9216])
        R_aqk = sb("R_aqk", [P, 8448])
        R_rec = sb("R_rec", [P, 24492])
        R_ring = sb("R_ring", [P, 6144])

        def view(region, at, pattern, **dims):
            n = int(np.prod(list(dims.values())))
            names = " ".join(dims)
            part = dict(list(dims.items())[1:])
            return region[:, at:at + n].rearrange(f"p ({names}) -> p {names}", **part)

        xnT = view(R_xn, 0, "", k=KD, t=NTOK)
        mix = view(R_xn, 0, "", i=NTILE, n=D)
        aqk = view(R_aqk, 0, "", k=8, t=NTOK)
        mqk = view(R_rec, 0, "", k=4, t=NTOK)
        hqk = view(R_rec, 4224, "", k=4, t=NTOK)
        hb = view(R_rec, 8448, "", k=2, t=NTOK)
        va = view(R_rec, 10560, "", i=NTILE, h=H, e=E + 1)
        vm = view(R_rec, 15240, "", i=NTILE, h=HM, e=E + 1)
        mo = view(R_rec, 17580, "", i=NTILE, n=256)
        hi = view(R_rec, 19884, "", i=NTILE, n=256)
        hg = view(R_rec, 22188, "", i=NTILE, n=256)

        ident = sb("ident", [P, P])
        seg = sb("seg", [P, NTOK])
        gmix = sb("gmix", [P, KD])
        gffn = sb("gffn", [P, KD])
        gout = sb("gout", [P, KD])
        convw = sb("convw", [P, 4, 4])
        lb3 = sb("lb3", [P, 6, 2])
        gateb = sb("gateb", [P, 1])
        m0 = sb("m0", [HM, NB])
        sel = sb("sel", [HM, (HM + 2) * P])
        selv = sel[:, :].rearrange("h (a p) -> h a p", p=P)
        stat = sb("stat", [P, 4, 12])
        cstate = sb("cstate", [P, 4, 24])
        ctail = sb("ctail", [P, 4, 27])
        bm = sb("bm", [HM, NTOK])
        egl = sb("egl", [HM, 16])
        gcol = sb("gcol", [P, NTILE, P])
        glc = sb("glc", [P, 2, 16])
        wgate = view(R_rec, 22700, "", k=KD, n=36)
        small = sb("small", [P, 64])

        def const(name):
            return i_[name]

        fdr = nc.dram_tensor("bias_by_distance", [H, FW], F32, kind="Internal").ap()
        frep = nc.dram_tensor("bias_by_distance_copies", [H, P, FW], F32, kind="Internal").ap()

        phase_end = sem("phase_end")
        phase = {}

        def barrier(eng, name):
            phase[name] = phase.get(name, 0) + 1
            eng.drain().then_inc(phase_end, 1)
            eng.wait_ge(phase_end, 5 * phase[name])

        consts_in = sem("consts_in")
        x_in = [sem(f"x_in{n}") for n in range(3)]
        sumsq_ready, meansq_ready, rms_ready = sem("sumsq_ready"), sem("meansq_ready"), sem("rms_ready")
        xs_ready, xs_transposed, xT_ready = sem("xs_ready"), sem("xs_transposed"), sem("xT_ready")
        dve_order, act_order, pe_order = sem("dve_order"), sem("act_order"), sem("pe_order")
        order = {"dve": 0, "act": 0, "pe": 0}

        def link(name, eng, ins):
            s = {"dve": dve_order, "act": act_order, "pe": pe_order}[name]
            order[name] += 1
            ins.then_inc(s, 1)
            eng.wait_ge(s, order[name])

        bias_in, bias_ready, bias_copied, bias_stored = sem("bias_in"), sem("bias_ready"), sem("bias_copied"), sem("bias_stored")
        wgate_zero, wgate_in = sem("wgate_zero"), sem("wgate_in")
        w_in_ready = [sem(f"w_in_ready{n}") for n in range(SLOTS)]
        unit_done = sem("unit_done")
        gate_psum, gate_taken = sem("gate_psum"), sem("gate_taken")
        gate_abs, gate_soft, gate_args, gate_rows = sem("gate_abs"), sem("gate_soft"), sem("gate_args"), sem("gate_rows")
        gate_last, gate_cols, gcol_ready, glc_psum = sem("gate_last"), sem("gate_cols"), sem("gcol_ready"), sem("glc_psum")
        cstate_psum, cstate_ready = sem("cstate_psum"), sem("cstate_ready")
        t_psum, t_taken = sem("t_psum"), sem("t_taken")
        sig_ready, conv_in, conv_done, h_done = sem("sig_ready"), sem("conv_in"), sem("conv_done"), sem("h_done")
        lnf_ready, f_ready = sem("lnf_ready"), sem("f_ready")
        n_psum, n_taken = sem("n_psum"), sem("n_taken")
        ones_ready = sem("ones_ready")
        tail_psum, tail_copied = sem("tail_psum"), sem("tail_copied")
        outs = sem("outs")
        n_out = [0]

        def store(eng, dst, src):
            eng.dma_start(dst, src).then_inc(outs, 16)
            n_out[0] += 1

        block = ctx.enter_context(nc.Block())

        xt = [R_rec[:, 10560 + n * D:10560 + (n + 1) * D] for n in range(3)]
        sqj = R_rec[:, 13632:13632 + D]
        cst_nat = R_rec[0:24, 0:512]
        toe_in = R_rec[0:33, 512:512 + FW]
        raug = R_rec[0:33, 1700:1708]
        F_sb = R_rec[0:8, 1800:1800 + FW]

        def phase_a_sync(sp):
            for n, (dst, src) in enumerate([
                (ident[:, :], const("c_ident")),
                (seg[:, :], const("c_seg").to_broadcast([P, NTOK])),
                (gmix[:, :], i_["g_mix"][0].rearrange("(k p) -> p k", p=P)),
                (gffn[:, :], i_["g_ffn"][0].rearrange("(k p) -> p k", p=P)),
                (gout[:, 4:6], i_["mlstm_norm_g"][0].rearrange("(k p) -> p k", p=P)),
                (gout[:, 6:8], i_["hgrn_norm_g"][0].rearrange("(k p) -> p k", p=P)),
                (lb3[:, 0, :], i_["hgrn_lb_raw"][0].rearrange("(k p) -> p k", p=P)),
                (gateb[0:4, :], i_["mlstm_gate_b"][0, 0:1, :].rearrange("o h -> h o")),
                (gateb[32:36, :], i_["mlstm_gate_b"][0, 1:2, :].rearrange("o h -> h o")),
                (m0[:, :], i_["state_mlstm_m"][0].rearrange("b h -> h b")),
                (selv, const("c_sel")),
                (cst_nat, i_["state_mlstm_conv"][0].rearrange("b j n -> (b j) n")),
            ] + [(convw[:, k, :], i_["mlstm_conv_w"][0, :, k * P:(k + 1) * P].rearrange("j p -> p j"))
                 for k in range(4)]):
                sp.dma_start(dst, src, allow_slow_non_contiguous=True).then_inc(consts_in, 16)
            sp.dma_start(toe_in, const("c_bias_toe")).then_inc(bias_in, 16)
            sp.dma_start(raug[0:32, :], i_["rel_bias"]).then_inc(bias_in, 16)
            for i in range(NTILE):
                if i >= 3:
                    sp.wait_ge(xs_transposed, 2 * (i - 2))
                src = i_["x_prompt"][0, i * P:(i + 1) * P, :] if i < NCH else i_["x_sample"].rearrange("b t d -> (b t) d")
                sp.dma_start(xt[i % 3][0:rows(i), :], src).then_inc(x_in[i % 3], 16)
            sp.wait_ge(bias_copied, 1)
            sp.dma_start(fdr, F_sb).then_inc(bias_stored, 16)
            sp.wait_ge(bias_stored, 16)
        NCONST = 16 * 16

        def phase_a_act(act):
            for i in range(NTILE):
                r = rows(i)
                act.wait_ge(x_in[i % 3], 16 * (i // 3 + 1))
                act.activation(sqj[0:r, :], xt[i % 3][0:r, :], ACT.Square,
                               accum_out=stat[0:r, 0, i:i + 1]).then_inc(sumsq_ready, 1)
                act.wait_ge(meansq_ready, i + 1)
                act.activation(stat[0:r, 2, i:i + 1], stat[0:r, 1, i:i + 1], ACT.Sqrt).then_inc(rms_ready, 1)
            act.wait_ge(lb_shifted, 1)
            act.activation(lb3[:, 2, :], lb3[:, 1, :], ACT.Exp).then_inc(lb_exp, 1)

        def phase_a_dve(dve):
            dve.wait_ge(bias_in, 32)
            dve.memset(raug[32:33, :], 1.0).then_inc(bias_ready, 1)
            dve.wait_ge(consts_in, NCONST)
            for i in range(NTILE + 1):
                if i < NTILE:
                    r = rows(i)
                    dve.wait_ge(sumsq_ready, i + 1)
                    dve.tensor_scalar(stat[0:r, 1, i:i + 1], stat[0:r, 0, i:i + 1], 1.0 / D, EPS,
                                      ALU.mult, ALU.add).then_inc(meansq_ready, 1)
                    dve.wait_ge(rms_ready, i + 1)
                    link("dve", dve, dve.reciprocal(stat[0:r, 3, i:i + 1], stat[0:r, 2, i:i + 1]))
                    dve.tensor_scalar(xt[i % 3][0:r, :], xt[i % 3][0:r, :], stat[0:r, 3, i:i + 1], None,
                                      ALU.mult).then_inc(xs_ready, 1)
                if i >= 1:
                    j = i - 1
                    for kk in range(2):
                        dve.wait_ge(xs_transposed, 2 * j + kk + 1)
                        src = PS[:, 2 * (j % 2) + kk, :].rearrange("p (k t) -> p k t", t=P)[:, :, 0:rows(j)]
                        dve.tensor_tensor(xnT[:, 4 * kk:4 * kk + 4, tile_tokens(j)], src,
                                          gmix[:, 4 * kk:4 * kk + 4].unsqueeze(2).to_broadcast([P, 4, rows(j)]),
                                          ALU.mult).then_inc(xT_ready, 1)
            dve.tensor_tensor(lb3[:, 1, :], lb3[:, 0, :], lb3[:, 0, :], ALU.subtract).then_inc(lb_shifted, 1)
            dve.wait_ge(lb_exp, 1)
            link("dve", dve, dve.reciprocal(lb3[:, 3, :], lb3[:, 2, :]))
            link("dve", dve, dve.tensor_tensor(lb3[:, 3, :], lb3[:, 2, :], lb3[:, 3, :], ALU.mult))
            link("dve", dve, dve.tensor_tensor(lb3[:, 4, :], lb3[:, 3, :], lb3[:, 3, :], ALU.subtract))
            link("dve", dve, dve.tensor_scalar(lb3[:, 5, :], lb3[:, 4, :], -1.0, 1.0, ALU.mult, ALU.add))
            for kk in range(4):
                dve.wait_ge(cstate_psum, 4)
                last = dve.tensor_copy(cstate[:, kk, :], PS[:, 7, kk * 32:kk * 32 + 24])
            link("dve", dve, last)
            dve.wait_ge(bias_psum, 3)
            dve.tensor_copy(F_sb.rearrange("h (a n) -> h a n", a=3), PS[0:8, 4:7, 0:384]).then_inc(bias_copied, 1)

        bias_copies = sem("bias_copies")
        lb_exp, lb_shifted, bias_psum, silu_done = sem("lb_exp"), sem("lb_shifted"), sem("bias_psum"), sem("silu_done")

        def phase_a_pe(pe):
            pe.wait_ge(consts_in, NCONST)
            pe.wait_ge(bias_in, 32)
            pe.wait_ge(bias_ready, 1)
            for a in range(3):
                pe.matmul(PS[0:8, 4 + a, 0:384], raug, toe_in[:, a * 384:(a + 1) * 384],
                          start=True, stop=True).then_inc(bias_psum, 1)
            for kk in range(4):
                pe.transpose(PS[:, 7, kk * 32:kk * 32 + 24], cst_nat[:, kk * P:(kk + 1) * P],
                             ident[0:24, 0:24]).then_inc(cstate_psum, 1)
            for i in range(NTILE):
                r = rows(i)
                pe.wait_ge(xs_ready, i + 1)
                if i >= 2:
                    pe.wait_ge(xT_ready, 2 * (i - 1))
                for k in range(KD):
                    t = pe.transpose(PS[:, 2 * (i % 2) + k // 4, (k % 4) * P:(k % 4) * P + r],
                                     xt[i % 3][0:r, k * P:(k + 1) * P], ident[0:r, 0:r])
                    if k % 4 == 3:
                        t.then_inc(xs_transposed, 1)

        T_UNITS = [HQ, HF, MQ, MK, AQ, AQ + UW, AK, AK + UW]
        N_UNITS = [MV, MO, HI, HG, AV, AV + UW]
        UNITS = T_UNITS + N_UNITS
        ring = [view(R_ring, n * 2048, "", k=KD, n=UW) for n in range(SLOTS)]
        w_in = i_["w_in"][0].rearrange("(k p) n -> p k n", p=P)
        CW = 3 + S + 7 * NB
        cst = [R_rec[:, 10560 + n * 1083:10560 + n * 1083 + CW] for n in range(2)]
        scr = [R_rec[:, 12726 + n * NTOK:12726 + (n + 1) * NTOK] for n in range(2)]
        gs = [R_aqk[0:4, n * NTOK:(n + 1) * NTOK] for n in range(7)]
        gr = R_aqk[:, 7 * NTOK:8 * NTOK]
        tailnat = R_rec[0:27, 22188:22700]

        def three(ap):
            return ap.rearrange("p (a t) -> p a t", a=3)

        def prompt(ap):
            return ap[:, 0:S].rearrange("p (c t) -> p c t", t=P)

        def sample(ap):
            return ap[:, S:NTOK].rearrange("p (b t) -> p b t", t=NT)

        def phase_b_sync(sp):
            sp.wait_ge(wgate_zero, 1)
            for col, at in ((MI, 0), (MF, 32)):
                sp.dma_start(wgate[:, :, at:at + 4], w_in[:, :, col:col + 4],
                             allow_slow_non_contiguous=True).then_inc(wgate_in, 16)
            for n, col in enumerate(UNITS):
                if n >= SLOTS:
                    m = n - SLOTS
                    if m < len(T_UNITS):
                        sp.wait_ge(t_psum, 2 * (m + 1))
                    else:
                        sp.wait_ge(n_psum, NTILE * (m - len(T_UNITS) + 1))
                sp.dma_start(ring[n % SLOTS], w_in[:, :, col:col + UW]).then_inc(w_in_ready[n % SLOTS], 16)
            for i in range(NTILE):
                sp.wait_ge(k_taken, i + 1)
                sp.dma_start(by_token("k", i), kstage[0:rows(i), :].rearrange("p (h e) -> p h e", e=E))\
                  .then_inc(k_stored, 16)
            sp.wait_ge(k_stored, 16 * NTILE)

        gate_stored = sem("gate_stored")
        k_psum, k_taken, k_stored = sem("k_psum"), sem("k_taken"), sem("k_stored")
        kstage = R_xn[:, 8448:8960]

        def by_token(what, i):
            if i < NCH:
                return o_["p_" + what][0, 0, i * P:(i + 1) * P]
            return o_["s_" + what][0].rearrange("b t h e -> (b t) h e")

        def phase_b_gps(pool):
            pool.memset(wgate[:, :, :], 0.0).then_inc(wgate_zero, 1)
            pool.dma_start(frep, fdr.unsqueeze(1).to_broadcast([H, P, FW])).then_inc(bias_copies, 16)
            pool.wait_ge(gate_args, 1)
            pool.dma_start(o_["p_m"][0].rearrange("b h -> h b"), gs[6][:, S - 1:S],
                           allow_slow_non_contiguous=True).then_inc(gate_stored, 16)
            pool.dma_start(o_["s_m"][0].rearrange("b h -> h b"), gs[6][:, S + 3::NT],
                           allow_slow_non_contiguous=True).then_inc(gate_stored, 16)
            pool.wait_ge(tail_copied, 1)
            pool.dma_start(o_["p_conv"][0, 0], tailnat[0:3, :]).then_inc(gate_stored, 16)
            pool.dma_start(o_["s_conv"][0].rearrange("b j n -> (b j) n"), tailnat[3:27, :]).then_inc(gate_stored, 16)
            pool.wait_ge(gate_stored, 64)

        def tile_taken(eng, tj):
            if tj < 2:
                eng.wait_ge(h_done, tj + 1)
            elif tj < 4:
                eng.wait_ge(sig_ready, tj + 1)
            else:
                eng.wait_ge(t_taken, tj - 3)

        def phase_b_pe(pe):
            pe.wait_ge(wgate_in, 32)
            for g in range(3):
                for k in range(KD):
                    mm = pe.matmul(PS[0:36, g, 0:TG], wgate[:, k, :], xnT[:, k, g * TG:(g + 1) * TG],
                                   start=(k == 0), stop=(k == KD - 1))
            mm.then_inc(gate_psum, 1)
            pe.wait_ge(gate_taken, 1)
            for n in range(len(T_UNITS)):
                pe.wait_ge(w_in_ready[n % SLOTS], 16 * (n // SLOTS + 1))
                for j in range(2):
                    tj = 2 * n + j
                    if tj >= 2:
                        tile_taken(pe, tj - 2)
                    for g in range(3):
                        for k in range(KD):
                            mm = pe.matmul(PS[:, 3 * (tj % 2) + g, 0:TG], ring[n % SLOTS][:, k, j * P:(j + 1) * P],
                                           xnT[:, k, g * TG:(g + 1) * TG], start=(k == 0), stop=(k == KD - 1))
                    mm.then_inc(t_psum, 1)
                if n == 1:
                    pe.wait_ge(gate_rows, 4)
                    for c in range(NTILE):
                        r = rows(c)
                        pe.transpose(PS[0:r, 6, (c % 4) * P:(c % 4 + 1) * P], gr[:, tile_tokens(c)], ident[:, :])\
                            .then_inc(gate_cols, 1)
                        if c % 4 == 3 or c == NTILE - 1:
                            pe.wait_ge(gcol_ready, c // 4 + 1)
                    pe.wait_ge(gate_last, 1)
                    for pr in range(2):
                        mm = pe.matmul(PS[:, 7, pr * 16:(pr + 1) * 16], selv[:, HM + pr, :], egl[:, :],
                                       start=True, stop=True)
                    mm.then_inc(glc_psum, 1)
            pe.wait_ge(conv_done, 4)
            for kk in range(4):
                t = pe.transpose(PS[0:27, 7, kk * P:(kk + 1) * P], ctail[:, kk, :], ident[:, :])
            t.then_inc(tail_psum, 1)
            pe.wait_ge(tail_copied, 1)
            for n in range(len(T_UNITS), len(UNITS)):
                pe.wait_ge(w_in_ready[n % SLOTS], 16 * (n // SLOTS + 1))
                for i in range(NTILE):
                    q = (n - len(T_UNITS)) * NTILE + i
                    if q >= 2:
                        pe.wait_ge(n_taken, q - 1)
                    for k in range(KD):
                        mm = pe.matmul(PS[0:rows(i), 6 + q % 2, 0:UW], xnT[:, k, tile_tokens(i)],
                                       ring[n % SLOTS][:, k, :], start=(k == 0), stop=(k == KD - 1))
                    mm.then_inc(n_psum, 1)
                    if n == len(T_UNITS) + 4:
                        if i == 0:
                            pe.wait_ge(t_taken, 12)
                        if i >= 2:
                            pe.wait_ge(k_taken, i - 1)
                        for k in range(4):
                            t = pe.transpose(PS[0:rows(i), i % 2, k * P:(k + 1) * P], aqk[:, 4 + k, tile_tokens(i)],
                                             ident[:, :])
                        t.then_inc(k_psum, 1)

        def phase_b_act(act):
            act.wait_ge(gate_abs, 1)
            link("act", act, act.activation(gs[2], gs[2], ACT.Exp, scale=-1.0))
            act.activation(gs[2], gs[2], ACT.Ln, bias=1.0).then_inc(gate_soft, 1)
            act.wait_ge(gate_args, 1)
            act.activation(gr[0:4, :], gs[3], ACT.Exp).then_inc(gate_rows, 1)
            act.activation(gr[32:36, :], gs[6], ACT.Exp, scale=-1.0).then_inc(gate_rows, 1)
            act.activation(gr[64:68, :], gs[4], ACT.Exp).then_inc(gate_rows, 1)
            act.activation(gr[96:100, :], gs[1], ACT.Copy).then_inc(gate_rows, 1)
            for tj in range(2 * len(T_UNITS)):
                kind, p = tj // 2, tj % 2
                bank = 3 * (tj % 2)
                src = PS[:, bank:bank + 3, 0:TG]
                act.wait_ge(t_psum, tj + 1)
                if kind < 2:
                    if tj >= 2:
                        act.wait_ge(h_done, tj - 1)
                    act.activation(three(scr[tj % 2]), src, ACT.Sigmoid).then_inc(sig_ready, 1)
                elif kind < 4:
                    n = tj - 4
                    c = cst[n % 2]
                    if n >= 2:
                        act.wait_ge(conv_done, n - 1)
                    c2 = c[:, 3 + S:].rearrange("p (b j) -> p b j", j=7)
                    act.activation(c[:, 3:3 + 2 * TG].rearrange("p (a t) -> p a t", a=2),
                                   PS[:, bank:bank + 2, 0:TG], ACT.Copy).then_inc(conv_in, 1)
                    act.activation(c[:, 3 + 2 * TG:3 + S], PS[:, bank + 2, 0:S - 2 * TG], ACT.Copy).then_inc(conv_in, 1)
                    act.activation(c2[:, :, 0:3], cstate[:, n, :].rearrange("p (b j) -> p b j", j=3), ACT.Copy)\
                        .then_inc(conv_in, 1)
                    act.activation(c2[:, :, 3:7], PS[:, bank + 2, S - 2 * TG:TG].rearrange("p (b j) -> p b j", j=4),
                                   ACT.Copy).then_inc(t_taken, 1)
                    if n >= 1:
                        conv_sigmoid(act, n - 1)
                    if n == 3:
                        conv_sigmoid(act, 3)
                else:
                    k = tj - 8
                    if k == 0:
                        act.wait_ge(gate_stored, 32)
                        act.wait_ge(gcol_ready, 3)
                    act.activation(three(aqk[:, k, :]), src, ACT.Copy, scale=0.125 if k < 4 else 1.0)\
                        .then_inc(t_taken, 1)
            act.wait_ge(tail_psum, 1)
            for nu in range(len(N_UNITS)):
                for i in range(NTILE):
                    q = nu * NTILE + i
                    r = rows(i)
                    act.wait_ge(n_psum, q + 1)
                    src = PS[0:r, 6 + q % 2, 0:UW]
                    if nu == 0:
                        act.activation(vm[0:r, i, :, 0:E], src.rearrange("p (h e) -> p h e", e=E), ACT.Copy)\
                            .then_inc(n_taken, 1)
                    elif nu in (1, 3):
                        if nu == 3 and i == 0:
                            act.wait_ge(gate_stored, 64)
                        act.activation((mo if nu == 1 else hg)[0:r, i, :], src, ACT.Sigmoid).then_inc(n_taken, 1)
                    elif nu == 2:
                        act.activation(hi[0:r, i, :], src, ACT.Copy).then_inc(n_taken, 1)
                    else:
                        act.wait_ge(silu_done, 4)
                        act.activation(va[0:r, i, 4 * (nu - 4):4 * (nu - 4) + 4, 0:E],
                                       src.rearrange("p (h e) -> p h e", e=E), ACT.Copy).then_inc(n_taken, 1)
                        if nu == 4:
                            act.wait_ge(k_psum, i + 1)
                            if i >= 1:
                                act.wait_ge(k_stored, 16 * i)
                            act.activation(kstage[0:r, :], PS[0:r, i % 2, :], ACT.Copy).then_inc(k_taken, 1)
            act.wait_ge(f_ready, 2)
            for p in range(2):
                act.activation(hb[:, p, :], hb[:, p, :], ACT.Ln).then_inc(lnf_ready, 1)

        def conv_sigmoid(act, n):
            act.wait_ge(conv_done, n + 1)
            if n >= 2:
                act.wait_ge(silu_done, n - 1)
            else:
                act.wait_ge(h_done, 4)
            act.activation(scr[n % 2], mqk[:, n, :], ACT.Sigmoid).then_inc(sig_ready, 1)

        def phase_b_dve(dve):
            dve.wait_ge(gate_psum, 1)
            link("dve", dve, dve.tensor_scalar(three(gs[0]), PS[0:4, 0:3, 0:TG], gateb[0:4, :], None, ALU.add))
            link("dve", dve, dve.tensor_scalar(three(gs[1]), PS[32:36, 0:3, 0:TG], gateb[32:36, :], None, ALU.add))
            dve.nop().then_inc(gate_taken, 1)
            dve.scalar_tensor_tensor(gs[2], gs[1], -1.0, gs[1], ALU.mult, ALU.max).then_inc(gate_abs, 1)
            link("dve", dve, dve.tensor_scalar(gs[1], gs[1], 0.0, None, ALU.min))
            link("dve", dve, dve.memset(gr[:, :], 0.0))
            dve.wait_ge(gate_soft, 1)
            link("dve", dve, dve.tensor_tensor(gs[3], gs[1], gs[2], ALU.subtract))
            link("dve", dve, dve.tensor_tensor_scan(gs[4], seg[0:4, :], gs[3], 0.0, ALU.mult, ALU.add))
            link("dve", dve, dve.tensor_tensor(small[0:4, 0:NB], gs[3][:, S::NT], m0[:, :], ALU.add))
            link("dve", dve, dve.tensor_copy(gs[5], gs[0]))
            link("dve", dve, dve.tensor_tensor(gs[5][:, S::NT], small[0:4, 0:NB], gs[0][:, S::NT], ALU.max))
            link("dve", dve, dve.memset(gs[3][:, S::NT], NEG))
            link("dve", dve, dve.tensor_tensor_scan(gs[6], gs[3], gs[5], 0.0, ALU.add, ALU.max))
            link("dve", dve, dve.tensor_tensor(bm[:, :], gs[4], gs[6], ALU.subtract))
            link("dve", dve, dve.tensor_tensor(gs[1], gs[0], gs[4], ALU.subtract))
            dve.tensor_copy(gs[3][:, 0:P], bm[:, 0:P])
            prev = gs[6][:, P - 1:S - 1:P].unsqueeze(2).to_broadcast([HM, NCH - 1, P])
            dve.tensor_tensor(prompt(gs[3])[:, 1:], prompt(bm[:, :])[:, 1:], prev, ALU.add)
            dve.tensor_tensor(sample(gs[3]), sample(bm[:, :]), m0[:, :].unsqueeze(2).to_broadcast([HM, NB, NT]), ALU.add)
            dve.tensor_tensor(prompt(gs[4]), prompt(gs[1]),
                              bm[:, P - 1:S:P].unsqueeze(2).to_broadcast([HM, NCH, P]), ALU.add)
            dve.tensor_tensor(sample(gs[4]), sample(gs[1]),
                              bm[:, S + NT - 1::NT].unsqueeze(2).to_broadcast([HM, NB, NT]), ALU.add).then_inc(gate_args, 1)
            dve.wait_ge(gate_rows, 4)
            link("dve", dve, dve.tensor_copy(egl[:, 0:8], gr[0:4, P - 1:S:P]))
            link("dve", dve, dve.tensor_copy(egl[:, 8:16], gr[0:4, S + NT - 1::NT]))
            dve.nop().then_inc(gate_last, 1)
            for tj in range(8):
                if tj == 4:
                    for c4 in range(3):
                        n = 4 if c4 < 2 else 1
                        r = rows(4 * c4)
                        dve.wait_ge(gate_cols, 4 * c4 + n)
                        dve.tensor_copy(gcol[0:r, 4 * c4:4 * c4 + n, :],
                                        PS[0:r, 6, 0:n * P].rearrange("p (c t) -> p c t", t=P)).then_inc(gcol_ready, 1)
                    dve.wait_ge(glc_psum, 1)
                    link("dve", dve, dve.tensor_copy(glc[:, :, :], PS[:, 7, 0:32].rearrange("p (a n) -> p a n", a=2)))
                kind, p = tj // 2, tj % 2
                bank = 3 * (tj % 2)
                src = PS[:, bank:bank + 3, 0:TG]
                if kind == 0:
                    dve.wait_ge(sig_ready, tj + 1)
                    dve.tensor_tensor(three(hqk[:, p, :]), src, three(scr[tj % 2]), ALU.mult).then_inc(h_done, 1)
                elif kind == 1:
                    dve.wait_ge(sig_ready, tj + 1)
                    dve.tensor_scalar(hb[:, p, :], scr[tj % 2], lb3[:, 5, p:p + 1], lb3[:, 4, p:p + 1],
                                      ALU.mult, ALU.add).then_inc(f_ready, 1)
                    dve.wait_ge(f_ready, p + 1)
                    dve.tensor_scalar(hqk[:, 2 + p, :], hb[:, p, :], -1.0, 1.0, ALU.mult, ALU.add).then_inc(h_done, 1)
                else:
                    n = tj - 4
                    c = cst[n % 2]
                    if n < 2:
                        link("dve", dve, dve.memset(c[:, 0:3], 0.0))
                    dve.wait_ge(conv_in, 3 * n + 3)
                    dve.wait_ge(t_taken, n + 1)
                    dst = mqk[:, n, :]
                    c2 = c[:, 3 + S:].rearrange("p (b j) -> p b j", j=7)
                    for j in range(4):
                        w = convw[:, n, j:j + 1]
                        for out, src in ((dst[:, 0:S], c[:, j:j + S]), (sample(dst), c2[:, :, j:j + NT])):
                            if j == 0:
                                ins = dve.tensor_scalar(out, src, w, None, ALU.mult)
                            else:
                                ins = dve.scalar_tensor_tensor(out, src, w, out, ALU.mult, ALU.add)
                        link("dve", dve, ins)
                    dve.tensor_copy(ctail[:, n, 0:3], c[:, S:S + 3])
                    dve.tensor_copy(ctail[:, n, 3:27].rearrange("p (b j) -> p b j", j=3), c2[:, :, 4:7])\
                        .then_inc(conv_done, 1)
                    if n >= 1:
                        conv_silu(dve, n - 1)
                    if n == 3:
                        conv_silu(dve, 3)
            dve.wait_ge(tail_psum, 1)
            dve.tensor_copy(tailnat[:, :], PS[0:27, 7, :]).then_inc(tail_copied, 1)
            dve.memset(vm[:, :, :, E:E + 1], 1.0)
            for p in range(2):
                dve.wait_ge(lnf_ready, p + 1)
                link("dve", dve, dve.tensor_tensor_scan(hb[:, p, :], seg[:, :], hb[:, p, :], 0.0, ALU.mult, ALU.add))
            dve.memset(va[:, :, :, E:E + 1], 1.0).then_inc(ones_ready, 1)

        def conv_silu(dve, n):
            dve.wait_ge(sig_ready, 4 + n + 1)
            dve.scalar_tensor_tensor(mqk[:, n, :], mqk[:, n, :], 1.0 if n < 2 else 0.125, scr[n % 2],
                                     ALU.mult, ALU.mult).then_inc(silu_done, 1)

        G = [R_ring[:, n * S:(n + 1) * S] for n in range(2)]
        PB = [R_ring[:, (2 + n) * S:(3 + n) * S] for n in range(2)]
        PT = [view(R_ring, (4 + n) * S, "", k=NCH, q=P) for n in range(2)]
        g_in = [sem(f"g_in{n}") for n in range(2)]
        s_psum, biased, exped = sem("s_psum"), sem("biased"), sem("exped")
        pT_psum = sem("pT_psum")
        pT_taken = [sem("pT_taken_act"), sem("pT_taken_dve")]
        o_psum, o_taken, v_stored = sem("o_psum"), sem("o_taken"), sem("v_stored")
        negm = sb("negm", [P, 2])
        rl = sb("rl", [P, 1])
        STEPS = [(h, i) for h in range(H) for i in range(NCH)]
        groups, gsum = [], [0]
        for n_, (h_, i_n) in enumerate(STEPS):
            groups.append([(k0, min(i_n + 1, k0 + 4)) for k0 in range(0, i_n + 1, 4)])
            gsum.append(gsum[-1] + len(groups[-1]))

        def taken_through(eng, gid):
            if (gid + 1) // 2:
                eng.wait_ge(pT_taken[0], (gid + 1) // 2)
            if gid // 2:
                eng.wait_ge(pT_taken[1], gid // 2)

        def phase_c_sync(sp):
            sp.wait_ge(bias_copies, 16)
            for h in range(H):
                if h >= 2:
                    sp.wait_ge(biased, NCH * (h - 1))
                src = bass.AP(frep.tensor, h * P * FW + P - 1, [[FW - 1, P], [1, S]])
                sp.dma_start(G[h % 2], src).then_inc(g_in[h % 2], 16)
                if h == 1:
                    for i in range(NTILE):
                        sp.dma_start(by_token("v", i), va[0:rows(i), i, :, 0:E]).then_inc(v_stored, 16)
            sp.wait_ge(v_stored, 16 * NTILE)

        def phase_c_pe(pe):
            for n in range(len(STEPS) + 2):
                if n < len(STEPS):
                    h, i = STEPS[n]
                    if n >= 2:
                        pe.wait_ge(biased, n - 1)
                    part = slice(64 * (h % 2), 64 * (h % 2) + 64)
                    nk = (i + 1) * P
                    for c in range(0, nk, 512):
                        mm = pe.matmul(PS[:, 2 * (n % 2) + c // 512, 0:min(512, nk - c)],
                                       aqk[part, h // 2, i * P:(i + 1) * P], aqk[part, 4 + h // 2, c:min(c + 512, nk)],
                                       start=True, stop=True)
                    mm.then_inc(s_psum, 1)
                if 1 <= n <= len(STEPS):
                    m = n - 1
                    pe.wait_ge(exped, m + 1)
                    for j, (k0, k1) in enumerate(groups[m]):
                        gid = gsum[m] + j
                        if gid >= 2:
                            taken_through(pe, gid - 1)
                        for k in range(k0, k1):
                            t = pe.transpose(PS[:, 4 + gid % 2, (k - k0) * P:(k - k0 + 1) * P],
                                             PB[m % 2][:, k * P:(k + 1) * P], ident[:, :])
                        t.then_inc(pT_psum, 1)
                if n >= 2:
                    m = n - 2
                    h, i = STEPS[m]
                    taken_through(pe, gsum[m + 1])
                    if m >= 2:
                        pe.wait_ge(o_taken, m - 1)
                    for k in range(i + 1):
                        mm = pe.matmul(PS[:, 6 + m % 2, 0:E + 1], PT[m % 2][:, k, :], va[:, k, h, :],
                                       start=(k == 0), stop=(k == i))
                    mm.then_inc(o_psum, 1)

        def copy_groups(eng, copy, m, parity):
            for j, (k0, k1) in enumerate(groups[m]):
                gid = gsum[m] + j
                if gid % 2 == parity:
                    eng.wait_ge(pT_psum, gid + 1)
                    if m >= 2:
                        eng.wait_ge(o_psum, m - 1)
                    copy(PT[m % 2][:, k0:k1, :],
                         PS[:, 4 + gid % 2, 0:(k1 - k0) * P].rearrange("p (k q) -> p k q", q=P))\
                        .then_inc(pT_taken[parity], 1)

        def phase_c_act(act):
            for n in range(len(STEPS) + 1):
                if n < len(STEPS):
                    h, i = STEPS[n]
                    nk = (i + 1) * P
                    act.wait_ge(biased, n + 1)
                    act.activation(PB[n % 2][:, 0:nk], PB[n % 2][:, 0:nk], ACT.Exp, bias=negm[:, n % 2:n % 2 + 1],
                                   scale=-1.0).then_inc(exped, 1)
                if n >= 1:
                    copy_groups(act, lambda o, s: act.activation(o, s, ACT.Copy), n - 1, 0)

        def phase_c_dve(dve):
            for n in range(len(STEPS) + 2):
                if n < len(STEPS):
                    h, i = STEPS[n]
                    nk = (i + 1) * P
                    if i == 0:
                        dve.wait_ge(g_in[h % 2], 16 * (h // 2 + 1))
                    if n >= 2:
                        dve.wait_ge(pT_psum, gsum[n - 1])
                    dve.wait_ge(s_psum, n + 1)
                    scores = PS[:, 2 * (n % 2):2 * (n % 2) + 2, :].rearrange("p a n -> p (a n)")[:, 0:nk]
                    dve.tensor_tensor_reduce(PB[n % 2][:, 0:nk], scores, G[h % 2][:, S - nk:S], -1.0, 3e38,
                                             ALU.add, ALU.min, negm[:, n % 2:n % 2 + 1]).then_inc(biased, 1)
                if 1 <= n <= len(STEPS):
                    copy_groups(dve, dve.tensor_copy, n - 1, 1)
                if n >= 2:
                    m = n - 2
                    h, i = STEPS[m]
                    dve.wait_ge(o_psum, m + 1)
                    if m >= 1:
                        dve.wait_ge(o_taken, m)
                    link("dve", dve, dve.reciprocal(rl[:, :], PS[:, 6 + m % 2, E:E + 1]))
                    dve.tensor_scalar(mix[:, i, h * E:(h + 1) * E], PS[:, 6 + m % 2, 0:E], rl[:, :], None,
                                      ALU.mult).then_inc(o_taken, 1)
            link("dve", dve, dve.memset(qblk[:, :, :, :, :], 0.0))
            for hp in range(4):
                for h2 in range(2):
                    pt = slice(64 * h2, 64 * h2 + 64)
                    ins = dve.tensor_copy(qblk[pt, hp, :, 2 * hp + h2, :], sample(aqk[pt, hp, :]))
            link("dve", dve, ins)
            link("dve", dve, dve.tensor_copy(knew[:, :, :], aqk[:, 4:8, S:NTOK]))
            link("dve", dve, dve.tensor_copy(vnew[0:NS, :].rearrange("p (h e) -> p h e", e=E), va[0:NS, 8, :, 0:E]))

        qblk = R_ring[:, 0:1024].rearrange("p (hp b h t) -> p hp b h t", hp=4, b=NB, h=H)
        knew = R_ring[:, 1024:1152].rearrange("p (k t) -> p k t", k=4)
        vnew = R_ring[:, 1152:1664]

        A_ = R_aqk
        Dm = [view(A_, n * 512, "", h=HM, t=P) for n in range(2)]
        Wm = [view(A_, 1024 + n * 512, "", h=HM, t=P) for n in range(2)]
        kd = [view(A_, 2048 + n * 256, "", h=HM, e=E) for n in range(2)]
        tmpN = view(A_, 2560, "", h=HM, e=E + 1)
        nd = view(A_, 2820, "", h=HM, e=E + 1)
        hh = view(A_, 3080, "", h=HM, e=E)
        sq = view(A_, 3336, "", h=HM, e=E)
        Cst = view(A_, 3592, "", a=2, e=E + 1)
        Css = view(A_, 3722, "", b=NB, a=2, e=E + 1)
        qm_flat = [A_[:, 4762 + n * 288:4762 + (n + 1) * 288] for n in range(2)]
        kdm = view(A_, 5338, "", b=NB, h=HM, e=E)
        cmask = A_[:, 7386:7386 + P + NS]
        bmask = A_[0:NS, 7546:7554]
        tmpC = view(A_, 7554, "", b=NB, e=E + 1)
        hstat = sb("hstat", [P, 2, NTILE, HM])
        hrstd = sb("hrstd", [P, 2, NTILE, HM])
        adn = sb("adn", [P, HM])
        d_in, d_zero = sem("d_in"), sem("d_zero")
        g1, g2 = sem("mlstm_scores"), sem("mlstm_sums")
        m_biased, m_exp, m_w, m_kd = sem("m_biased"), sem("m_exp"), sem("m_w"), sem("m_kd")
        m_state, m_taken, m_masked, m_upd, m_updt = (sem("m_state"), sem("m_taken"), sem("m_masked"), sem("m_upd"),
                                                     sem("m_updt"))
        st_out = sem("state_stored")

        def masked_q(flat):
            return (flat[:, 0:256].rearrange("p (b t) -> p b t", b=NB),
                    flat.rearrange("p (b s) -> p b s", s=36)[:, :, 0:NT])

        def halves():
            return [(a, h2, slice(64 * h2, 64 * h2 + 64)) for a in range(2) for h2 in range(2)]

        def phase_d1_sync(sp):
            sp.dma_start(cmask, const("c_causal")).then_inc(d_in, 16)
            sp.dma_start(bmask, const("c_batch")).then_inc(d_in, 16)
            for a, h2, pt in halves():
                sp.dma_start(Css[pt, :, a, 0:E], i_["state_mlstm_C"][0, :, 2 * a + h2].rearrange("b k v -> k b v"))\
                  .then_inc(d_in, 16)
                sp.dma_start(Css[pt, :, a, E:E + 1], i_["state_mlstm_n"][0, :, 2 * a + h2:2 * a + h2 + 1].rearrange(
                    "b o k -> k b o"), allow_slow_non_contiguous=True).then_inc(d_in, 16)
            sp.wait_ge(m_state, NCH)
            for a, h2, pt in halves():
                h = 2 * a + h2
                sp.dma_start(o_["p_C"][0, 0, h], Cst[pt, a, 0:E]).then_inc(st_out, 16)
                sp.dma_start(o_["p_n"][0, 0, h:h + 1].rearrange("o k -> k o"), Cst[pt, a, E:E + 1],
                             allow_slow_non_contiguous=True).then_inc(st_out, 16)
            sp.wait_ge(m_upd, 4)
            for a, h2, pt in halves():
                h = 2 * a + h2
                sp.dma_start(o_["s_C"][0, :, h].rearrange("b k v -> k b v"), Css[pt, :, a, 0:E]).then_inc(st_out, 16)
                sp.dma_start(o_["s_n"][0, :, h:h + 1].rearrange("b o k -> k b o"), Css[pt, :, a, E:E + 1],
                             allow_slow_non_contiguous=True).then_inc(st_out, 16)
            sp.wait_ge(st_out, 16 * 16)

        def phase_d1_pe(pe):
            def scores(c):
                r, tt = rows(c), tile_tokens(c)
                if c >= 2:
                    pe.wait_ge(m_w, c - 1)
                if c >= 1:
                    pe.wait_ge(m_kd, c)
                for h in (0, 2, 1, 3):
                    pt = slice(64 * (h % 2), 64 * (h % 2) + 64)
                    mm = pe.matmul(PS[0:r, c % 2, h * P:h * P + r], mqk[pt, 2 + h // 2, tt], mqk[pt, h // 2, tt],
                                   start=True, stop=True)
                    if h == 2:
                        link("pe", pe, mm)
                for h in range(HM):
                    pe.matmul(PS[0:r, 2 + c % 2, h * P:h * P + r], selv[:, h, 0:r], bm[:, tt], start=True, stop=True)
                for a in range(2):
                    t = pe.transpose(PS[0:r, 4, a * P:(a + 1) * P], mqk[:, 2 + a, tt], ident[:, :])
                t.then_inc(g1, 1)

            def sums(c):
                r, tt = rows(c), tile_tokens(c)
                pe.wait_ge(m_kd, c + 1)
                pe.wait_ge(m_w, c + 1)
                pe.wait_ge(d_zero, 1)
                if c >= 1:
                    pe.wait_ge(m_state, c)
                    pe.wait_ge(m_taken, c)
                if c == NCH:
                    pe.wait_ge(m_masked, 1)
                for h in (0, 2, 1, 3):
                    pt = slice(64 * (h % 2), 64 * (h % 2) + 64)
                    o = PS[0:r, 5, h * (E + 1):(h + 1) * (E + 1)]
                    if c < NCH:
                        mm = pe.matmul(o, mqk[pt, h // 2, tt], Cst[pt, h // 2, :], start=True, stop=True)
                    else:
                        for b in range(NB):
                            mm = pe.matmul(o, masked_q(qm_flat[h // 2])[0][pt, b, :], Css[pt, b, h // 2, :],
                                           start=(b == 0), stop=(b == NB - 1))
                    if h == 2:
                        link("pe", pe, mm)
                for h in range(HM):
                    mm = pe.matmul(PS[0:r, 6, h * (E + 1):(h + 1) * (E + 1)], Wm[c % 2][0:r, h, 0:r], vm[0:r, c, h, :],
                                   start=True, stop=True)
                if c < NCH:
                    for a in range(2):
                        mm = pe.matmul(PS[:, 7, a * 130:(a + 1) * 130],
                                       kd[c % 2][0:r, 2 * a:2 * a + 2, :].rearrange("p h e -> p (h e)"),
                                       vm[0:r, c, 2 * a:2 * a + 2, :].rearrange("p h e -> p (h e)"), start=True, stop=True)
                mm.then_inc(g2, 1)

            pe.wait_ge(d_in, 160)
            scores(0)
            for c in range(NTILE):
                if c + 1 < NTILE:
                    scores(c + 1)
                sums(c)
            for a in range(2):
                if a:
                    pe.wait_ge(m_upd, 2)
                for b in range(NB):
                    mm = pe.matmul(PS[:, b // 2, (b % 2) * 130:(b % 2 + 1) * 130],
                                   kdm[0:NS, b, 2 * a:2 * a + 2, :].rearrange("p h e -> p (h e)"),
                                   vm[0:NS, NCH, 2 * a:2 * a + 2, :].rearrange("p h e -> p (h e)"), start=True, stop=True)
                mm.then_inc(m_updt, 1)

        def phase_d1_act(act):
            for c in range(NTILE):
                r = rows(c)
                act.wait_ge(m_biased, c + 1)
                for h in range(HM):
                    e = act.activation(Dm[c % 2][0:r, h, 0:r], Dm[c % 2][0:r, h, 0:r], ACT.Exp,
                                       bias=gcol[0:r, c, 96 + h:97 + h])
                e.then_inc(m_exp, 1)

        def phase_d1_dve(dve):
            def biased_(c):
                r = rows(c)
                dve.wait_ge(g1, c + 1)
                m = cmask[0:r, 0:P] if c < NCH else cmask[0:r, P:P + NS]
                dve.tensor_tensor(Dm[c % 2][0:r, :, 0:r],
                                  PS[0:r, 2 + c % 2, :].rearrange("p (h t) -> p h t", t=P)[:, :, 0:r],
                                  m.unsqueeze(1).to_broadcast([r, HM, r]), ALU.add).then_inc(m_biased, 1)

            def col(c, at, n):
                return gcol[0:rows(c), c, at:at + HM].unsqueeze(2).to_broadcast([rows(c), HM, n])

            dve.wait_ge(d_in, 160)
            dve.memset(Cst[:, :, :], 0.0).then_inc(d_zero, 1)
            for a in range(2):
                link("dve", dve, dve.memset(qm_flat[a], 0.0))
                dve.tensor_copy(masked_q(qm_flat[a])[1], sample(mqk[:, a, :]))
            biased_(0)
            for c in range(NTILE):
                r = rows(c)
                if c >= 2:
                    dve.wait_ge(g2, c - 1)
                dve.tensor_tensor(kd[c % 2][0:r], PS[0:r, 4, 0:256].rearrange("p (h e) -> p h e", e=E),
                                  col(c, 64, E), ALU.mult).then_inc(m_kd, 1)
                if c + 1 < NTILE:
                    biased_(c + 1)
                dve.wait_ge(m_exp, c + 1)
                dve.tensor_tensor(Wm[c % 2][0:r, :, 0:r], Dm[c % 2][0:r, :, 0:r],
                                  PS[0:r, c % 2, :].rearrange("p (h t) -> p h t", t=P)[:, :, 0:r], ALU.mult)\
                   .then_inc(m_w, 1)
                if c == NCH:
                    dve.wait_ge(m_kd, c + 1)
                    for h in range(HM):
                        ins = dve.tensor_tensor(kdm[0:NS, :, h, :], kd[c % 2][0:NS, h, :].unsqueeze(1).to_broadcast([NS, NB, E]),
                                                bmask.unsqueeze(2).to_broadcast([NS, NB, E]), ALU.mult)
                    ins.then_inc(m_masked, 1)
                dve.wait_ge(g2, c + 1)
                if c < NCH:
                    for a, h2, pt in halves():
                        ins = dve.scalar_tensor_tensor(Cst[pt, a, :], Cst[pt, a, :], glc[pt, a, c:c + 1],
                                                       PS[pt, 7, a * 130 + h2 * 65:a * 130 + h2 * 65 + 65],
                                                       ALU.mult, ALU.add)
                    ins.then_inc(m_state, 1)
                heads4 = lambda bank: PS[0:r, bank, 0:4 * (E + 1)].rearrange("p (h e) -> p h e", e=E + 1)
                link("dve", dve, dve.tensor_tensor(tmpN[0:r], heads4(5), col(c, 0, E + 1), ALU.mult))
                dve.tensor_tensor(nd[0:r], heads4(6), tmpN[0:r], ALU.add).then_inc(m_taken, 1)
                dve.wait_ge(m_taken, c + 1)
                den = nd[0:r, :, E]
                link("dve", dve, dve.scalar_tensor_tensor(adn[0:r, :], den, -1.0, den, ALU.mult, ALU.max))
                link("dve", dve, dve.tensor_tensor(adn[0:r, :], adn[0:r, :], gcol[0:r, c, 32:36], ALU.max))
                link("dve", dve, dve.reciprocal(adn[0:r, :], adn[0:r, :]))
                link("dve", dve, dve.tensor_tensor(hh[0:r], nd[0:r, :, 0:E],
                                                   adn[0:r, :].unsqueeze(2).to_broadcast([r, HM, E]), ALU.mult))
                gated_head(dve, c, hh[0:r], mo, 512)
                link("dve", dve, dve.tensor_tensor(sq[0:r], hh[0:r], hh[0:r], ALU.mult))
                link("dve", dve, dve.tensor_reduce(hstat[0:r, 0, c, :], sq[0:r], AX.X, ALU.add))
            for a in range(2):
                dve.wait_ge(m_updt, a + 1)
                for h2 in range(2):
                    pt = slice(64 * h2, 64 * h2 + 64)
                    link("dve", dve, dve.tensor_tensor(tmpC[pt], Css[pt, :, a, :],
                                                       glc[pt, a, 8:16].unsqueeze(2).to_broadcast([64, NB, E + 1]), ALU.mult))
                    upd = PS[pt, 0:4, 0:260].rearrange("p a (b e) -> p a b e", b=2)[:, :, :, h2 * 65:h2 * 65 + 65]
                    dve.tensor_tensor(Css[pt, :, a, :].rearrange("p (x y) e -> p x y e", y=2),
                                      tmpC[pt].rearrange("p (x y) e -> p x y e", y=2), upd, ALU.add).then_inc(m_upd, 1)

        def gated_head(eng, c, h, gate, at):
            r = rows(c)
            eng.tensor_tensor(mix[0:r, c, at:at + 256].rearrange("p (h e) -> p h e", e=E), h,
                              gate[0:r, c, :].rearrange("p (h e) -> p h e", e=E), ALU.mult)

        NX = NLEV + 1
        X = [view(R_aqk, n * 2304, "", l=NX, a=2, t=P) for n in range(2)]
        AM = [view(R_aqk, 4608 + n * 1024, "", l=NLEV, t=P) for n in range(2)]
        Sst = view(R_aqk, 6656, "", a=2, e=E)
        Sss = view(R_aqk, 6784, "", b=NB, a=2, e=E)
        kl = [R_aqk[:, 7808 + n * 256:8064 + n * 256] for n in range(2)]
        lev = view(R_ring, 1664, "", l=NLEV, t=P)
        hqm_flat = [R_ring[:, 2688 + n * 288:2688 + (n + 1) * 288] for n in range(2)]
        klm = view(R_ring, 3264, "", b=NB, n=256)
        osb = view(R_ring, 5312, "", h=HM, e=E)
        osq = view(R_ring, 5568, "", h=HM, e=E)
        tmpS = view(R_aqk, 0, "", b=NB, e=E)
        bmask2 = R_ring[0:NS, 5824:5832]
        eb = sb("eb", [P, 2, 2])
        ebs = sb("ebs", [P, 2, NB])
        h_in, h_zero, h_arg, h_exp, h_prod = sem("h_in"), sem("h_zero"), sem("h_arg"), sem("h_exp"), sem("h_prod")
        a_psum, a_masked, kl_psum, kl_taken = sem("a_psum"), sem("a_masked"), sem("kl_psum"), sem("kl_taken")
        ho_psum, ho_copied, ho_taken, h_state = sem("ho_psum"), sem("ho_copied"), sem("ho_taken"), sem("h_state")
        h_masked, hu_psum, h_upd = sem("h_masked"), sem("hu_psum"), sem("h_upd")

        def split(ap, m):
            return ap.rearrange("p a (n z m) -> p a n z m", z=2, m=m)

        def levels_of(c):
            return range(NLEV - 1) if c < NCH else range(NLEV - 3, NLEV - 1)

        def phase_d2_sync(sp):
            sp.dma_start(lev, const("c_levels")).then_inc(h_in, 16)
            sp.dma_start(bmask2, const("c_batch")).then_inc(h_in, 16)
            for a, h2, pt in halves():
                sp.dma_start(Sss[pt, :, a, :], i_["state_hgrn_S"][0, :, 2 * a + h2].rearrange("b k v -> k b v"))\
                  .then_inc(h_in, 16)
            sp.wait_ge(h_state, NCH)
            for a, h2, pt in halves():
                sp.dma_start(o_["p_S"][0, 0, 2 * a + h2], Sst[pt, a, :]).then_inc(st_out, 16)
            sp.wait_ge(h_upd, 4)
            for a, h2, pt in halves():
                sp.dma_start(o_["s_S"][0, :, 2 * a + h2].rearrange("b k v -> k b v"), Sss[pt, :, a, :]).then_inc(st_out, 16)
            sp.wait_ge(st_out, 16 * 24)

        def phase_d2_gps(pool):
            for c in range(NTILE):
                r, tt = rows(c), tile_tokens(c)
                x = X[c % 2]
                if c >= 2:
                    pool.wait_ge(ho_psum, c - 1)
                    pool.wait_ge(kl_psum, c - 1)
                b = hb[:, :, tt]
                for l in levels_of(c):
                    m = 64 >> l
                    bb, xx = split(b, m), split(x[:, l, :, 0:r], m)
                    mid = bb[:, :, :, 0, m - 1:m].to_broadcast([P, 2, r // (2 * m), m])
                    pool.tensor_tensor(xx[:, :, :, 1, :], bb[:, :, :, 1, :], mid, ALU.subtract)
                    pool.tensor_tensor(xx[:, :, :, 0, :], mid, bb[:, :, :, 0, :], ALU.subtract)
                pool.tensor_copy(x[:, NLEV - 1, :, 0:r], b)
                seglen = P if c < NCH else NT
                bs = b.rearrange("p a (n s) -> p a n s", s=seglen)
                last = bs[:, :, :, seglen - 1:seglen].to_broadcast([P, 2, r // seglen, seglen])
                pool.tensor_tensor(x[:, NLEV, :, 0:r].rearrange("p a (n s) -> p a n s", s=seglen), last, bs,
                                   ALU.subtract).then_inc(h_arg, 1)

        def phase_d2_act(act):
            for c in range(NTILE):
                r = rows(c)
                x = X[c % 2]
                act.wait_ge(h_arg, c + 1)
                l0 = 0 if c < NCH else NLEV - 3
                act.activation(x[:, l0:, :, 0:r], x[:, l0:, :, 0:r], ACT.Exp).then_inc(h_exp, 1)
                if c >= 1:
                    out_copy(act, c - 1)
            out_copy(act, NTILE - 1)

        def out_copy(act, c):
            r = rows(c)
            act.wait_ge(ho_psum, c + 1)
            if c >= 1:
                act.wait_ge(ho_taken, c)
            src = PS[0:r, 4 + c % 2, 0:256].rearrange("p (h e) -> p h e", e=E)
            act.activation(osq[0:r], src, ACT.Square).then_inc(ho_copied, 1)

        def phase_d2_dve(dve):
            dve.wait_ge(h_in, 96)
            for a in range(2):
                link("dve", dve, dve.memset(hqm_flat[a], 0.0))
            link("dve", dve, dve.memset(Sst[:, :, :], 0.0))
            dve.nop().then_inc(h_zero, 1)

            def products(c):
                r, tt = rows(c), tile_tokens(c)
                x = X[c % 2]
                dve.wait_ge(h_exp, c + 1)
                q, k = hqk[:, 0:2, tt], hqk[:, 2:4, tt]
                if c < NCH:
                    link("dve", dve, dve.tensor_copy(eb[:, :, c % 2:c % 2 + 1], x[:, NLEV - 1, :, P - 1:P]))
                else:
                    link("dve", dve, dve.tensor_copy(ebs[:, :, :], x[:, NLEV - 1, :, NT - 1:NS:NT]))
                for l in levels_of(c):
                    m = 64 >> l
                    xx = split(x[:, l, :, 0:r], m)
                    dve.tensor_tensor(xx[:, :, :, 1, :], xx[:, :, :, 1, :], split(q, m)[:, :, :, 1, :], ALU.mult)
                    dve.tensor_tensor(xx[:, :, :, 0, :], xx[:, :, :, 0, :], split(k, m)[:, :, :, 0, :], ALU.mult)
                link("dve", dve, dve.tensor_tensor(x[:, NLEV - 1, :, 0:r], x[:, NLEV - 1, :, 0:r], q, ALU.mult))
                if c == NCH:
                    for a in range(2):
                        link("dve", dve, dve.tensor_copy(masked_q(hqm_flat[a])[1],
                                                         x[:, NLEV - 1, a, 0:r].rearrange("p (b t) -> p b t", t=NT)))
                dve.tensor_tensor(x[:, NLEV, :, 0:r], x[:, NLEV, :, 0:r], k, ALU.mult).then_inc(h_prod, 1)

            products(0)
            for c in range(NTILE):
                r = rows(c)
                for h in range(HM):
                    j = c * HM + h
                    dve.wait_ge(a_psum, j + 1)
                    if j >= 2:
                        dve.wait_ge(am_used, j - 1)
                    l0 = 0 if c < NCH else NLEV - 3
                    src = PS[0:r, 2 * (j % 2):2 * (j % 2) + 2, :].rearrange("p b (l t) -> p (b l) t", t=P)
                    dve.tensor_tensor(AM[j % 2][0:r, l0:, 0:r], src[:, l0:, 0:r], lev[0:r, l0:, 0:r], ALU.mult)\
                       .then_inc(a_masked, 1)
                    if h == 1:
                        dve.wait_ge(kl_psum, c + 1)
                        dve.tensor_copy(kl[c % 2][0:r, :], PS[0:r, 6, 0:256]).then_inc(kl_taken, 1)
                if c == NCH:
                    dve.wait_ge(kl_taken, c + 1)
                    link("dve", dve, dve.tensor_tensor(klm[0:NS], kl[c % 2][0:NS, :].unsqueeze(1).to_broadcast([NS, NB, 256]),
                                                       bmask2.unsqueeze(2).to_broadcast([NS, NB, 256]), ALU.mult))
                    dve.nop().then_inc(h_masked, 1)
                if c + 1 < NTILE:
                    products(c + 1)
                dve.wait_ge(ho_psum, c + 1)
                if c < NCH:
                    for a, h2, pt in halves():
                        ins = dve.scalar_tensor_tensor(Sst[pt, a, :], Sst[pt, a, :], eb[pt, a, c % 2:c % 2 + 1],
                                                       PS[pt, 7, a * P + h2 * 64:a * P + h2 * 64 + 64], ALU.mult, ALU.add)
                    ins.then_inc(h_state, 1)
                dve.wait_ge(ho_copied, c + 1)
                gated_head(dve, c, PS[0:r, 4 + c % 2, 0:256].rearrange("p (h e) -> p h e", e=E), hg, 768)
                dve.tensor_reduce(hstat[0:r, 1, c, :], osq[0:r], AX.X, ALU.add).then_inc(ho_taken, 1)
            for a in range(2):
                if a:
                    dve.wait_ge(hu_psum, 1)
                for h2 in range(2):
                    pt = slice(64 * h2, 64 * h2 + 64)
                    link("dve", dve, dve.tensor_tensor(tmpS[pt], Sss[pt, :, a, :],
                                                       ebs[pt, a, :].unsqueeze(2).to_broadcast([64, NB, E]), ALU.mult))
                    upd = PS[pt, 0:2, :].rearrange("p x (b e) -> p x b e", b=4)[:, :, :, h2 * 64:h2 * 64 + 64]
                    dve.tensor_tensor(Sss[pt, :, a, :].rearrange("p (x y) e -> p x y e", y=4),
                                      tmpS[pt].rearrange("p (x y) e -> p x y e", y=4), upd, ALU.add).then_inc(h_upd, 1)

        am_used, inter_done = sem("am_used"), sem("inter_done")

        def phase_d2_pe(pe):
            def level_scores(c, h):
                r, tt = rows(c), tile_tokens(c)
                j = c * HM + h
                if h == 0:
                    pe.wait_ge(h_prod, c + 1)
                if j >= 2:
                    pe.wait_ge(a_masked, j - 1)
                pt, a = slice(64 * (h % 2), 64 * (h % 2) + 64), h // 2
                x = X[c % 2]
                for l in levels_of(c):
                    pe.matmul(PS[0:r, 2 * (j % 2) + l // 4, (l % 4) * P:(l % 4) * P + r], x[pt, l, a, 0:r], x[pt, l, a, 0:r],
                              start=True, stop=True)
                pe.matmul(PS[0:r, 2 * (j % 2) + 1, 3 * P:3 * P + r], hqk[pt, 2 + a, tt], hqk[pt, a, tt],
                          start=True, stop=True).then_inc(a_psum, 1)

            def apply(c, h):
                r = rows(c)
                j = c * HM + h
                pt, a = slice(64 * (h % 2), 64 * (h % 2) + 64), h // 2
                pe.wait_ge(a_masked, j + 1)
                if h == 0:
                    if c >= 2:
                        pe.wait_ge(ho_taken, c - 1)
                    pe.wait_ge(h_zero, 1)
                    if c >= 1:
                        pe.wait_ge(h_state, c)
                o = PS[0:r, 4 + c % 2, h * E:(h + 1) * E]
                ls = [*levels_of(c), NLEV - 1]
                for n, l in enumerate(ls):
                    mm = pe.matmul(o, AM[j % 2][0:r, l, 0:r], hi[0:r, c, h * E:(h + 1) * E], start=(n == 0), stop=False)
                mm.then_inc(am_used, 1)
                if j >= 1:
                    pe.wait_ge(inter_done, j)
                if c < NCH:
                    mm = pe.matmul(o, X[c % 2][pt, NLEV - 1, a, 0:r], Sst[pt, a, :], start=False, stop=True)
                else:
                    for b in range(NB):
                        mm = pe.matmul(o, masked_q(hqm_flat[a])[0][pt, b, :], Sss[pt, b, a, :], start=False, stop=(b == NB - 1))
                mm.then_inc(inter_done, 1)

            def keys(c):
                r = rows(c)
                if c >= 1:
                    pe.wait_ge(kl_taken, c)
                for a in range(2):
                    t = pe.transpose(PS[0:r, 6, a * P:(a + 1) * P], X[c % 2][:, NLEV, a, 0:r], ident[:, :])
                t.then_inc(kl_psum, 1)

            pe.wait_ge(h_in, 96)
            level_scores(0, 0)
            for c in range(NTILE):
                r = rows(c)
                level_scores(c, 1)
                keys(c)
                apply(c, 0)
                level_scores(c, 2)
                apply(c, 1)
                level_scores(c, 3)
                apply(c, 2)
                if c + 1 < NTILE and False:
                    level_scores(c + 1, 0)
                apply(c, 3)
                pe.wait_ge(kl_taken, c + 1)
                if c < NCH:
                    for a in range(2):
                        mm = pe.matmul(PS[:, 7, a * P:(a + 1) * P], kl[c % 2][:, a * P:(a + 1) * P],
                                       hi[:, c, a * P:(a + 1) * P], start=True, stop=True)
                    mm.then_inc(ho_psum, 1)
                    level_scores(c + 1, 0)
                else:
                    pe.wait_ge(h_masked, 1)
                    for a in range(2):
                        if a:
                            pe.wait_ge(h_upd, 2)
                        for b in range(NB):
                            mm = pe.matmul(PS[:, b // 4, (b % 4) * P:(b % 4 + 1) * P], klm[0:NS, b, a * P:(a + 1) * P],
                                           hi[0:NS, c, a * P:(a + 1) * P], start=True, stop=True)
                        mm.then_inc(hu_psum if a else ho_psum, 1)

        NK8 = 8
        NSLOT = 5
        cache = [view(R_rec, n * 4096, "", k=NK8, n=512) for n in range(NSLOT)]
        ktile = [view(R_ring, 1664 + n * 512, "", a=4, s=P) for n in range(2)]
        sts = view(R_ring, 2688, "", k=NK8, q=P)
        pb = R_ring[:, 3712:3712 + NKEY]
        bkey = R_ring[:, 4640:4640 + NKEY]
        bother = view(R_ring, 5568, "", g=2, n=NS)
        rexp = R_ring[0:33, 5632:6144].rearrange("p (t c) -> p t c", t=NT)
        ptk = view(R_rec, 20480, "", k=NK8 + 1, q=P)
        keyrows = R_rec[0:33, 20480:20480 + NT * NKEY].rearrange("p (t n) -> p t n", t=NT)
        mixT = aqk
        ra = small[0:33, 0:H]
        estat = sb("estat", [P, 8])
        e_in, ra_ready, rexp_ready, bkey_psum, bkey_ready = (sem("e_in"), sem("ra_ready"), sem("rexp_ready"),
                                                             sem("bkey_psum"), sem("bkey_ready"))
        cache_in = [sem(f"cache_in{n}") for n in range(NSLOT)]
        kt_psum, st_psum, sb_psum = sem("kt_psum"), sem("st_psum"), sem("sb_psum")
        kt_taken = [sem("kt_taken_act"), sem("kt_taken_dve")]
        sts_ready, e_min, e_exp, p_ready = sem("sts_ready"), sem("e_min"), sem("e_exp"), sem("p_ready")
        pk_psum, ptk_ready, eo_psum, eo_taken = sem("pk_psum"), sem("ptk_ready"), sem("eo_psum"), sem("eo_taken")
        ITEMS = [("cache_attn_" + kv, 4 * g + b) for g in range(2) for kv in "kv" for b in range(4)]

        def krows(k):
            return NFAR if k < 4 else P

        def kcols(k):
            return slice(k * NFAR, (k + 1) * NFAR) if k < 4 else slice(4 * NFAR + (k - 4) * P, 4 * NFAR + (k - 3) * P)

        def item_in(eng, m):
            eng.wait_ge(cache_in[m % NSLOT], 32 * (m // NSLOT + 1))

        def phase_e_sync(sp):
            sp.dma_start(keyrows, const("c_bias_keys")).then_inc(e_in, 16)
            sp.dma_start(ra[0:32, :], i_["rel_bias"]).then_inc(e_in, 16)
            sp.dma_start(bother, const("c_other_batch")).then_inc(e_in, 16)
            for m, (name, b) in enumerate(ITEMS):
                if m >= NSLOT:
                    f = m - NSLOT
                    g, kv, fb = f // 8, (f % 8) // 4, f % 4
                    if kv == 0:
                        sp.wait_ge(kt_psum, NK8 * (4 * g + fb + 1))
                    else:
                        sp.wait_ge(eo_psum, 4 * g + fb + 1)
                rows_ = i_[name][0, b].rearrange("s h e -> s (h e)")
                far = rows_[0:FAR, :].rearrange("(m s) n -> m s n", s=16)[:, 0:4, :]
                near = rows_[FAR:WB, :].rearrange("(p k) n -> p k n", k=4)
                sp.dma_start(cache[m % NSLOT][0:NFAR, 0:4, :], far).then_inc(cache_in[m % NSLOT], 16)
                sp.dma_start(cache[m % NSLOT][:, 4:8, :], near).then_inc(cache_in[m % NSLOT], 16)

        def phase_e_pe(pe):
            pe.wait_ge(e_in, 48)
            pe.wait_ge(rexp_ready, 1)
            for half in range(2):
                for t in range(NT):
                    mm = pe.matmul(PS[:, half, 0:NKEY // 2], rexp[:, t, :],
                                   keyrows[:, t, half * (NKEY // 2):(half + 1) * (NKEY // 2)],
                                   start=(t == 0), stop=(t == NT - 1))
                mm.then_inc(bkey_psum, 1)
            pe.wait_ge(bkey_ready, 1)
            for g in range(2):
                jobs = [(b, k) for b in range(4) for k in range(NK8)]
                for j in range(len(jobs) + 1):
                    if j < len(jobs):
                        b, k = jobs[j]
                        J = g * 32 + j
                        if k == 0:
                            item_in(pe, 8 * g + b)
                        if J >= 2:
                            pe.wait_ge(kt_taken[J % 2], J // 2)
                        r = krows(k)
                        for a in range(4):
                            t = pe.transpose(PS[:, J % 2, a * P:a * P + r],
                                             cache[(8 * g + b) % NSLOT][0:r, k, a * P:(a + 1) * P], ident[0:r, 0:r])
                        t.then_inc(kt_psum, 1)
                    if j >= 1:
                        b, k = jobs[j - 1]
                        J = g * 32 + j - 1
                        r = krows(k)
                        pe.wait_ge(kt_taken[J % 2], J // 2 + 1)
                        if g and j == 1:
                            pe.wait_ge(sts_ready, 2)
                        for a in range(4):
                            mm = pe.matmul(PS[0:r, 2 + k // 4, (k % 4) * P + b * 32:(k % 4) * P + (b + 1) * 32],
                                           ktile[J % 2][:, a, 0:r],
                                           qblk[:, a, 4 * g + b, :, :].rearrange("p h t -> p (h t)"),
                                           start=(a == 0), stop=(a == 3))
                        mm.then_inc(st_psum, 1)
                pe.wait_ge(sts_ready, 2 * g + 2)
                for k in range(NK8):
                    r = krows(k)
                    c = (k % 4) * r
                    pe.transpose(PS[:, 4 + k // 4, c:c + r], sts[0:r, k, :], ident[0:r, 0:r])
                for a in range(4):
                    mm = pe.matmul(PS[:, 6, 0:NS], qblk[:, a, 4 * g:4 * g + 4, :, :].rearrange("p b h t -> p (b h t)"),
                                   knew[:, a, :], start=(a == 0), stop=(a == 3))
                mm.then_inc(sb_psum, 1)
                pe.wait_ge(p_ready, g + 1)
                for k in range(NK8 + 1):
                    r = krows(k) if k < NK8 else NS
                    cols = kcols(k) if k < NK8 else slice(NKEY - NS, NKEY)
                    bank, at = ((k // 4, (k % 4) * P) if k < NK8 else (2, 0))
                    t = pe.transpose(PS[0:r, bank, at:at + P], pb[:, cols], ident[:, :])
                t.then_inc(pk_psum, 1)
                pe.wait_ge(ptk_ready, g + 1)
                if g:
                    pe.wait_ge(eo_taken, 2)
                for b in range(4):
                    item_in(pe, 8 * g + 4 + b)
                    v = cache[(8 * g + 4 + b) % NSLOT]
                    for a in range(4):
                        o = PS[:, 7, b * 32 + a * 8:b * 32 + (a + 1) * 8]
                        for k in range(NK8):
                            r = krows(k)
                            pe.matmul(o, v[0:r, k, a * P:(a + 1) * P], ptk[0:r, k, b * 32 + a * 8:b * 32 + a * 8 + 8],
                                      start=(k == 0), stop=False)
                        mm = pe.matmul(o, vnew[0:NS, a * P:(a + 1) * P], ptk[0:NS, NK8, b * 32 + a * 8:b * 32 + a * 8 + 8],
                                       start=False, stop=True)
                    mm.then_inc(eo_psum, 1)

        def take_kt(eng, copy, J):
            g, j = J // 32, J % 32
            b, k = j // NK8, j % NK8
            r = krows(k)
            eng.wait_ge(kt_psum, J + 1)
            if J >= 2:
                eng.wait_ge(st_psum, J - 1)
            copy(ktile[J % 2][:, :, 0:r], PS[:, J % 2, :].rearrange("p (a t) -> p a t", t=P)[:, :, 0:r])\
                .then_inc(kt_taken[J % 2], 1)

        def phase_e_act(act):
            for g in range(2):
                for J in range(32 * g, 32 * g + 32, 2):
                    take_kt(act, lambda o, s: act.activation(o, s, ACT.Copy), J)
                act.wait_ge(e_min, g + 1)
                act.activation(pb, pb, ACT.Exp, bias=estat[:, 3:4], scale=-1.0,
                               accum_out=estat[:, 4:5]).then_inc(e_exp, 1)

        def phase_e_dve(dve):
            dve.wait_ge(e_in, 48)
            dve.memset(ra[32:33, :], 1.0).then_inc(ra_ready, 1)
            link("dve", dve, dve.memset(rexp, 0.0))
            dve.wait_ge(ra_ready, 1)
            for t in range(NT):
                ins = dve.tensor_copy(rexp[:, t, :].rearrange("p (b h t) -> p b h t", b=4, h=H)[:, :, :, t],
                                      ra.unsqueeze(1).to_broadcast([33, 4, H]))
            ins.then_inc(rexp_ready, 1)
            dve.wait_ge(bkey_psum, 2)
            link("dve", dve, dve.tensor_copy(bkey.rearrange("p (a n) -> p a n", a=2), PS[:, 0:2, 0:NKEY // 2]))
            link("dve", dve, dve.tensor_tensor(bother, bother, bkey[:, NKEY - NS:].unsqueeze(1).to_broadcast([P, 2, NS]), ALU.add))
            dve.nop().then_inc(bkey_ready, 1)
            for g in range(2):
                for J in range(32 * g + 1, 32 * g + 32, 2):
                    take_kt(dve, dve.tensor_copy, J)
                dve.wait_ge(st_psum, 32 * (g + 1))
                if g:
                    dve.wait_ge(sb_psum, g)
                dve.tensor_copy(sts[0:NFAR, 0:4, :], PS[0:NFAR, 2, :].rearrange("p (k q) -> p k q", q=P)).then_inc(sts_ready, 1)
                dve.tensor_copy(sts[:, 4:8, :], PS[:, 3, :].rearrange("p (k q) -> p k q", q=P)).then_inc(sts_ready, 1)
                dve.wait_ge(sb_psum, g + 1)
                if g:
                    dve.wait_ge(pk_psum, g)
                segs = ((0, 4 * NFAR, 4, bkey[:, 0:4 * NFAR]), (4 * NFAR, 4 * P, 5, bkey[:, 4 * NFAR:NKEY - NS]),
                        (NKEY - NS, NS, 6, bother[:, g, :]))
                for n, (at, w, bank, bias) in enumerate(segs):
                    link("dve", dve, dve.tensor_tensor_reduce(pb[:, at:at + w], PS[:, bank, 0:w], bias, -1.0, 3e38,
                                                              ALU.add, ALU.min, estat[:, n:n + 1]))
                dve.tensor_reduce(estat[:, 3:4], estat[:, 0:3], AX.X, ALU.min).then_inc(e_min, 1)
                dve.wait_ge(e_exp, g + 1)
                link("dve", dve, dve.reciprocal(estat[:, 5:6], estat[:, 4:5]))
                dve.tensor_scalar(pb, pb, estat[:, 5:6], None, ALU.mult).then_inc(p_ready, 1)
                dve.wait_ge(pk_psum, g + 1)
                if g:
                    dve.wait_ge(eo_psum, 4)
                for k0, bank, r in ((0, 0, NFAR), (4, 1, P)):
                    dve.tensor_copy(ptk[0:r, k0:k0 + 4, :], PS[0:r, bank, :].rearrange("p (k q) -> p k q", q=P))
                dve.tensor_copy(ptk[0:NS, NK8, :], PS[0:NS, 2, 0:P]).then_inc(ptk_ready, 1)
                dve.wait_ge(eo_psum, 4 * g + 4)
                for h2 in range(2):
                    pt = slice(64 * h2, 64 * h2 + 64)
                    for a in range(4):
                        ins = dve.tensor_copy(mixT[pt, a, S + 16 * g:S + 16 * g + 16].rearrange("p (b t) -> p b t", t=NT),
                                              PS[pt, 7, 0:P].rearrange("p (b a z t) -> p b a z t", b=4, a=4, z=2)[:, :, a, h2, :])
                    ins.then_inc(eo_taken, 1)

        head_ms, head_rms, f_scaled, f_psum, f_taken = (sem("head_ms"), sem("head_rms"), sem("f_scaled"),
                                                        sem("f_psum"), sem("f_taken"))
        PARTS = ((slice(0, P), slice(0, NCH)), (slice(0, NS), slice(NCH, NTILE)))

        def phase_f1_act(act):
            for n, (pt, cs) in enumerate(PARTS):
                act.wait_ge(head_ms, n + 1)
                act.activation(hrstd[pt, :, cs, :], hstat[pt, :, cs, :], ACT.Sqrt).then_inc(head_rms, 1)

        def phase_f1_dve(dve):
            dve.memset(gout[:, 0:4], 1.0)
            for pt, cs in PARTS:
                dve.tensor_scalar(hstat[pt, :, cs, :], hstat[pt, :, cs, :], 1.0 / E, EPS, ALU.mult, ALU.add)\
                   .then_inc(head_ms, 1)
            for n, (pt, cs) in enumerate(PARTS):
                dve.wait_ge(head_rms, n + 1)
                link("dve", dve, dve.reciprocal(hrstd[pt, :, cs, :], hrstd[pt, :, cs, :]))

            for i in range(NTILE + 2):
                if i < NTILE:
                    r = rows(i)
                    for w in range(2):
                        part = mix[0:r, i, 512 + 256 * w:768 + 256 * w].rearrange("p (h e) -> p h e", e=E)
                        ins = dve.tensor_tensor(part, part, hrstd[0:r, w, i, :].unsqueeze(2).to_broadcast([r, HM, E]), ALU.mult)
                    ins.then_inc(f_scaled, 1)
                if i >= 2:
                    j = i - 2
                    for kk in range(2) if j < NCH else (1,):
                        dve.wait_ge(f_psum, 2 * j + (kk if j < NCH else 0) + 1)
                        src = PS[:, 2 * (j % 2) + kk, :].rearrange("p (k t) -> p k t", t=P)[:, :, 0:rows(j)]
                        dve.tensor_tensor(mixT[:, 4 * kk:4 * kk + 4, tile_tokens(j)], src,
                                          gout[:, 4 * kk:4 * kk + 4].unsqueeze(2).to_broadcast([P, 4, rows(j)]),
                                          ALU.mult).then_inc(f_taken, 1)

        def phase_f1_pe(pe):
            for i in range(NTILE):
                r = rows(i)
                pe.wait_ge(f_scaled, i + 1)
                if i >= 2:
                    pe.wait_ge(f_taken, 2 * (i - 1))
                for k in range(KD) if i < NCH else range(4, KD):
                    t = pe.transpose(PS[:, 2 * (i % 2) + k // 4, (k % 4) * P:(k % 4) * P + r],
                                     mix[0:r, i, k * P:(k + 1) * P], ident[0:r, 0:r])
                    if k % 4 == 3:
                        t.then_inc(f_psum, 1)

        x1 = view(R_rec, 0, "", i=NTILE, n=D)
        wo = view(R_rec, 9216, "", k=KD, n=D)
        xs2 = [R_ring[:, n * D:(n + 1) * D] for n in range(2)]
        sqj2 = R_ring[:, 2048:3072]
        x2T = xnT
        x1_in, wo_in = sem("x1_in"), [sem(f"wo_in{n}") for n in range(2)]
        op_psum, x1_ready, ss2, ms2, rms2, xs2_ready, xs2_T, x2T_ready = (
            sem("op_psum"), sem("x1_ready"), sem("ss2"), sem("ms2"), sem("rms2"), sem("xs2_ready"), sem("xs2_T"),
            sem("x2T_ready"))

        def phase_f1_sync(sp):
            for n in range(2):
                sp.dma_start(wo[:, :, n * 512:(n + 1) * 512],
                             i_["w_out"][0].rearrange("(k p) n -> p k n", p=P)[:, :, n * 512:(n + 1) * 512]).then_inc(wo_in[n], 16)
            sp.dma_start(x1[:, 0:NCH, :], i_["x_prompt"][0].rearrange("(i p) d -> p i d", p=P)).then_inc(x1_in, 16)
            sp.dma_start(x1[0:NS, NCH, :], i_["x_sample"].rearrange("b t d -> (b t) d")).then_inc(x1_in, 16)

        def phase_f2_pe(pe):
            pe.wait_ge(wo_in[0], 16)
            pe.wait_ge(wo_in[1], 16)
            for i in range(NTILE + 2):
                if i < NTILE:
                    r = rows(i)
                    if i >= 2:
                        pe.wait_ge(x1_ready, 2 * (i - 1))
                    for n in range(2):
                        for k in range(KD):
                            mm = pe.matmul(PS[0:r, 4 + 2 * (i % 2) + n, :], mixT[:, k, tile_tokens(i)],
                                           wo[:, k, n * 512:(n + 1) * 512], start=(k == 0), stop=(k == KD - 1))
                        mm.then_inc(op_psum, 1)
                if i >= 2:
                    j = i - 2
                    r = rows(j)
                    pe.wait_ge(xs2_ready, j + 1)
                    if j >= 2:
                        pe.wait_ge(x2T_ready, 2 * (j - 1))
                    for k in range(KD):
                        t = pe.transpose(PS[:, 2 * (j % 2) + k // 4, (k % 4) * P:(k % 4) * P + r],
                                         xs2[j % 2][0:r, k * P:(k + 1) * P], ident[0:r, 0:r])
                        if k % 4 == 3:
                            t.then_inc(xs2_T, 1)

        def phase_f2_act(act):
            for i in range(NTILE):
                r = rows(i)
                act.wait_ge(x1_ready, 2 * i + 2)
                act.activation(sqj2[0:r, :], x1[0:r, i, :], ACT.Square, accum_out=stat[0:r, 0, i:i + 1]).then_inc(ss2, 1)
                act.wait_ge(ms2, i + 1)
                act.activation(stat[0:r, 2, i:i + 1], stat[0:r, 1, i:i + 1], ACT.Sqrt).then_inc(rms2, 1)

        def phase_f2_dve(dve):
            dve.wait_ge(x1_in, 32)
            for i in range(NTILE + 2):
                if i < NTILE:
                    r = rows(i)
                    for n in range(2):
                        dve.wait_ge(op_psum, 2 * i + n + 1)
                        part = x1[0:r, i, n * 512:(n + 1) * 512]
                        dve.tensor_tensor(part, part, PS[0:r, 4 + 2 * (i % 2) + n, :], ALU.add).then_inc(x1_ready, 1)
                    dve.wait_ge(ss2, i + 1)
                    dve.tensor_scalar(stat[0:r, 1, i:i + 1], stat[0:r, 0, i:i + 1], 1.0 / D, EPS,
                                      ALU.mult, ALU.add).then_inc(ms2, 1)
                    dve.wait_ge(rms2, i + 1)
                    link("dve", dve, dve.reciprocal(stat[0:r, 3, i:i + 1], stat[0:r, 2, i:i + 1]))
                    if i >= 2:
                        dve.wait_ge(xs2_T, 2 * (i - 1))
                    dve.tensor_scalar(xs2[i % 2][0:r, :], x1[0:r, i, :], stat[0:r, 3, i:i + 1], None,
                                      ALU.mult).then_inc(xs2_ready, 1)
                if i >= 2:
                    j = i - 2
                    for kk in range(2):
                        dve.wait_ge(xs2_T, 2 * j + kk + 1)
                        src = PS[:, 2 * (j % 2) + kk, :].rearrange("p (k t) -> p k t", t=P)[:, :, 0:rows(j)]
                        dve.tensor_tensor(x2T[:, 4 * kk:4 * kk + 4, tile_tokens(j)], src,
                                          gffn[:, 4 * kk:4 * kk + 4].unsqueeze(2).to_broadcast([P, 4, rows(j)]),
                                          ALU.mult).then_inc(x2T_ready, 1)

        uT = view(R_aqk, 0, "", f=8, t=NTOK)
        wslot = [R_rec[:, 9216 + n * 4096:9216 + (n + 1) * 4096] for n in range(3)] + [R_ring[:, 2048:6144]]
        grow = R_rec[:, 21504:21504 + D]
        sqj3 = R_rec[:, 22528:22528 + D]
        NQ = DFF // 1024
        W_UNITS = [(kind, q, n) for q in range(NQ) for kind in ("up", "down") for n in range(2)]
        w_ready = [sem(f"w_ready{n}") for n in range(4)]
        u_psum, u_relu, u_ready, d_psum, d_taken = sem("u_psum"), sem("u_relu"), sem("u_ready"), sem("d_psum"), sem("d_taken")
        g_row_in, ss3, ms3, rms3, y_ready, y_stored = (sem("g_row_in"), sem("ss3"), sem("ms3"), sem("rms3"), sem("y_ready"),
                                                       sem("y_stored"))

        def phase_g_sync(sp):
            sp.dma_start(grow, i_["g_final"].rearrange("(o d) -> o d", o=1).to_broadcast([P, D])).then_inc(g_row_in, 16)
            wup = i_["w_up"][0].rearrange("(k p) n -> p k n", p=P)
            wdn = i_["w_down"][0].rearrange("(q n f p) d -> q n p f d", n=2, f=4, p=P)
            for m, (kind, q, n) in enumerate(W_UNITS):
                if m >= 4:
                    if kind == "up":
                        sp.wait_ge(u_psum, 8 * (q - 1) + 4 * (n + 1))
                    else:
                        sp.wait_ge(d_psum, 2 * NTILE * q)
                if kind == "up":
                    c = q * 1024 + n * 512
                    sp.dma_start(wslot[m % 4].rearrange("p (k n) -> p k n", k=KD), wup[:, :, c:c + 512])\
                      .then_inc(w_ready[m % 4], 16)
                else:
                    sp.dma_start(wslot[m % 4].rearrange("p (f d) -> p f d", f=4), wdn[q, n]).then_inc(w_ready[m % 4], 16)
            for i in range(NTILE):
                sp.wait_ge(y_ready, i + 1)
                dst = o_["y_p"][0, i * P:(i + 1) * P, :] if i < NCH else o_["y_s"].rearrange("b t d -> (b t) d")
                sp.dma_start(dst, x1[0:rows(i), i, :]).then_inc(y_stored, 16)
            sp.wait_ge(y_stored, 16 * NTILE)

        def phase_g_pe(pe):
            for q in range(NQ):
                for n in range(2):
                    w = wslot[n].rearrange("p (k n) -> p k n", k=KD)
                    pe.wait_ge(w_ready[n], 16 * (q + 1))
                    for f in range(4):
                        tj = q * 8 + n * 4 + f
                        if tj >= 2:
                            pe.wait_ge(u_relu, tj - 1)
                        for g in range(3):
                            for k in range(KD):
                                mm = pe.matmul(PS[:, 3 * (tj % 2) + g, 0:TG], w[:, k, f * P:(f + 1) * P],
                                               x2T[:, k, g * TG:(g + 1) * TG], start=(k == 0), stop=(k == KD - 1))
                        mm.then_inc(u_psum, 1)
                pe.wait_ge(w_ready[2], 16 * (q + 1))
                pe.wait_ge(w_ready[3], 16 * (q + 1))
                pe.wait_ge(u_ready, 8 * (q + 1))
                for i in range(NTILE):
                    for n in range(2):
                        j = (q * NTILE + i) * 2 + n
                        if j >= 2:
                            pe.wait_ge(d_taken, j - 1)
                        for f in range(8):
                            w = wslot[2 + f // 4].rearrange("p (f d) -> p f d", f=4)
                            mm = pe.matmul(PS[0:rows(i), 6 + j % 2, :], uT[:, f, tile_tokens(i)],
                                           w[:, f % 4, n * 512:(n + 1) * 512], start=(f == 0), stop=(f == 7))
                        mm.then_inc(d_psum, 1)

        def phase_g_act(act):
            for q in range(NQ):
                for f in range(8):
                    act.wait_ge(u_relu, q * 8 + f + 1)
                    act.activation(uT[:, f, :], uT[:, f, :], ACT.Square).then_inc(u_ready, 1)
            for i in range(NTILE):
                r = rows(i)
                act.wait_ge(d_taken, ((NQ - 1) * NTILE + i) * 2 + 2)
                act.activation(sqj3[0:r, :], x1[0:r, i, :], ACT.Square, accum_out=stat[0:r, 0, i:i + 1]).then_inc(ss3, 1)
                act.wait_ge(ms3, i + 1)
                act.activation(stat[0:r, 2, i:i + 1], stat[0:r, 1, i:i + 1], ACT.Sqrt).then_inc(rms3, 1)

        def phase_g_dve(dve):
            def final(i):
                r = rows(i)
                dve.wait_ge(ss3, i + 1)
                dve.tensor_scalar(stat[0:r, 1, i:i + 1], stat[0:r, 0, i:i + 1], 1.0 / D, EPS,
                                  ALU.mult, ALU.add).then_inc(ms3, 1)
                dve.wait_ge(rms3, i + 1)
                link("dve", dve, dve.reciprocal(stat[0:r, 3, i:i + 1], stat[0:r, 2, i:i + 1]))
                dve.scalar_tensor_tensor(x1[0:r, i, :], x1[0:r, i, :], stat[0:r, 3, i:i + 1], grow[0:r, :],
                                         ALU.mult, ALU.mult).then_inc(y_ready, 1)

            dve.wait_ge(g_row_in, 16)
            for q in range(NQ):
                for f in range(8):
                    tj = q * 8 + f
                    dve.wait_ge(u_psum, tj + 1)
                    if q:
                        dve.wait_ge(d_psum, 2 * NTILE * q)
                    dve.tensor_scalar(three(uT[:, f, :]), PS[:, 3 * (tj % 2):3 * (tj % 2) + 3, 0:TG], 0.0, None,
                                      ALU.max).then_inc(u_relu, 1)
                for i in range(NTILE):
                    for n in range(2):
                        j = (q * NTILE + i) * 2 + n
                        dve.wait_ge(d_psum, j + 1)
                        part = x1[0:rows(i), i, n * 512:(n + 1) * 512]
                        dve.tensor_tensor(part, part, PS[0:rows(i), 6 + j % 2, :], ALU.add).then_inc(d_taken, 1)
                    if q == NQ - 1 and i >= 1:
                        final(i - 1)
            final(NTILE - 1)

        PH = {"sync": [phase_a_sync, phase_b_sync, phase_c_sync, phase_d1_sync, phase_d2_sync, phase_e_sync, phase_f1_sync, None,
                       phase_g_sync], "gps": [None, phase_b_gps, None, None, phase_d2_gps, None, None, None, None],
              "act": [phase_a_act, phase_b_act, phase_c_act, phase_d1_act, phase_d2_act, phase_e_act,
                      phase_f1_act, phase_f2_act, phase_g_act], "dve": [phase_a_dve, phase_b_dve, phase_c_dve, phase_d1_dve, phase_d2_dve, phase_e_dve,
                      phase_f1_dve, phase_f2_dve, phase_g_dve],
              "pe": [phase_a_pe, phase_b_pe, phase_c_pe, phase_d1_pe, phase_d2_pe, phase_e_pe,
                     phase_f1_pe, phase_f2_pe, phase_g_pe]}

        def run(eng, name):
            for f in PH[name][:upto]:
                if f is not None:
                    f(eng)
                barrier(eng, name)

        tap_sem = sem("tap_sem")

        locals_ = dict(xnT=xnT, aqk=aqk, mqk=mqk, hqk=hqk, hb=hb, va=va, vm=vm, mo=mo[:, 0:8, :], hi=hi, hg=hg, gcol=gcol[:, 0:8, :], glc=glc[:, :, :], bm=bm[:, :], mix=mix[:, 0:8, :], hstat=hstat[:, :, 0:8, :], ctail=ctail[:, :, :], gr=gr)

        @block.sync
        def _(sp):
            run(sp, "sync")
            if taps is not None:
                for n, (name, ap) in enumerate(taps(locals_).items()):
                    sp.dma_start(o_[name], ap).then_inc(tap_sem, 16)
                    sp.wait_ge(tap_sem, 16 * (n + 1))


        @block.gpsimd
        def _(pool):
            run(pool, "gps")

        @block.scalar
        def _(act):
            run(act, "act")

        @block.vector
        def _(dve):
            run(dve, "dve")

        @block.tensor
        def _(pe):
            run(pe, "pe")


OUTPUTS = {
    "y_p": (1, S, D), "y_s": (NB, NT, D), "p_k": (1, 1, S, H, E), "p_v": (1, 1, S, H, E), "p_conv": (1, 1, 3, 512),
    "p_C": (1, 1, HM, E, E), "p_n": (1, 1, HM, E), "p_m": (1, 1, HM), "p_S": (1, 1, HM, E, E),
    "s_k": (1, NB, NT, H, E), "s_v": (1, NB, NT, H, E), "s_conv": (1, NB, 3, 512), "s_C": (1, NB, HM, E, E),
    "s_n": (1, NB, HM, E), "s_m": (1, NB, HM), "s_S": (1, NB, HM, E, E),
}
INPUTS = ["x_prompt", "x_sample", "cache_attn_k", "cache_attn_v", "state_mlstm_conv", "state_mlstm_C", "state_mlstm_n",
          "state_mlstm_m", "state_hgrn_S", "rel_bias", "g_mix", "w_in", "mlstm_gate_b", "mlstm_conv_w", "mlstm_norm_g",
          "hgrn_lb_raw", "hgrn_norm_g", "w_out", "g_ffn", "w_up", "w_down", "g_final"]


def kernel(**inputs):
    import numpy as _np
    import concourse.bacc as _bacc
    from concourse import mybir as _mybir
    from concourse.bass_utils import run_bass_kernel_spmd as _run

    nc = _bacc.Bacc("TRN2", target_bir_lowering=False, num_devices=1)
    arrays = {f"in_{n}": _np.ascontiguousarray(inputs[n]) for n in INPUTS}
    arrays.update({f"in_{n}": a for n, a in constants().items()})
    i_ = {n[3:]: nc.dram_tensor(n, a.shape, _mybir.dt.from_np(a.dtype), kind="ExternalInput").ap()
          for n, a in arrays.items()}
    o_ = {n: nc.dram_tensor(f"out_{n}", shape, _mybir.dt.float32, kind="ExternalOutput").ap()
          for n, shape in OUTPUTS.items()}
    program(nc, i_, o_)
    r = _run(nc, [arrays], core_ids=[0])
    return tuple(r.results[0][f"out_{n}"] for n in OUTPUTS)
```

```python
from contextlib import ExitStack

import numpy as np
import concourse.bass as bass
from concourse import mybir

ALU = mybir.AluOpType
ACT = mybir.ActivationFunctionType
AX = mybir.AxisListType
F32 = mybir.dt.float32
F32R = mybir.dt.float32r

P = 128
D = 1024
KD = D // P
S = 1024
NB, NT = 8, 4
NS = NB * NT
NTOK = S + NS
TG = NTOK // 3
H, E = 8, 64
HM = 4
NCH = S // P
NTILE = NCH + 1
WB = 2048
FAR, NFAR = 1536, 96
DFF = 4096
EPS = 1e-6
NEG = -1e30
NLEV = 8
UW = 256
SLOTS = 3
TOE = S + P - 1
FOFF = P
NKEY = 4 * NFAR + 4 * P + NS
FW = 1152

AQ, AK, AV = 0, 512, 1024
MQ, MK, MV, MO, MI, MF = 1536, 1792, 2048, 2304, 2560, 2564
HQ, HF, HI, HG = 2568, 2824, 3080, 3336


def rows(i):
    return P if i < NCH else NS


def tile_tokens(i):
    return slice(i * P, i * P + rows(i))


def _bucket(dist):
    n = np.asarray(dist).astype(np.int32)
    scaled = np.log(np.maximum(n, 1) / 16) / np.log(2048 / 16)
    large = np.minimum(16 + (scaled * 16).astype(np.int32), 31)
    return np.where(n < 16, n, large).astype(np.int32)


def _bias_rows(dist):
    d = np.asarray(dist)
    out = np.zeros((33,) + d.shape, np.float32)
    b = _bucket(np.clip(d, 0, None))
    for n in range(32):
        out[n] = b == n
    c = np.zeros(d.shape, np.int32)
    for window, dil in ((128, 1), (512, 4), (2048, 16)):
        c += (d >= 0) & (d <= window) & (d % dil == 0)
    out[32] = np.where(c > 0, np.log(np.maximum(c, 1).astype(np.float64)), NEG)
    return out


def constants():
    c = {}
    c["c_ident"] = np.eye(P, dtype=np.float32)
    toe = np.full(FW, 1 << 20, np.int64)
    toe[:TOE] = S - 1 - np.arange(TOE)
    c["c_bias_toe"] = _bias_rows(toe)
    idx = np.concatenate([
        16 * (np.arange(4 * NFAR) // 4) + np.arange(4 * NFAR) % 4,
        np.concatenate([FAR + 4 * np.arange(P) + k for k in range(4)]),
    ])
    dist = np.zeros((NT, NKEY), np.int64)
    for t in range(NT):
        dist[t, :NKEY - NS] = WB + t - idx
        dist[t, NKEY - NS:] = t - np.arange(NS) % NT
    c["c_bias_keys"] = np.ascontiguousarray(_bias_rows(dist))
    other = np.zeros((P, 2, NS), np.float32)
    for p in range(P):
        for g in range(2):
            other[p, g] = np.where(np.arange(NS) // NT == 4 * g + p // 32, 0.0, NEG)
    c["c_other_batch"] = other
    s, t = np.arange(P)[:, None], np.arange(P)[None]
    lev = np.zeros((P, NLEV, P), np.float32)
    for l in range(NLEV - 1):
        m = 64 >> l
        lev[:, l] = (s // (2 * m) == t // (2 * m)) & (s % (2 * m) < m) & (t % (2 * m) >= m)
    lev[:, NLEV - 1] = s == t
    c["c_levels"] = lev
    cm = np.zeros((P, P + NS), np.float32)
    cm[:, :P] = np.where(s <= t, 0.0, NEG)
    s4, t4 = np.arange(NS)[:, None], np.arange(NS)[None]
    cm[:NS, P:] = np.where((s4 // NT == t4 // NT) & (s4 <= t4), 0.0, NEG)
    c["c_causal"] = cm
    seg = np.ones((1, NTOK), np.float32)
    seg[0, 0:S:P] = 0.0
    seg[0, S::NT] = 0.0
    c["c_seg"] = seg
    sel = np.zeros((HM, HM + 2, P), np.float32)
    for h in range(HM):
        sel[h, h] = 1.0
        sel[h, HM + h // 2, 64 * (h % 2):64 * (h % 2) + 64] = 1.0
    c["c_sel"] = sel
    c["c_batch"] = (np.arange(NS)[:, None] // NT == np.arange(NB)[None]).astype(np.float32)
    return c


def program(nc, i_, o_, taps=None, upto=99):
    ctx = ExitStack()
    with ctx:
        def sb(name, shape):
            return ctx.enter_context(nc.sbuf_tensor(name, shape, F32))

        def sem(name):
            return ctx.enter_context(nc.semaphore(name))

        PS = ctx.enter_context(nc.psum_tensor("PS", [P, 8, 512], F32))

        def place(name, at, n, dtype=F32):
            with nc.sbuf_tensor(name + "_before", [P, max(at, 8)], F32):
                if at:
                    with nc.sbuf_tensor(name, [P, n], dtype) as t:
                        return t[:, :]
            with nc.sbuf_tensor(name, [P, n], dtype) as t:
                return t[:, :]

        XNH, XNL = place("xn_high", 0, KD * NTOK, F32R), place("xn_low", 8448, KD * NTOK, F32R)
        R_mo = place("R_mo", 16896, 2304)
        R_hg = place("R_hg", 19200, 2304)
        R_a = place("R_a", 21504, 14656)
        R_mqk = place("R_mqk", 21504, 4224)
        R_hqk = place("R_hqk", 25728, 4224)
        R_hb = place("R_hb", 29952, 2112)
        R_vm = place("R_vm", 32064, 2340)
        R_hi = place("R_hi", 34404, 2304)
        R_gs = [place("R_gs0", 16896, 4 * NTOK), place("R_gs1", 32064, 4 * NTOK)]
        R_wa = place("R_wa", 36708, 4096, F32R)
        R_wb = place("R_wb", 40804, 4096, F32R)
        R_conv = place("R_conv", 40804, 4278)
        R_wstage = place("R_wstage", 45082, 3072)
        R_d = place("R_d", 36708, 8704)
        R_d2 = place("R_d2", 21504, 4224)
        R_aqk = place("R_aqk", 21504, 8448)
        R_va = place("R_va", 29952, 4680)
        R_wc = [place("R_wc0", 34632, 4096, F32R), place("R_wc1", 38728, 4096, F32R)]
        R_kstage = place("R_kstage", 42824, 1024)
        R_att = place("R_att", 0, 6144)
        R_mixa = place("R_mixa", 12800, 4096)
        R_cache = [place(f"R_cache{n}", at, 3584) for n, at in enumerate(
            (6144, 34632, 38728, 42824, 46920, 21504, 25600, 29952))]
        R_ptk = place("R_ptk", 10240, 1024)
        R_eout = place("R_eout", 11264, 1024)
        R_keyrows = place("R_keyrows", 29952, NT * NKEY)
        R_atts = place("R_atts", 12416, 128)
        seg = place("seg", 48300, NTOK)
        bm = place("bm", 49356, NTOK)[0:HM, :]
        R_gcol = place("R_gcol", 50412, NTILE * P)
        sel = place("sel", 51564, (HM + 2) * P)[0:HM, :]
        XH, XL = (place(n, at, 8448, F32R) for n, at in (("x_high", 21504), ("x_low", 29952)))
        R_x1 = place("R_x1", 38400, 9216)
        R_wo = place("R_wo", 0, 12288, F32R)
        R_wo2 = place("R_wo2", 47616, 4096, F32R)
        R_up = [place("R_up0", 12288, 4096, F32R), place("R_up1", 16384, 4096, F32R)]
        R_down = place("R_down", 0, 4096, F32R)
        R_stage = place("R_stage", 4096, 3072)
        R_upos = place("R_upos", 7168, 704)
        R_usq = place("R_usq", 7872, 704)
        R_u = place("R_u", 47616, 4224, F32R)
        R_first = place("R_first", 16384, 2048)
        R_xs2 = place("R_xs2", 18432, 2048)
        R_row = place("R_row", 20480, 1024)
        R_junk = place("R_junk", 12288, 1024)
        sb("arena", [P, 52336])

        def view(region, at, pattern, **dims):
            n = int(np.prod(list(dims.values())))
            names = " ".join(dims)
            part = dict(list(dims.items())[1:])
            return region[:, at:at + n].rearrange(f"p ({names}) -> p {names}", **part)

        XNH, XNL = (view(x, 0, "", k=KD, t=NTOK) for x in (XNH, XNL))
        mixa = view(R_mixa, 0, "", i=NCH, n=512)
        atts = view(R_atts, 0, "", a=4, s=NS)
        aqk = view(R_aqk, 0, "", k=8, t=NTOK)
        mqk = view(R_mqk, 0, "", k=4, t=NTOK)
        hqk = view(R_hqk, 0, "", k=4, t=NTOK)
        hb = view(R_hb, 0, "", k=2, t=NTOK)
        va = view(R_va, 0, "", i=NTILE, h=H, e=E + 1)
        vm = view(R_vm, 0, "", i=NTILE, h=HM, e=E + 1)
        mo = view(R_mo, 0, "", i=NTILE, n=256)
        hi = view(R_hi, 0, "", i=NTILE, n=256)
        hg = view(R_hg, 0, "", i=NTILE, n=256)

        ident = sb("ident", [P, P])
        gmix = sb("gmix", [P, KD])
        gffn = sb("gffn", [P, KD])
        gout = sb("gout", [P, KD])
        convw = sb("convw", [P, 4, 4])
        lb3 = sb("lb3", [P, 6, 2])
        gateb = sb("gateb", [P, 1])
        m0 = sb("m0", [HM, NB])
        selv = sel[:, :].rearrange("h (a p) -> h a p", p=P)
        stat = sb("stat", [P, 4, 12])
        cstate = sb("cstate", [P, 4, 24])
        ctail = sb("ctail", [P, 4, 27])
        egl = sb("egl", [HM, 16])
        gcol = view(R_gcol, 0, "", i=NTILE, n=P)
        glc = sb("glc", [P, 2, 16])
        small = sb("small", [P, 64])

        def const(name):
            return i_[name]

        fdr = nc.dram_tensor("bias_by_distance", [H, FW], F32, kind="Internal").ap()
        frep = nc.dram_tensor("bias_by_distance_copies", [H, P, FW], F32, kind="Internal").ap()

        phase_end = sem("phase_end")
        phase = {}

        def barrier(eng, name):
            phase[name] = phase.get(name, 0) + 1
            eng.drain().then_inc(phase_end, 1)
            eng.wait_ge(phase_end, 5 * phase[name])

        consts_in = sem("consts_in")
        x_in = [sem(f"x_in{n}") for n in range(3)]
        sumsq_ready, meansq_ready, rms_ready = sem("sumsq_ready"), sem("meansq_ready"), sem("rms_ready")
        xs_ready, xs_transposed = sem("xs_ready"), sem("xs_transposed")
        f_taken, f_high, f_split = sem("half_taken"), sem("half_high"), sem("half_split")
        chunk_high, chunk_split = sem("chunk_high"), sem("chunk_split")
        dve_order, act_order, pe_order = sem("dve_order"), sem("act_order"), sem("pe_order")
        order = {"dve": 0, "act": 0, "pe": 0}

        def link(name, eng, ins):
            s = {"dve": dve_order, "act": act_order, "pe": pe_order}[name]
            order[name] += 1
            ins.then_inc(s, 1)
            eng.wait_ge(s, order[name])

        bias_in, bias_ready, bias_copied, bias_stored = sem("bias_in"), sem("bias_ready"), sem("bias_copied"), sem("bias_stored")
        wgate_zero, wgate_in = sem("wgate_zero"), sem("wgate_in")
        w_in_ready = [sem(f"w_in_ready{n}") for n in range(SLOTS)]
        gate_psum, gate_taken = sem("gate_psum"), sem("gate_taken")
        gate_abs, gate_soft, gate_args, gate_rows = sem("gate_abs"), sem("gate_soft"), sem("gate_args"), sem("gate_rows")
        gate_last, gate_cols, gcol_ready, glc_psum = sem("gate_last"), sem("gate_cols"), sem("gcol_ready"), sem("glc_psum")
        cstate_psum = sem("cstate_psum")
        t_psum, t_taken = sem("t_psum"), sem("t_taken")
        sig_ready, conv_in, conv_done, h_done = sem("sig_ready"), sem("conv_in"), sem("conv_done"), sem("h_done")
        lnf_ready, f_ready = sem("lnf_ready"), sem("f_ready")
        n_psum, n_taken = sem("n_psum"), sem("n_taken")
        tail_psum, tail_copied = sem("tail_psum"), sem("tail_copied")
        def half(j, kk):
            return slice(4 * kk, 4 * kk + 4), tile_tokens(j)

        def last_tokens(i):
            return slice(i * P, (i + 1) * P) if i < NCH else slice(NTOK - P, NTOK)

        def product(pe, out, lhs, rhs, n):
            for k in range(n):
                (lh, ll), (rh, rl_) = lhs(k), rhs(k)
                pe.matmul(out, ll, rh, start=(k == 0), stop=False)
                pe.matmul(out, lh, rl_, start=False, stop=False)
                mm = pe.matmul(out, lh, rh, start=False, stop=(k == n - 1))
            return mm

        block = ctx.enter_context(nc.Block())

        xt = [R_a[:, 10560 + n * D:10560 + (n + 1) * D] for n in range(3)]
        sqj = R_a[:, 13632:13632 + D]
        tmpx = [view(R_conv, n * 512, "", k=4, t=P) for n in range(2)]
        cst_nat = R_a[0:24, 0:512]
        toe_in = R_a[0:33, 512:512 + FW]
        raug = R_a[0:33, 1700:1708]
        F_sb = R_a[0:8, 1800:1800 + FW]

        def phase_a_sync(sp):
            for n, (dst, src) in enumerate([
                (ident[:, :], const("c_ident")),
                (seg[:, :], const("c_seg").to_broadcast([P, NTOK])),
                (gmix[:, :], i_["g_mix"][0].rearrange("(k p) -> p k", p=P)),
                (gffn[:, :], i_["g_ffn"][0].rearrange("(k p) -> p k", p=P)),
                (gout[:, 4:6], i_["mlstm_norm_g"][0].rearrange("(k p) -> p k", p=P)),
                (gout[:, 6:8], i_["hgrn_norm_g"][0].rearrange("(k p) -> p k", p=P)),
                (lb3[:, 0, :], i_["hgrn_lb_raw"][0].rearrange("(k p) -> p k", p=P)),
                (gateb[0:4, :], i_["mlstm_gate_b"][0, 0:1, :].rearrange("o h -> h o")),
                (gateb[32:36, :], i_["mlstm_gate_b"][0, 1:2, :].rearrange("o h -> h o")),
                (m0[:, :], i_["state_mlstm_m"][0].rearrange("b h -> h b")),
                (selv, const("c_sel")),
                (cst_nat, i_["state_mlstm_conv"][0].rearrange("b j n -> (b j) n")),
            ] + [(convw[:, k, :], i_["mlstm_conv_w"][0, :, k * P:(k + 1) * P].rearrange("j p -> p j"))
                 for k in range(4)]):
                sp.dma_start(dst, src, allow_slow_non_contiguous=True).then_inc(consts_in, 16)
            sp.dma_start(toe_in, const("c_bias_toe")).then_inc(bias_in, 16)
            sp.dma_start(raug[0:32, :], i_["rel_bias"]).then_inc(bias_in, 16)
            for i in range(NTILE):
                if i >= 3:
                    sp.wait_ge(xs_transposed, 2 * (i - 2))
                src = i_["x_prompt"][0, i * P:(i + 1) * P, :] if i < NCH else i_["x_sample"].rearrange("b t d -> (b t) d")
                sp.dma_start(xt[i % 3][0:rows(i), :], src).then_inc(x_in[i % 3], 16)
            sp.wait_ge(bias_copied, 1)
            sp.dma_start(fdr, F_sb).then_inc(bias_stored, 16)
            sp.wait_ge(bias_stored, 16)
        NCONST = 16 * 16

        def phase_a_act(act):
            def high_part(j):
                for kk in range(2):
                    act.wait_ge(f_taken, 2 * j + kk + 1)
                    ks, ts = half(j, kk)
                    act.activation(XNH[:, ks, ts], tmpx[kk][:, :, 0:rows(j)], ACT.Copy).then_inc(f_high, 1)

            for i in range(NTILE):
                r = rows(i)
                act.wait_ge(x_in[i % 3], 16 * (i // 3 + 1))
                act.activation(sqj[0:r, :], xt[i % 3][0:r, :], ACT.Square,
                               accum_out=stat[0:r, 0, i:i + 1]).then_inc(sumsq_ready, 1)
                act.wait_ge(meansq_ready, i + 1)
                act.activation(stat[0:r, 2, i:i + 1], stat[0:r, 1, i:i + 1], ACT.Sqrt).then_inc(rms_ready, 1)
                if i >= 1:
                    high_part(i - 1)
            high_part(NTILE - 1)
            act.wait_ge(lb_shifted, 1)
            act.activation(lb3[:, 2, :], lb3[:, 1, :], ACT.Exp).then_inc(lb_exp, 1)

        def phase_a_gps(pool):
            for j in range(NTILE):
                for kk in range(2):
                    pool.wait_ge(f_high, 2 * j + kk + 1)
                    ks, ts = half(j, kk)
                    pool.tensor_tensor(XNL[:, ks, ts], tmpx[kk][:, :, 0:rows(j)], XNH.bitcast(F32)[:, ks, ts],
                                       ALU.subtract).then_inc(f_split, 1)

        def phase_a_dve(dve):
            dve.wait_ge(bias_in, 32)
            dve.memset(raug[32:33, :], 1.0).then_inc(bias_ready, 1)
            dve.wait_ge(consts_in, NCONST)
            for i in range(NTILE + 1):
                if i < NTILE:
                    r = rows(i)
                    dve.wait_ge(sumsq_ready, i + 1)
                    dve.tensor_scalar(stat[0:r, 1, i:i + 1], stat[0:r, 0, i:i + 1], 1.0 / D, EPS,
                                      ALU.mult, ALU.add).then_inc(meansq_ready, 1)
                    dve.wait_ge(rms_ready, i + 1)
                    link("dve", dve, dve.reciprocal(stat[0:r, 3, i:i + 1], stat[0:r, 2, i:i + 1]))
                    dve.tensor_scalar(xt[i % 3][0:r, :], xt[i % 3][0:r, :], stat[0:r, 3, i:i + 1], None,
                                      ALU.mult).then_inc(xs_ready, 1)
                if i >= 1:
                    j = i - 1
                    for kk in range(2):
                        dve.wait_ge(xs_transposed, 2 * j + kk + 1)
                        src = PS[:, 2 * (j % 2) + kk, :].rearrange("p (k t) -> p k t", t=P)[:, :, 0:rows(j)]
                        if j:
                            dve.wait_ge(f_split, 2 * j - 1 + kk)
                        dve.tensor_tensor(tmpx[kk][:, :, 0:rows(j)], src,
                                          gmix[:, 4 * kk:4 * kk + 4].unsqueeze(2).to_broadcast([P, 4, rows(j)]),
                                          ALU.mult).then_inc(f_taken, 1)
            dve.tensor_tensor(lb3[:, 1, :], lb3[:, 0, :], lb3[:, 0, :], ALU.subtract).then_inc(lb_shifted, 1)
            dve.wait_ge(lb_exp, 1)
            link("dve", dve, dve.reciprocal(lb3[:, 3, :], lb3[:, 2, :]))
            link("dve", dve, dve.tensor_tensor(lb3[:, 3, :], lb3[:, 2, :], lb3[:, 3, :], ALU.mult))
            link("dve", dve, dve.tensor_tensor(lb3[:, 4, :], lb3[:, 3, :], lb3[:, 3, :], ALU.subtract))
            link("dve", dve, dve.tensor_scalar(lb3[:, 5, :], lb3[:, 4, :], -1.0, 1.0, ALU.mult, ALU.add))
            for kk in range(4):
                dve.wait_ge(cstate_psum, 4)
                last = dve.tensor_copy(cstate[:, kk, :], PS[:, 7, kk * 32:kk * 32 + 24])
            link("dve", dve, last)
            dve.wait_ge(bias_psum, 3)
            dve.tensor_copy(F_sb.rearrange("h (a n) -> h a n", a=3), PS[0:8, 4:7, 0:384]).then_inc(bias_copied, 1)

        bias_copies = sem("bias_copies")
        lb_exp, lb_shifted, bias_psum, silu_done = sem("lb_exp"), sem("lb_shifted"), sem("bias_psum"), sem("silu_done")

        def phase_a_pe(pe):
            pe.wait_ge(consts_in, NCONST)
            pe.wait_ge(bias_in, 32)
            pe.wait_ge(bias_ready, 1)
            for a in range(3):
                pe.matmul(PS[0:8, 4 + a, 0:384], raug, toe_in[:, a * 384:(a + 1) * 384],
                          start=True, stop=True).then_inc(bias_psum, 1)
            for kk in range(4):
                pe.transpose(PS[:, 7, kk * 32:kk * 32 + 24], cst_nat[:, kk * P:(kk + 1) * P],
                             ident[0:24, 0:24]).then_inc(cstate_psum, 1)
            for i in range(NTILE):
                r = rows(i)
                pe.wait_ge(xs_ready, i + 1)
                if i >= 2:
                    pe.wait_ge(f_taken, 2 * (i - 1))
                for k in range(KD):
                    t = pe.transpose(PS[:, 2 * (i % 2) + k // 4, (k % 4) * P:(k % 4) * P + r],
                                     xt[i % 3][0:r, k * P:(k + 1) * P], ident[0:r, 0:r])
                    if k % 4 == 3:
                        t.then_inc(xs_transposed, 1)

        W_CHUNKS = ([("g", None)] + [("t", c + n * P) for c in (HQ, HF, MQ, MK) for n in range(2)] +
                    [("n", c + n * P) for c in (MV, MO, HI, HG) for n in range(2)] +
                    [("t", c + n * P) for c in (AQ, AK) for n in range(4)] +
                    [("n", c + n * P) for c in (AV, AV + UW) for n in range(2)])
        NW1 = 17
        TB2, NB2 = 8, 4
        w_in = i_["w_in"][0].rearrange("(k p) n -> p k n", p=P)
        wst = [view(R_wstage, n * 1024, "", k=KD, n=P) for n in range(3)]

        def parts_at(m):
            if m < 9:
                r, half_ = R_wa, m % 2
            elif m < NW1:
                r, half_ = (R_wa, R_wb)[(m - 9) // 2 % 2], (m - 9) % 2
            else:
                r, half_ = R_wc[(m - NW1) // 2 % 2], (m - NW1) % 2
            return [r[:, 2048 * z + 1024 * half_:2048 * z + 1024 * half_ + 1024].rearrange("p (k n) -> p k n", k=KD)
                    for z in range(2)]

        def unit_parts(m):
            r = (R_wa, R_wb)[(m - 9) // 2 % 2] if m < NW1 else R_wc[(m - NW1) // 2 % 2]
            return [r[:, 2048 * z:2048 * (z + 1)].rearrange("p (c k n) -> p k c n", c=2, k=KD) for z in range(2)]

        def chunk_place_free(eng, m):
            if m == 2:
                eng.wait_ge(gate_psum, 1)
            elif 3 <= m < 9:
                eng.wait_ge(t_psum, m - 2)
            elif m < 11 and m >= 9:
                eng.wait_ge(t_psum, TB2)
            elif m in (11, 12):
                eng.wait_ge(silu_done, 4)
            elif m in (13, 14, 15, 16):
                eng.wait_ge(n_psum, NTILE * ((m - 11) // 2))
            elif 21 <= m:
                eng.wait_ge(t_psum, TB2 + (m - 20 if m < 25 else 6 if m < 27 else 8))

        def w_high_part(act, m):
            if m:
                act.wait_ge(w_in_ready[m % 3], 16 * ((m + 2) // 3))
            else:
                act.wait_ge(wgate_in, 32)
            chunk_place_free(act, m)
            act.activation(parts_at(m)[0], wst[m % 3], ACT.Copy).then_inc(chunk_high, 1)

        def w_low_parts(pool, first, last):
            for m in range(first, last):
                pool.wait_ge(chunk_high, m + 1)
                pool.tensor_tensor(parts_at(m)[1], wst[m % 3], parts_at(m)[0].bitcast(F32), ALU.subtract)\
                    .then_inc(chunk_split, 1)

        def load_w(sp, first, last):
            for m in range(first, last):
                if m >= 3:
                    sp.wait_ge(chunk_split, m - 2)
                kind, col = W_CHUNKS[m]
                sp.dma_start(wst[m % 3], w_in[:, :, col:col + P]).then_inc(w_in_ready[m % 3], 16)

        CW = 3 + S + 7 * NB
        cst = [R_conv[:, n * 1083:n * 1083 + CW] for n in range(2)]
        scr = [R_conv[:, 2166 + n * NTOK:2166 + (n + 1) * NTOK] for n in range(2)]
        gs = [R_gs[n // 4][0:4, n % 4 * NTOK:(n % 4 + 1) * NTOK] for n in range(7)]
        gr = R_gs[1][:, 3 * NTOK:4 * NTOK]
        tailnat = R_hi[0:27, 0:512]

        def three(ap):
            return ap.rearrange("p (a t) -> p a t", a=3)

        def prompt(ap):
            return ap[:, 0:S].rearrange("p (c t) -> p c t", t=P)

        def sample(ap):
            return ap[:, S:NTOK].rearrange("p (b t) -> p b t", t=NT)

        def phase_b1_sync(sp):
            sp.wait_ge(wgate_zero, 1)
            for col, at in ((MI, 0), (MF, 32)):
                sp.dma_start(wst[0][:, :, at:at + 4], w_in[:, :, col:col + 4],
                             allow_slow_non_contiguous=True).then_inc(wgate_in, 16)
            load_w(sp, 1, 9)
            sp.wait_ge(gate_args, 1)
            sp.dma_start(o_["p_m"][0].rearrange("b h -> h b"), gs[6][:, S - 1:S],
                         allow_slow_non_contiguous=True).then_inc(gate_stored, 16)
            sp.dma_start(o_["s_m"][0].rearrange("b h -> h b"), gs[6][:, S + 3::NT],
                         allow_slow_non_contiguous=True).then_inc(gate_stored, 16)
            load_w(sp, 9, 13)
            sp.wait_ge(tail_copied, 1)
            sp.dma_start(o_["p_conv"][0, 0], tailnat[0:3, :]).then_inc(gate_stored, 16)
            sp.dma_start(o_["s_conv"][0].rearrange("b j n -> (b j) n"), tailnat[3:27, :]).then_inc(gate_stored, 16)
            load_w(sp, 13, NW1)
            sp.wait_ge(gate_stored, 64)

        def phase_b2_sync(sp):
            load_w(sp, NW1, len(W_CHUNKS))
            for i in range(NTILE):
                sp.wait_ge(k_taken, i + 1)
                sp.dma_start(by_token("k", i), kstage[i % 2][0:rows(i), :].rearrange("p (h e) -> p h e", e=E))\
                  .then_inc(k_stored[i % 2], 16)
            sp.wait_ge(k_stored[0], 16 * 5)
            sp.wait_ge(k_stored[1], 16 * 4)

        gate_stored = sem("gate_stored")
        k_psum, k_taken, k_stored = sem("k_psum"), sem("k_taken"), [sem(f"k_stored{n}") for n in range(2)]
        kstage = [R_kstage[:, n * 512:(n + 1) * 512] for n in range(2)]

        def by_token(what, i):
            if i < NCH:
                return o_["p_" + what][0, 0, i * P:(i + 1) * P]
            return o_["s_" + what][0].rearrange("b t h e -> (b t) h e")

        def phase_b1_gps(pool):
            pool.memset(wst[0], 0.0).then_inc(wgate_zero, 1)
            pool.dma_start(frep, fdr.unsqueeze(1).to_broadcast([H, P, FW])).then_inc(bias_copies, 16)
            w_low_parts(pool, 0, NW1)

        def phase_b2_gps(pool):
            w_low_parts(pool, NW1, len(W_CHUNKS))

        def tile_taken(eng, tj):
            if tj < 2:
                eng.wait_ge(h_done, tj + 1)
            elif tj < 4:
                eng.wait_ge(sig_ready, tj + 1)
            else:
                eng.wait_ge(t_taken, tj - 3)

        def tile_banks(tj):
            return 3 * ((tj + 1) % 2)

        def column_tile(pe, m, bank):
            pe.wait_ge(chunk_split, m + 1)
            wh, wl = parts_at(m)
            for g in range(3):
                ts = slice(g * TG, (g + 1) * TG)
                mm = product(pe, PS[:, bank + g, 0:TG], lambda k: (wh[:, k, :], wl[:, k, :]),
                             lambda k: (XNH[:, k, ts], XNL[:, k, ts]), KD)
            return mm

        def natural_tile(pe, m, i, q):
            if q >= 2:
                pe.wait_ge(n_taken, q - 1)
            wh, wl = unit_parts(m)
            ts = last_tokens(i)
            product(pe, PS[:, 6 + q % 2, 0:UW].rearrange("p (c n) -> p c n", c=2),
                    lambda k: (XNH[:, k, ts], XNL[:, k, ts]), lambda k: (wh[:, k], wl[:, k]), KD).then_inc(n_psum, 1)

        def phase_b1_pe(pe):
            column_tile(pe, 0, 0).then_inc(gate_psum, 1)
            for tj in range(TB2):
                if tj == 1:
                    pe.wait_ge(gate_taken, 1)
                if tj >= 2:
                    tile_taken(pe, tj - 2)
                column_tile(pe, 1 + tj, tile_banks(tj)).then_inc(t_psum, 1)
                if tj == 3:
                    pe.wait_ge(gate_rows, 4)
                    for c in range(NTILE):
                        r = rows(c)
                        pe.transpose(PS[0:r, 6, (c % 4) * P:(c % 4 + 1) * P], gr[:, tile_tokens(c)], ident[:, :])\
                            .then_inc(gate_cols, 1)
                        if c % 4 == 3 or c == NTILE - 1:
                            pe.wait_ge(gcol_ready, c // 4 + 1)
                    pe.wait_ge(gate_last, 1)
                    for pr in range(2):
                        mm = pe.matmul(PS[:, 7, pr * 16:(pr + 1) * 16], selv[:, HM + pr, :], egl[:, :],
                                       start=True, stop=True)
                    mm.then_inc(glc_psum, 1)
            for nu in range(NB2):
                m = 9 + 2 * nu
                if nu == 1:
                    pe.wait_ge(conv_done, 4)
                    for kk in range(4):
                        t = pe.transpose(PS[0:27, 0, kk * P:(kk + 1) * P], ctail[:, kk, :], ident[:, :])
                    t.then_inc(tail_psum, 1)
                pe.wait_ge(chunk_split, m + 2)
                for i in range(NTILE):
                    natural_tile(pe, m, i, nu * NTILE + i)

        def phase_b2_pe(pe):
            for tj in range(TB2, 2 * TB2):
                if tj >= TB2 + 2:
                    tile_taken(pe, tj - 2)
                column_tile(pe, NW1 + tj - TB2, tile_banks(tj)).then_inc(t_psum, 1)
            pe.wait_ge(t_taken, 12)
            for nu in range(NB2, NB2 + 2):
                m = NW1 + TB2 + 2 * (nu - NB2)
                pe.wait_ge(chunk_split, m + 2)
                for i in range(NTILE):
                    natural_tile(pe, m, i, nu * NTILE + i)
                    if nu == NB2:
                        if i >= 2:
                            pe.wait_ge(k_taken, i - 1)
                        for k in range(4):
                            t = pe.transpose(PS[0:rows(i), i % 2, k * P:(k + 1) * P], aqk[:, 4 + k, tile_tokens(i)],
                                             ident[:, :])
                        t.then_inc(k_psum, 1)

        def natural_out(act, q):
            act.wait_ge(n_psum, q + 1)
            return PS[0:P, 6 + q % 2, 0:UW] if q % NTILE < NCH else PS[P - NS:P, 6 + q % 2, 0:UW]

        def phase_b1_act(act):
            w_high_part(act, 0)
            w_high_part(act, 1)
            act.wait_ge(gate_abs, 1)
            link("act", act, act.activation(gs[2], gs[2], ACT.Exp, scale=-1.0))
            act.activation(gs[2], gs[2], ACT.Ln, bias=1.0).then_inc(gate_soft, 1)
            w_high_part(act, 2)
            for tj in range(TB2):
                bank = tile_banks(tj)
                src = PS[:, bank:bank + 3, 0:TG]
                act.wait_ge(t_psum, tj + 1)
                if tj < 4:
                    if tj >= 2:
                        act.wait_ge(h_done, tj - 1)
                    act.activation(three(scr[tj % 2]), src, ACT.Sigmoid).then_inc(sig_ready, 1)
                else:
                    n = tj - 4
                    c = cst[n % 2]
                    if n >= 2:
                        act.wait_ge(conv_done, n - 1)
                    c2 = c[:, 3 + S:].rearrange("p (b j) -> p b j", j=7)
                    act.activation(c[:, 3:3 + 2 * TG].rearrange("p (a t) -> p a t", a=2),
                                   PS[:, bank:bank + 2, 0:TG], ACT.Copy).then_inc(conv_in, 1)
                    act.activation(c[:, 3 + 2 * TG:3 + S], PS[:, bank + 2, 0:S - 2 * TG], ACT.Copy).then_inc(conv_in, 1)
                    act.activation(c2[:, :, 0:3], cstate[:, n, :].rearrange("p (b j) -> p b j", j=3), ACT.Copy)\
                        .then_inc(conv_in, 1)
                    act.activation(c2[:, :, 3:7], PS[:, bank + 2, S - 2 * TG:TG].rearrange("p (b j) -> p b j", j=4),
                                   ACT.Copy).then_inc(t_taken, 1)
                if tj + 3 < 9:
                    w_high_part(act, tj + 3)
                if tj == 7:
                    w_high_part(act, 9)
                    w_high_part(act, 10)
                if tj == 0:
                    act.wait_ge(gate_args, 1)
                    act.activation(gr[0:4, :], gs[3], ACT.Exp).then_inc(gate_rows, 1)
                    act.activation(gr[32:36, :], gs[6], ACT.Exp, scale=-1.0).then_inc(gate_rows, 1)
                    act.activation(gr[64:68, :], gs[4], ACT.Exp).then_inc(gate_rows, 1)
                    act.activation(gr[96:100, :], gs[1], ACT.Copy).then_inc(gate_rows, 1)
                if tj >= 5:
                    conv_sigmoid(act, tj - 5)
            conv_sigmoid(act, 3)
            act.wait_ge(gate_stored, 32)
            act.wait_ge(gcol_ready, 3)
            for nu in range(NB2):
                for i in range(NTILE):
                    q = nu * NTILE + i
                    r = rows(i)
                    src = natural_out(act, q)
                    if nu == 0:
                        act.activation(vm[0:r, i, :, 0:E], src.rearrange("p (h e) -> p h e", e=E), ACT.Copy)\
                            .then_inc(n_taken, 1)
                    elif nu in (1, 3):
                        act.activation((mo if nu == 1 else hg)[0:r, i, :], src, ACT.Sigmoid).then_inc(n_taken, 1)
                    else:
                        if i == 0:
                            act.wait_ge(gate_stored, 64)
                        act.activation(hi[0:r, i, :], src, ACT.Copy).then_inc(n_taken, 1)
                    if i == 1 and nu + 1 < NB2:
                        w_high_part(act, 11 + 2 * nu)
                        w_high_part(act, 12 + 2 * nu)
                if nu == 0:
                    act.wait_ge(f_ready, 2)
                    for p in range(2):
                        act.activation(hb[:, p, :], hb[:, p, :], ACT.Ln).then_inc(lnf_ready, 1)

        def phase_b2_act(act):
            for m in range(NW1, NW1 + 4):
                w_high_part(act, m)
            for k in range(8):
                bank = tile_banks(TB2 + k)
                act.wait_ge(t_psum, TB2 + k + 1)
                act.activation(three(aqk[:, k, :]), PS[:, bank:bank + 3, 0:TG], ACT.Copy, scale=0.125 if k < 4 else 1.0)\
                    .then_inc(t_taken, 1)
                if k < 4:
                    w_high_part(act, NW1 + 4 + k)
                elif k in (5, 7):
                    w_high_part(act, NW1 + 3 + k)
                    w_high_part(act, NW1 + 4 + k)
            for nu in range(2):
                for i in range(NTILE):
                    q = (NB2 + nu) * NTILE + i
                    r = rows(i)
                    act.activation(va[0:r, i, 4 * nu:4 * nu + 4, 0:E],
                                   natural_out(act, q).rearrange("p (h e) -> p h e", e=E), ACT.Copy).then_inc(n_taken, 1)
                    if nu == 0:
                        act.wait_ge(k_psum, i + 1)
                        if i >= 2:
                            act.wait_ge(k_stored[i % 2], 16 * (i // 2))
                        act.activation(kstage[i % 2][0:r, :], PS[0:r, i % 2, :], ACT.Copy).then_inc(k_taken, 1)

        def conv_sigmoid(act, n):
            act.wait_ge(conv_done, n + 1)
            if n >= 2:
                act.wait_ge(silu_done, n - 1)
            else:
                act.wait_ge(h_done, 4)
            act.activation(scr[n % 2], mqk[:, n, :], ACT.Sigmoid).then_inc(sig_ready, 1)

        def phase_b1_dve(dve):
            dve.wait_ge(gate_psum, 1)
            link("dve", dve, dve.tensor_scalar(three(gs[0]), PS[0:4, 0:3, 0:TG], gateb[0:4, :], None, ALU.add))
            link("dve", dve, dve.tensor_scalar(three(gs[1]), PS[32:36, 0:3, 0:TG], gateb[32:36, :], None, ALU.add))
            dve.nop().then_inc(gate_taken, 1)
            dve.scalar_tensor_tensor(gs[2], gs[1], -1.0, gs[1], ALU.mult, ALU.max).then_inc(gate_abs, 1)
            link("dve", dve, dve.tensor_scalar(gs[1], gs[1], 0.0, None, ALU.min))
            link("dve", dve, dve.memset(gr[:, :], 0.0))
            dve.wait_ge(gate_soft, 1)
            link("dve", dve, dve.tensor_tensor(gs[3], gs[1], gs[2], ALU.subtract))
            link("dve", dve, dve.tensor_tensor_scan(gs[4], seg[0:4, :], gs[3], 0.0, ALU.mult, ALU.add))
            link("dve", dve, dve.tensor_tensor(small[0:4, 0:NB], gs[3][:, S::NT], m0[:, :], ALU.add))
            link("dve", dve, dve.tensor_copy(gs[5], gs[0]))
            link("dve", dve, dve.tensor_tensor(gs[5][:, S::NT], small[0:4, 0:NB], gs[0][:, S::NT], ALU.max))
            link("dve", dve, dve.memset(gs[3][:, S::NT], NEG))
            link("dve", dve, dve.tensor_tensor_scan(gs[6], gs[3], gs[5], 0.0, ALU.add, ALU.max))
            link("dve", dve, dve.tensor_tensor(bm[:, :], gs[4], gs[6], ALU.subtract))
            link("dve", dve, dve.tensor_tensor(gs[1], gs[0], gs[4], ALU.subtract))
            dve.tensor_copy(gs[3][:, 0:P], bm[:, 0:P])
            prev = gs[6][:, P - 1:S - 1:P].unsqueeze(2).to_broadcast([HM, NCH - 1, P])
            dve.tensor_tensor(prompt(gs[3])[:, 1:], prompt(bm[:, :])[:, 1:], prev, ALU.add)
            dve.tensor_tensor(sample(gs[3]), sample(bm[:, :]), m0[:, :].unsqueeze(2).to_broadcast([HM, NB, NT]), ALU.add)
            dve.tensor_tensor(prompt(gs[4]), prompt(gs[1]),
                              bm[:, P - 1:S:P].unsqueeze(2).to_broadcast([HM, NCH, P]), ALU.add)
            dve.tensor_tensor(sample(gs[4]), sample(gs[1]),
                              bm[:, S + NT - 1::NT].unsqueeze(2).to_broadcast([HM, NB, NT]), ALU.add).then_inc(gate_args, 1)
            dve.wait_ge(gate_rows, 4)
            link("dve", dve, dve.tensor_copy(egl[:, 0:8], gr[0:4, P - 1:S:P]))
            link("dve", dve, dve.tensor_copy(egl[:, 8:16], gr[0:4, S + NT - 1::NT]))
            dve.nop().then_inc(gate_last, 1)
            for tj in range(8):
                if tj == 4:
                    for c4 in range(3):
                        n = 4 if c4 < 2 else 1
                        r = rows(4 * c4)
                        dve.wait_ge(gate_cols, 4 * c4 + n)
                        dve.tensor_copy(gcol[0:r, 4 * c4:4 * c4 + n, :],
                                        PS[0:r, 6, 0:n * P].rearrange("p (c t) -> p c t", t=P)).then_inc(gcol_ready, 1)
                    dve.wait_ge(glc_psum, 1)
                    link("dve", dve, dve.tensor_copy(glc[:, :, :], PS[:, 7, 0:32].rearrange("p (a n) -> p a n", a=2)))
                kind, p = tj // 2, tj % 2
                bank = tile_banks(tj)
                src = PS[:, bank:bank + 3, 0:TG]
                if kind == 0:
                    dve.wait_ge(sig_ready, tj + 1)
                    dve.tensor_tensor(three(hqk[:, p, :]), src, three(scr[tj % 2]), ALU.mult).then_inc(h_done, 1)
                elif kind == 1:
                    dve.wait_ge(sig_ready, tj + 1)
                    dve.tensor_scalar(hb[:, p, :], scr[tj % 2], lb3[:, 5, p:p + 1], lb3[:, 4, p:p + 1],
                                      ALU.mult, ALU.add).then_inc(f_ready, 1)
                    dve.wait_ge(f_ready, p + 1)
                    dve.tensor_scalar(hqk[:, 2 + p, :], hb[:, p, :], -1.0, 1.0, ALU.mult, ALU.add).then_inc(h_done, 1)
                else:
                    n = tj - 4
                    c = cst[n % 2]
                    if n < 2:
                        link("dve", dve, dve.memset(c[:, 0:3], 0.0))
                    dve.wait_ge(conv_in, 3 * n + 3)
                    dve.wait_ge(t_taken, n + 1)
                    dst = mqk[:, n, :]
                    c2 = c[:, 3 + S:].rearrange("p (b j) -> p b j", j=7)
                    for j in range(4):
                        w = convw[:, n, j:j + 1]
                        for out, src in ((dst[:, 0:S], c[:, j:j + S]), (sample(dst), c2[:, :, j:j + NT])):
                            if j == 0:
                                ins = dve.tensor_scalar(out, src, w, None, ALU.mult)
                            else:
                                ins = dve.scalar_tensor_tensor(out, src, w, out, ALU.mult, ALU.add)
                        link("dve", dve, ins)
                    dve.tensor_copy(ctail[:, n, 0:3], c[:, S:S + 3])
                    dve.tensor_copy(ctail[:, n, 3:27].rearrange("p (b j) -> p b j", j=3), c2[:, :, 4:7])\
                        .then_inc(conv_done, 1)
                    if n >= 1:
                        conv_silu(dve, n - 1)
                    if n == 3:
                        conv_silu(dve, 3)
            dve.wait_ge(tail_psum, 1)
            dve.tensor_copy(tailnat[:, :], PS[0:27, 0, :]).then_inc(tail_copied, 1)
            dve.memset(vm[:, :, :, E:E + 1], 1.0)
            for p in range(2):
                dve.wait_ge(lnf_ready, p + 1)
                link("dve", dve, dve.tensor_tensor_scan(hb[:, p, :], seg[:, :], hb[:, p, :], 0.0, ALU.mult, ALU.add))

        def phase_b2_dve(dve):
            dve.memset(va[:, :, :, E:E + 1], 1.0)

        def conv_silu(dve, n):
            dve.wait_ge(sig_ready, 4 + n + 1)
            dve.scalar_tensor_tensor(mqk[:, n, :], mqk[:, n, :], 1.0 if n < 2 else 0.125, scr[n % 2],
                                     ALU.mult, ALU.mult).then_inc(silu_done, 1)

        G = [R_att[:, n * S:(n + 1) * S] for n in range(2)]
        PB = [R_att[:, (2 + n) * S:(3 + n) * S] for n in range(2)]
        PT = [view(R_att, (4 + n) * S, "", k=NCH, q=P) for n in range(2)]
        g_in = [sem(f"g_in{n}") for n in range(2)]
        s_psum, biased, exped = sem("s_psum"), sem("biased"), sem("exped")
        pT_psum = sem("pT_psum")
        pT_taken = [sem("pT_taken_act"), sem("pT_taken_dve")]
        o_psum, o_taken, v_stored = sem("o_psum"), sem("o_taken"), sem("v_stored")
        negm = sb("negm", [P, 2])
        rl = sb("rl", [P, 1])
        STEPS = [(h, i) for h in range(H) for i in range(NCH)]
        groups, gsum = [], [0]
        for n_, (h_, i_n) in enumerate(STEPS):
            groups.append([(k0, min(i_n + 1, k0 + 4)) for k0 in range(0, i_n + 1, 4)])
            gsum.append(gsum[-1] + len(groups[-1]))

        def taken_through(eng, gid):
            if (gid + 1) // 2:
                eng.wait_ge(pT_taken[0], (gid + 1) // 2)
            if gid // 2:
                eng.wait_ge(pT_taken[1], gid // 2)

        def phase_c_sync(sp):
            sp.wait_ge(bias_copies, 16)
            for h in range(H):
                if h >= 2:
                    sp.wait_ge(biased, NCH * (h - 1))
                src = bass.AP(frep.tensor, h * P * FW + P - 1, [[FW - 1, P], [1, S]])
                sp.dma_start(G[h % 2], src).then_inc(g_in[h % 2], 16)
                if h == 1:
                    load_caches(sp, 0, NAHEAD)
                    for i in range(NTILE):
                        sp.dma_start(by_token("v", i), va[0:rows(i), i, :, 0:E]).then_inc(v_stored, 16)
            sp.wait_ge(v_stored, 16 * NTILE)

        def phase_c_pe(pe):
            for n in range(len(STEPS) + 2):
                if n < len(STEPS):
                    h, i = STEPS[n]
                    if n >= 2:
                        pe.wait_ge(biased, n - 1)
                    part = slice(64 * (h % 2), 64 * (h % 2) + 64)
                    nk = (i + 1) * P
                    for c in range(0, nk, 512):
                        mm = pe.matmul(PS[:, 2 * (n % 2) + c // 512, 0:min(512, nk - c)],
                                       aqk[part, h // 2, i * P:(i + 1) * P], aqk[part, 4 + h // 2, c:min(c + 512, nk)],
                                       start=True, stop=True)
                    mm.then_inc(s_psum, 1)
                if 1 <= n <= len(STEPS):
                    m = n - 1
                    pe.wait_ge(exped, m + 1)
                    for j, (k0, k1) in enumerate(groups[m]):
                        gid = gsum[m] + j
                        if gid >= 2:
                            taken_through(pe, gid - 1)
                        for k in range(k0, k1):
                            t = pe.transpose(PS[:, 4 + gid % 2, (k - k0) * P:(k - k0 + 1) * P],
                                             PB[m % 2][:, k * P:(k + 1) * P], ident[:, :])
                        t.then_inc(pT_psum, 1)
                if n >= 2:
                    m = n - 2
                    h, i = STEPS[m]
                    taken_through(pe, gsum[m + 1])
                    if m >= 2:
                        pe.wait_ge(o_taken, m - 1)
                    for k in range(i + 1):
                        mm = pe.matmul(PS[:, 6 + m % 2, 0:E + 1], PT[m % 2][:, k, :], va[:, k, h, :],
                                       start=(k == 0), stop=(k == i))
                    mm.then_inc(o_psum, 1)

        def copy_groups(eng, copy, m, parity):
            for j, (k0, k1) in enumerate(groups[m]):
                gid = gsum[m] + j
                if gid % 2 == parity:
                    eng.wait_ge(pT_psum, gid + 1)
                    if m >= 2:
                        eng.wait_ge(o_psum, m - 1)
                    copy(PT[m % 2][:, k0:k1, :],
                         PS[:, 4 + gid % 2, 0:(k1 - k0) * P].rearrange("p (k q) -> p k q", q=P))\
                        .then_inc(pT_taken[parity], 1)

        def phase_c_act(act):
            for n in range(len(STEPS) + 1):
                if n < len(STEPS):
                    h, i = STEPS[n]
                    nk = (i + 1) * P
                    act.wait_ge(biased, n + 1)
                    act.activation(PB[n % 2][:, 0:nk], PB[n % 2][:, 0:nk], ACT.Exp, bias=negm[:, n % 2:n % 2 + 1],
                                   scale=-1.0).then_inc(exped, 1)
                if n >= 1:
                    copy_groups(act, lambda o, s: act.activation(o, s, ACT.Copy), n - 1, 0)

        def phase_c_dve(dve):
            for n in range(len(STEPS) + 2):
                if n < len(STEPS):
                    h, i = STEPS[n]
                    nk = (i + 1) * P
                    if i == 0:
                        dve.wait_ge(g_in[h % 2], 16 * (h // 2 + 1))
                    if n >= 2:
                        dve.wait_ge(pT_psum, gsum[n - 1])
                    dve.wait_ge(s_psum, n + 1)
                    scores = PS[:, 2 * (n % 2):2 * (n % 2) + 2, :].rearrange("p a n -> p (a n)")[:, 0:nk]
                    dve.tensor_tensor_reduce(PB[n % 2][:, 0:nk], scores, G[h % 2][:, S - nk:S], -1.0, 3e38,
                                             ALU.add, ALU.min, negm[:, n % 2:n % 2 + 1]).then_inc(biased, 1)
                if 1 <= n <= len(STEPS):
                    copy_groups(dve, dve.tensor_copy, n - 1, 1)
                if n >= 2:
                    m = n - 2
                    h, i = STEPS[m]
                    dve.wait_ge(o_psum, m + 1)
                    if m >= 1:
                        dve.wait_ge(o_taken, m)
                    link("dve", dve, dve.reciprocal(rl[:, :], PS[:, 6 + m % 2, E:E + 1]))
                    dve.tensor_scalar(mixa[:, i, h * E:(h + 1) * E], PS[:, 6 + m % 2, 0:E], rl[:, :], None,
                                      ALU.mult).then_inc(o_taken, 1)
            link("dve", dve, dve.memset(qblk[:, :, :, :, :], 0.0))
            for hp in range(4):
                for h2 in range(2):
                    pt = slice(64 * h2, 64 * h2 + 64)
                    ins = dve.tensor_copy(qblk[pt, hp, :, 2 * hp + h2, :], sample(aqk[pt, hp, :]))
            link("dve", dve, ins)
            link("dve", dve, dve.tensor_copy(knew[:, :, :], aqk[:, 4:8, S:NTOK]))
            link("dve", dve, dve.tensor_copy(vnew[0:NS, :].rearrange("p (h e) -> p h e", e=E), va[0:NS, 8, :, 0:E]))

        qblk = R_att[:, 0:1024].rearrange("p (hp b h t) -> p hp b h t", hp=4, b=NB, h=H)
        knew = R_att[:, 1024:1152].rearrange("p (k t) -> p k t", k=4)
        vnew = R_att[:, 1152:1664]

        A_ = R_d
        Dm = [view(A_, n * 512, "", h=HM, t=P) for n in range(2)]
        Wm = [view(A_, 1024 + n * 512, "", h=HM, t=P) for n in range(2)]
        kd = [view(A_, 2048 + n * 256, "", h=HM, e=E) for n in range(2)]
        tmpN = view(A_, 2560, "", h=HM, e=E + 1)
        nd = view(A_, 2820, "", h=HM, e=E + 1)
        hh = view(A_, 3080, "", h=HM, e=E)
        sq = view(A_, 3336, "", h=HM, e=E)
        Cst = view(A_, 3592, "", a=2, e=E + 1)
        Css = view(A_, 3722, "", b=NB, a=2, e=E + 1)
        qm_flat = [A_[:, 4762 + n * 288:4762 + (n + 1) * 288] for n in range(2)]
        kdm = view(A_, 5338, "", b=NB, h=HM, e=E)
        cmask = A_[:, 7386:7386 + P + NS]
        bmask = A_[0:NS, 7546:7554]
        tmpC = view(A_, 7554, "", b=NB, e=E + 1)
        hstat = sb("hstat", [P, 2, NTILE, HM])
        hrstd = sb("hrstd", [P, 2, NTILE, HM])
        adn = sb("adn", [P, HM])
        d_in, d_zero = sem("d_in"), sem("d_zero")
        g1, g2 = sem("mlstm_scores"), sem("mlstm_sums")
        m_biased, m_exp, m_w, m_kd = sem("m_biased"), sem("m_exp"), sem("m_w"), sem("m_kd")
        m_state, m_taken, m_masked, m_upd, m_updt = (sem("m_state"), sem("m_taken"), sem("m_masked"), sem("m_upd"),
                                                     sem("m_updt"))
        st_out = sem("state_stored")

        def masked_q(flat):
            return (flat[:, 0:256].rearrange("p (b t) -> p b t", b=NB),
                    flat.rearrange("p (b s) -> p b s", s=36)[:, :, 0:NT])

        def halves():
            return [(a, h2, slice(64 * h2, 64 * h2 + 64)) for a in range(2) for h2 in range(2)]

        def phase_d1_sync(sp):
            sp.dma_start(cmask, const("c_causal")).then_inc(d_in, 16)
            sp.dma_start(bmask, const("c_batch")).then_inc(d_in, 16)
            for a, h2, pt in halves():
                sp.dma_start(Css[pt, :, a, 0:E], i_["state_mlstm_C"][0, :, 2 * a + h2].rearrange("b k v -> k b v"))\
                  .then_inc(d_in, 16)
                sp.dma_start(Css[pt, :, a, E:E + 1], i_["state_mlstm_n"][0, :, 2 * a + h2:2 * a + h2 + 1].rearrange(
                    "b o k -> k b o"), allow_slow_non_contiguous=True).then_inc(d_in, 16)
            sp.wait_ge(m_state, NCH)
            for a, h2, pt in halves():
                h = 2 * a + h2
                sp.dma_start(o_["p_C"][0, 0, h], Cst[pt, a, 0:E]).then_inc(st_out, 16)
                sp.dma_start(o_["p_n"][0, 0, h:h + 1].rearrange("o k -> k o"), Cst[pt, a, E:E + 1],
                             allow_slow_non_contiguous=True).then_inc(st_out, 16)
            sp.wait_ge(m_upd, 4)
            for a, h2, pt in halves():
                h = 2 * a + h2
                sp.dma_start(o_["s_C"][0, :, h].rearrange("b k v -> k b v"), Css[pt, :, a, 0:E]).then_inc(st_out, 16)
                sp.dma_start(o_["s_n"][0, :, h:h + 1].rearrange("b o k -> k b o"), Css[pt, :, a, E:E + 1],
                             allow_slow_non_contiguous=True).then_inc(st_out, 16)
            sp.wait_ge(st_out, 16 * 16)

        def phase_d1_pe(pe):
            def scores(c):
                r, tt = rows(c), tile_tokens(c)
                if c >= 2:
                    pe.wait_ge(m_w, c - 1)
                    pe.wait_ge(m_kd, c - 1)
                for h in (0, 2, 1, 3):
                    pt = slice(64 * (h % 2), 64 * (h % 2) + 64)
                    mm = pe.matmul(PS[0:r, c % 2, h * P:h * P + r], mqk[pt, 2 + h // 2, tt], mqk[pt, h // 2, tt],
                                   start=True, stop=True)
                    if h == 2:
                        link("pe", pe, mm)
                if c:
                    pe.wait_ge(m_biased, c)
                for h in range(HM):
                    pe.matmul(PS[0:r, 2, h * P:h * P + r], selv[:, h, 0:r], bm[:, tt], start=True, stop=True)
                for a in range(2):
                    t = pe.transpose(PS[0:r, 3 + c % 2, a * P:(a + 1) * P], mqk[:, 2 + a, tt], ident[:, :])
                t.then_inc(g1, 1)

            def sums(c):
                r, tt = rows(c), tile_tokens(c)
                pe.wait_ge(m_kd, c + 1)
                pe.wait_ge(m_w, c + 1)
                pe.wait_ge(d_zero, 1)
                if c >= 1:
                    pe.wait_ge(m_state, c)
                    pe.wait_ge(m_taken, c)
                if c == NCH:
                    pe.wait_ge(m_masked, 1)
                for h in (0, 2, 1, 3):
                    pt = slice(64 * (h % 2), 64 * (h % 2) + 64)
                    o = PS[0:r, 5, h * (E + 1):(h + 1) * (E + 1)]
                    if c < NCH:
                        mm = pe.matmul(o, mqk[pt, h // 2, tt], Cst[pt, h // 2, :], start=True, stop=True)
                    else:
                        for b in range(NB):
                            mm = pe.matmul(o, masked_q(qm_flat[h // 2])[0][pt, b, :], Css[pt, b, h // 2, :],
                                           start=(b == 0), stop=(b == NB - 1))
                    if h == 2:
                        link("pe", pe, mm)
                for h in range(HM):
                    mm = pe.matmul(PS[0:r, 6, h * (E + 1):(h + 1) * (E + 1)], Wm[c % 2][0:r, h, 0:r], vm[0:r, c, h, :],
                                   start=True, stop=True)
                if c < NCH:
                    for a in range(2):
                        mm = pe.matmul(PS[:, 7, a * 130:(a + 1) * 130],
                                       kd[c % 2][0:r, 2 * a:2 * a + 2, :].rearrange("p h e -> p (h e)"),
                                       vm[0:r, c, 2 * a:2 * a + 2, :].rearrange("p h e -> p (h e)"), start=True, stop=True)
                mm.then_inc(g2, 1)

            pe.wait_ge(d_in, 160)
            scores(0)
            scores(1)
            for c in range(NTILE):
                sums(c)
                if c + 2 < NTILE:
                    scores(c + 2)
            for a in range(2):
                if a:
                    pe.wait_ge(m_upd, 2)
                for b in range(NB):
                    mm = pe.matmul(PS[:, b // 2, (b % 2) * 130:(b % 2 + 1) * 130],
                                   kdm[0:NS, b, 2 * a:2 * a + 2, :].rearrange("p h e -> p (h e)"),
                                   vm[0:NS, NCH, 2 * a:2 * a + 2, :].rearrange("p h e -> p (h e)"), start=True, stop=True)
                mm.then_inc(m_updt, 1)

        def phase_d1_act(act):
            for c in range(NTILE):
                r = rows(c)
                act.wait_ge(m_biased, c + 1)
                for h in range(HM):
                    e = act.activation(Dm[c % 2][0:r, h, 0:r], Dm[c % 2][0:r, h, 0:r], ACT.Exp,
                                       bias=gcol[0:r, c, 96 + h:97 + h])
                e.then_inc(m_exp, 1)

        def phase_d1_dve(dve):
            def biased_(c):
                r = rows(c)
                dve.wait_ge(g1, c + 1)
                m = cmask[0:r, 0:P] if c < NCH else cmask[0:r, P:P + NS]
                dve.tensor_tensor(Dm[c % 2][0:r, :, 0:r],
                                  PS[0:r, 2, :].rearrange("p (h t) -> p h t", t=P)[:, :, 0:r],
                                  m.unsqueeze(1).to_broadcast([r, HM, r]), ALU.add).then_inc(m_biased, 1)

            def col(c, at, n):
                return gcol[0:rows(c), c, at:at + HM].unsqueeze(2).to_broadcast([rows(c), HM, n])

            dve.wait_ge(d_in, 160)
            dve.memset(Cst[:, :, :], 0.0).then_inc(d_zero, 1)
            for a in range(2):
                link("dve", dve, dve.memset(qm_flat[a], 0.0))
                dve.tensor_copy(masked_q(qm_flat[a])[1], sample(mqk[:, a, :]))

            def weighted(c):
                r = rows(c)
                dve.wait_ge(m_exp, c + 1)
                dve.tensor_tensor(Wm[c % 2][0:r, :, 0:r], Dm[c % 2][0:r, :, 0:r],
                                  PS[0:r, c % 2, :].rearrange("p (h t) -> p h t", t=P)[:, :, 0:r], ALU.mult)\
                   .then_inc(m_w, 1)
                if c == NCH:
                    dve.wait_ge(m_kd, c + 1)
                    for h in range(HM):
                        ins = dve.tensor_tensor(kdm[0:NS, :, h, :], kd[c % 2][0:NS, h, :].unsqueeze(1).to_broadcast([NS, NB, E]),
                                                bmask.unsqueeze(2).to_broadcast([NS, NB, E]), ALU.mult)
                    ins.then_inc(m_masked, 1)

            def keys_and_bias(c):
                r = rows(c)
                dve.wait_ge(g1, c + 1)
                if c >= 2:
                    dve.wait_ge(g2, c - 1)
                dve.tensor_tensor(kd[c % 2][0:r], PS[0:r, 3 + c % 2, 0:256].rearrange("p (h e) -> p h e", e=E),
                                  col(c, 64, E), ALU.mult).then_inc(m_kd, 1)
                biased_(c)

            keys_and_bias(0)
            weighted(0)
            for c in range(NTILE):
                r = rows(c)
                if c + 1 < NTILE:
                    keys_and_bias(c + 1)
                dve.wait_ge(g2, c + 1)
                if c < NCH:
                    for a, h2, pt in halves():
                        ins = dve.scalar_tensor_tensor(Cst[pt, a, :], Cst[pt, a, :], glc[pt, a, c:c + 1],
                                                       PS[pt, 7, a * 130 + h2 * 65:a * 130 + h2 * 65 + 65],
                                                       ALU.mult, ALU.add)
                    ins.then_inc(m_state, 1)
                heads4 = lambda bank: PS[0:r, bank, 0:4 * (E + 1)].rearrange("p (h e) -> p h e", e=E + 1)
                link("dve", dve, dve.tensor_tensor(tmpN[0:r], heads4(5), col(c, 0, E + 1), ALU.mult))
                dve.tensor_tensor(nd[0:r], heads4(6), tmpN[0:r], ALU.add).then_inc(m_taken, 1)
                dve.wait_ge(m_taken, c + 1)
                if c + 1 < NTILE:
                    weighted(c + 1)
                den = nd[0:r, :, E]
                link("dve", dve, dve.scalar_tensor_tensor(adn[0:r, :], den, -1.0, den, ALU.mult, ALU.max))
                link("dve", dve, dve.tensor_tensor(adn[0:r, :], adn[0:r, :], gcol[0:r, c, 32:36], ALU.max))
                link("dve", dve, dve.reciprocal(adn[0:r, :], adn[0:r, :]))
                link("dve", dve, dve.tensor_tensor(hh[0:r], nd[0:r, :, 0:E],
                                                   adn[0:r, :].unsqueeze(2).to_broadcast([r, HM, E]), ALU.mult))
                gated_head(dve, c, hh[0:r], mo)
                link("dve", dve, dve.tensor_tensor(sq[0:r], hh[0:r], hh[0:r], ALU.mult))
                link("dve", dve, dve.tensor_reduce(hstat[0:r, 0, c, :], sq[0:r], AX.X, ALU.add))
            for a in range(2):
                dve.wait_ge(m_updt, a + 1)
                for h2 in range(2):
                    pt = slice(64 * h2, 64 * h2 + 64)
                    link("dve", dve, dve.tensor_tensor(tmpC[pt], Css[pt, :, a, :],
                                                       glc[pt, a, 8:16].unsqueeze(2).to_broadcast([64, NB, E + 1]), ALU.mult))
                    upd = PS[pt, 0:4, 0:260].rearrange("p a (b e) -> p a b e", b=2)[:, :, :, h2 * 65:h2 * 65 + 65]
                    dve.tensor_tensor(Css[pt, :, a, :].rearrange("p (x y) e -> p x y e", y=2),
                                      tmpC[pt].rearrange("p (x y) e -> p x y e", y=2), upd, ALU.add).then_inc(m_upd, 1)

        def gated_head(eng, c, h, gate):
            r = rows(c)
            g = gate[0:r, c, :].rearrange("p (h e) -> p h e", e=E)
            eng.tensor_tensor(g, h, g, ALU.mult)

        NX = NLEV + 1
        X = [view(R_d, n * 2304, "", l=NX, a=2, t=P) for n in range(2)]
        AM = [view(R_d, 4608 + n * 1024, "", l=NLEV, t=P) for n in range(2)]
        AS = [R_d[:, 8448 + n * P:8448 + (n + 1) * P] for n in range(2)]
        Sst = view(R_d, 6656, "", a=2, e=E)
        Sss = view(R_d, 6784, "", b=NB, a=2, e=E)
        kl = [R_d[:, 7808 + n * 256:8064 + n * 256] for n in range(2)]
        lev = view(R_d2, 0, "", l=NLEV, t=P)
        hqm_flat = [R_d2[:, 1024 + n * 288:1024 + (n + 1) * 288] for n in range(2)]
        klm = view(R_d2, 1600, "", b=NB, n=256)
        osb = view(R_d2, 3648, "", h=HM, e=E)
        osq = view(R_d2, 3904, "", h=HM, e=E)
        tmpS = view(R_d, 0, "", b=NB, e=E)
        bmask2 = R_d2[0:NS, 4160:4168]
        eb = sb("eb", [P, 2, 2])
        ebs = sb("ebs", [P, 2, NB])
        h_in, h_zero, h_arg, h_exp, h_prod = sem("h_in"), sem("h_zero"), sem("h_arg"), sem("h_exp"), sem("h_prod")
        a_psum, a_masked, kl_psum, kl_taken = sem("a_psum"), sem("a_masked"), sem("kl_psum"), sem("kl_taken")
        ho_psum, ho_copied, ho_taken, h_state = sem("ho_psum"), sem("ho_copied"), sem("ho_taken"), sem("h_state")
        h_masked, hu_psum, h_upd = sem("h_masked"), sem("hu_psum"), sem("h_upd")

        def split(ap, m):
            return ap.rearrange("p a (n z m) -> p a n z m", z=2, m=m)

        def levels_of(c):
            return range(NLEV - 1) if c < NCH else range(NLEV - 3, NLEV - 1)

        def phase_d2_sync(sp):
            sp.dma_start(lev, const("c_levels")).then_inc(h_in, 16)
            sp.dma_start(bmask2, const("c_batch")).then_inc(h_in, 16)
            for a, h2, pt in halves():
                sp.dma_start(Sss[pt, :, a, :], i_["state_hgrn_S"][0, :, 2 * a + h2].rearrange("b k v -> k b v"))\
                  .then_inc(h_in, 16)
            sp.wait_ge(h_state, NCH)
            for a, h2, pt in halves():
                sp.dma_start(o_["p_S"][0, 0, 2 * a + h2], Sst[pt, a, :]).then_inc(st_out, 16)
            sp.wait_ge(h_upd, 4)
            for a, h2, pt in halves():
                sp.dma_start(o_["s_S"][0, :, 2 * a + h2].rearrange("b k v -> k b v"), Sss[pt, :, a, :]).then_inc(st_out, 16)
            sp.wait_ge(st_out, 16 * 24)

        def phase_d2_gps(pool):
            for c in range(NTILE):
                r, tt = rows(c), tile_tokens(c)
                x = X[c % 2]
                if c >= 2:
                    pool.wait_ge(ho_psum, c - 1)
                    pool.wait_ge(kl_psum, c - 1)
                b = hb[:, :, tt]
                for l in levels_of(c):
                    m = 64 >> l
                    bb, xx = split(b, m), split(x[:, l, :, 0:r], m)
                    mid = bb[:, :, :, 0, m - 1:m].to_broadcast([P, 2, r // (2 * m), m])
                    pool.tensor_tensor(xx[:, :, :, 1, :], bb[:, :, :, 1, :], mid, ALU.subtract)
                    pool.tensor_tensor(xx[:, :, :, 0, :], mid, bb[:, :, :, 0, :], ALU.subtract)
                pool.tensor_copy(x[:, NLEV - 1, :, 0:r], b)
                seglen = P if c < NCH else NT
                bs = b.rearrange("p a (n s) -> p a n s", s=seglen)
                last = bs[:, :, :, seglen - 1:seglen].to_broadcast([P, 2, r // seglen, seglen])
                pool.tensor_tensor(x[:, NLEV, :, 0:r].rearrange("p a (n s) -> p a n s", s=seglen), last, bs,
                                   ALU.subtract).then_inc(h_arg, 1)

        def phase_d2_act(act):
            for c in range(NTILE):
                r = rows(c)
                x = X[c % 2]
                act.wait_ge(h_arg, c + 1)
                l0 = 0 if c < NCH else NLEV - 3
                act.activation(x[:, l0:, :, 0:r], x[:, l0:, :, 0:r], ACT.Exp).then_inc(h_exp, 1)
                if c >= 1:
                    out_copy(act, c - 1)
            out_copy(act, NTILE - 1)

        def out_copy(act, c):
            r = rows(c)
            act.wait_ge(ho_psum, c + 1)
            if c >= 1:
                act.wait_ge(ho_taken, c)
            src = PS[0:r, 4 + c % 2, 0:256].rearrange("p (h e) -> p h e", e=E)
            act.activation(osq[0:r], src, ACT.Square).then_inc(ho_copied, 1)

        def phase_d2_dve(dve):
            dve.wait_ge(h_in, 96)
            for a in range(2):
                link("dve", dve, dve.memset(hqm_flat[a], 0.0))
            link("dve", dve, dve.memset(Sst[:, :, :], 0.0))
            dve.nop().then_inc(h_zero, 1)

            def products(c):
                r, tt = rows(c), tile_tokens(c)
                x = X[c % 2]
                dve.wait_ge(h_exp, c + 1)
                q, k = hqk[:, 0:2, tt], hqk[:, 2:4, tt]
                if c < NCH:
                    link("dve", dve, dve.tensor_copy(eb[:, :, c % 2:c % 2 + 1], x[:, NLEV - 1, :, P - 1:P]))
                else:
                    link("dve", dve, dve.tensor_copy(ebs[:, :, :], x[:, NLEV - 1, :, NT - 1:NS:NT]))
                for l in levels_of(c):
                    m = 64 >> l
                    xx = split(x[:, l, :, 0:r], m)
                    dve.tensor_tensor(xx[:, :, :, 1, :], xx[:, :, :, 1, :], split(q, m)[:, :, :, 1, :], ALU.mult)
                    dve.tensor_tensor(xx[:, :, :, 0, :], xx[:, :, :, 0, :], split(k, m)[:, :, :, 0, :], ALU.mult)
                link("dve", dve, dve.tensor_tensor(x[:, NLEV - 1, :, 0:r], x[:, NLEV - 1, :, 0:r], q, ALU.mult))
                if c == NCH:
                    for a in range(2):
                        link("dve", dve, dve.tensor_copy(masked_q(hqm_flat[a])[1],
                                                         x[:, NLEV - 1, a, 0:r].rearrange("p (b t) -> p b t", t=NT)))
                dve.tensor_tensor(x[:, NLEV, :, 0:r], x[:, NLEV, :, 0:r], k, ALU.mult).then_inc(h_prod, 1)

            products(0)
            for c in range(NTILE):
                r = rows(c)
                for h in range(HM):
                    j = c * HM + h
                    dve.wait_ge(a_psum, j + 1)
                    if j >= 2:
                        dve.wait_ge(am_used, j - 1)
                    l0 = 0 if c < NCH else NLEV - 3
                    src = PS[0:r, 2 * (j % 2):2 * (j % 2) + 2, :].rearrange("p b (l t) -> p (b l) t", t=P)
                    link("dve", dve, dve.tensor_tensor(AM[j % 2][0:r, l0:, 0:r], src[:, l0:, 0:r], lev[0:r, l0:, 0:r], ALU.mult))
                    dve.tensor_reduce(AS[j % 2][0:r, 0:r], AM[j % 2][0:r, l0:, 0:r].rearrange("p l t -> p t l"), AX.X, ALU.add)\
                       .then_inc(a_masked, 1)
                    if h == 0 and c + 1 < NTILE:
                        products(c + 1)
                    if h == 1:
                        dve.wait_ge(kl_psum, c + 1)
                        dve.tensor_copy(kl[c % 2][0:r, :], PS[0:r, 6, 0:256]).then_inc(kl_taken, 1)
                if c == NCH:
                    dve.wait_ge(kl_taken, c + 1)
                    link("dve", dve, dve.tensor_tensor(klm[0:NS], kl[c % 2][0:NS, :].unsqueeze(1).to_broadcast([NS, NB, 256]),
                                                       bmask2.unsqueeze(2).to_broadcast([NS, NB, 256]), ALU.mult))
                    dve.nop().then_inc(h_masked, 1)
                dve.wait_ge(ho_psum, c + 1)
                if c < NCH:
                    for a, h2, pt in halves():
                        ins = dve.scalar_tensor_tensor(Sst[pt, a, :], Sst[pt, a, :], eb[pt, a, c % 2:c % 2 + 1],
                                                       PS[pt, 7, a * P + h2 * 64:a * P + h2 * 64 + 64], ALU.mult, ALU.add)
                    ins.then_inc(h_state, 1)
                dve.wait_ge(ho_copied, c + 1)
                gated_head(dve, c, PS[0:r, 4 + c % 2, 0:256].rearrange("p (h e) -> p h e", e=E), hg)
                dve.tensor_reduce(hstat[0:r, 1, c, :], osq[0:r], AX.X, ALU.add).then_inc(ho_taken, 1)
            for a in range(2):
                if a:
                    dve.wait_ge(hu_psum, 1)
                for h2 in range(2):
                    pt = slice(64 * h2, 64 * h2 + 64)
                    link("dve", dve, dve.tensor_tensor(tmpS[pt], Sss[pt, :, a, :],
                                                       ebs[pt, a, :].unsqueeze(2).to_broadcast([64, NB, E]), ALU.mult))
                    upd = PS[pt, 0:2, :].rearrange("p x (b e) -> p x b e", b=4)[:, :, :, h2 * 64:h2 * 64 + 64]
                    dve.tensor_tensor(Sss[pt, :, a, :].rearrange("p (x y) e -> p x y e", y=4),
                                      tmpS[pt].rearrange("p (x y) e -> p x y e", y=4), upd, ALU.add).then_inc(h_upd, 1)

        am_used, inter_done = sem("am_used"), sem("inter_done")

        def phase_d2_pe(pe):
            def level_scores(c, h):
                r, tt = rows(c), tile_tokens(c)
                j = c * HM + h
                if h == 0:
                    pe.wait_ge(h_prod, c + 1)
                if j >= 2:
                    pe.wait_ge(a_masked, j - 1)
                pt, a = slice(64 * (h % 2), 64 * (h % 2) + 64), h // 2
                x = X[c % 2]
                for l in levels_of(c):
                    pe.matmul(PS[0:r, 2 * (j % 2) + l // 4, (l % 4) * P:(l % 4) * P + r], x[pt, l, a, 0:r], x[pt, l, a, 0:r],
                              start=True, stop=True)
                pe.matmul(PS[0:r, 2 * (j % 2) + 1, 3 * P:3 * P + r], hqk[pt, 2 + a, tt], hqk[pt, a, tt],
                          start=True, stop=True).then_inc(a_psum, 1)

            def apply(c, h):
                r = rows(c)
                j = c * HM + h
                pt, a = slice(64 * (h % 2), 64 * (h % 2) + 64), h // 2
                pe.wait_ge(a_masked, j + 1)
                if h == 0:
                    if c >= 2:
                        pe.wait_ge(ho_taken, c - 1)
                    pe.wait_ge(h_zero, 1)
                    if c >= 1:
                        pe.wait_ge(h_state, c)
                o = PS[0:r, 4 + c % 2, h * E:(h + 1) * E]
                pe.matmul(o, AS[j % 2][0:r, 0:r], hi[0:r, c, h * E:(h + 1) * E], start=True, stop=False).then_inc(am_used, 1)
                if j >= 1:
                    pe.wait_ge(inter_done, j)
                if c < NCH:
                    mm = pe.matmul(o, X[c % 2][pt, NLEV - 1, a, 0:r], Sst[pt, a, :], start=False, stop=True)
                else:
                    for b in range(NB):
                        mm = pe.matmul(o, masked_q(hqm_flat[a])[0][pt, b, :], Sss[pt, b, a, :], start=False, stop=(b == NB - 1))
                mm.then_inc(inter_done, 1)

            def keys(c):
                r = rows(c)
                if c >= 1:
                    pe.wait_ge(kl_taken, c)
                for a in range(2):
                    t = pe.transpose(PS[0:r, 6, a * P:(a + 1) * P], X[c % 2][:, NLEV, a, 0:r], ident[:, :])
                t.then_inc(kl_psum, 1)

            pe.wait_ge(h_in, 96)
            level_scores(0, 0)
            for c in range(NTILE):
                r = rows(c)
                level_scores(c, 1)
                keys(c)
                apply(c, 0)
                level_scores(c, 2)
                apply(c, 1)
                level_scores(c, 3)
                apply(c, 2)
                if c + 1 < NTILE:
                    level_scores(c + 1, 0)
                apply(c, 3)
                pe.wait_ge(kl_taken, c + 1)
                if c < NCH:
                    for a in range(2):
                        mm = pe.matmul(PS[:, 7, a * P:(a + 1) * P], kl[c % 2][:, a * P:(a + 1) * P],
                                       hi[:, c, a * P:(a + 1) * P], start=True, stop=True)
                    mm.then_inc(ho_psum, 1)
                else:
                    pe.wait_ge(h_masked, 1)
                    for a in range(2):
                        if a:
                            pe.wait_ge(h_upd, 2)
                        for b in range(NB):
                            mm = pe.matmul(PS[:, b // 4, (b % 4) * P:(b % 4 + 1) * P], klm[0:NS, b, a * P:(a + 1) * P],
                                           hi[0:NS, c, a * P:(a + 1) * P], start=True, stop=True)
                        mm.then_inc(hu_psum if a else ho_psum, 1)

        NFT = 4 * NFAR // P
        NKT = NFT + 4
        NSLOT = 8
        NAHEAD = 5
        cache = [view(r, 0, "", k=NKT, n=512) for r in R_cache]
        ktile = [view(R_att, 1664 + n * 512, "", a=4, s=P) for n in range(2)]
        pb = [R_att[:, at:at + NKEY] for at in (2688, 3712)]
        bkey = R_att[:, 4640:4640 + NKEY]
        bother = view(R_att, 5568, "", g=2, n=NS)
        rexp = R_att[0:33, 5632:6144].rearrange("p (t c) -> p t c", t=NT)
        ptk = view(R_ptk, 0, "", k=NKT + 1, q=P)
        eout = [R_eout[:, n * 512:(n + 1) * 512] for n in range(2)]
        keyrows = R_keyrows[0:33, :].rearrange("p (t n) -> p t n", t=NT)
        ra = small[0:33, 0:H]
        estat = sb("estat", [P, 2, 8])
        e_in, ra_ready, rexp_ready, bkey_psum, bkey_ready = (sem("e_in"), sem("ra_ready"), sem("rexp_ready"),
                                                             sem("bkey_psum"), sem("bkey_ready"))
        cache_in = [sem(f"cache_in{n}") for n in range(NSLOT)]
        kt_psum, st_psum, sb_psum = sem("kt_psum"), sem("st_psum"), sem("sb_psum")
        kt_taken = [sem("kt_taken_act"), sem("kt_taken_dve")]
        st_taken, e_min, e_exp, p_ready = sem("st_taken"), sem("e_min"), sem("e_exp"), sem("p_ready")
        pk_psum, ptk_ready, ov_psum, ov_taken = sem("pk_psum"), sem("ptk_ready"), sem("ov_psum"), sem("ov_taken")
        eo_psum = sem("eo_psum")
        ITEMS = [("cache_attn_" + kv, b) for kv in "kv" for b in range(NB)]
        NJ = NB * NKT

        def score_banks(B):
            return 2 + 2 * (B % 2)

        def key_bank(B, k):
            return (score_banks(B), k * P) if k < NFT else (score_banks(B) + 1, (k - NFT) * P)

        def item_in(eng, m):
            eng.wait_ge(cache_in[m % NSLOT], 64 * (m // NSLOT + 1))

        def phase_e_sync(sp):
            sp.dma_start(keyrows, const("c_bias_keys")).then_inc(e_in, 16)
            sp.dma_start(ra[0:32, :], i_["rel_bias"]).then_inc(e_in, 16)
            sp.dma_start(bother, const("c_other_batch")).then_inc(e_in, 16)
            load_caches(sp, NAHEAD, NSLOT - 1)
            sp.wait_ge(bkey_psum, 2)
            load_caches(sp, NSLOT - 1, len(ITEMS))

        def load_caches(sp, first, last):
            for m in range(first, last):
                name, b = ITEMS[m]
                if m >= NSLOT:
                    sp.wait_ge(kt_psum, NKT * (m - NSLOT + 1))
                rows_ = i_[name][0, b].rearrange("s h e -> s (h e)")
                far = rows_[0:FAR, :].rearrange("(c m s) n -> c m s n", s=16, m=P // 4)
                near = rows_[FAR:WB, :].rearrange("(p k) n -> p k n", k=4)
                for c in range(NFT):
                    sp.dma_start(cache[m % NSLOT][:, c, :], far[c, :, 0:4, :]).then_inc(cache_in[m % NSLOT], 16)
                sp.dma_start(cache[m % NSLOT][:, NFT:, :], near).then_inc(cache_in[m % NSLOT], 16)

        def phase_e_pe(pe):
            pe.wait_ge(e_in, 48)
            pe.wait_ge(rexp_ready, 1)
            for n in range(2):
                for t in range(NT):
                    mm = pe.matmul(PS[:, n, 0:NKEY // 2], rexp[:, t, :],
                                   keyrows[:, t, n * (NKEY // 2):(n + 1) * (NKEY // 2)],
                                   start=(t == 0), stop=(t == NT - 1))
                mm.then_inc(bkey_psum, 1)
            pe.wait_ge(bkey_ready, 1)
            for J in range(NJ + 1):
                if J < NJ:
                    B, k = J // NKT, J % NKT
                    if k == 0:
                        item_in(pe, B)
                    if J >= 2:
                        pe.wait_ge(kt_taken[J % 2], J // 2)
                    for a in range(4):
                        t = pe.transpose(PS[:, J % 2, a * P:(a + 1) * P], cache[B % NSLOT][:, k, a * P:(a + 1) * P],
                                         ident[:, :])
                    t.then_inc(kt_psum, 1)
                if J >= 1:
                    B, k = (J - 1) // NKT, (J - 1) % NKT
                    g = B // 4
                    pe.wait_ge(kt_taken[(J - 1) % 2], (J - 1) // 2 + 1)
                    if k == 0 and B >= 2:
                        pe.wait_ge(st_taken, B - 1)
                    bank, at_ = key_bank(B, k)
                    for a in range(4):
                        mm = pe.matmul(PS[:, bank, at_:at_ + P], qblk[:, a, 4 * g:4 * g + 4, :, :].rearrange("p b h t -> p (b h t)"),
                                       ktile[(J - 1) % 2][:, a, :], start=(a == 0), stop=(a == 3))
                    mm.then_inc(st_psum, 1)
                    if k == NKT - 1 and B % 4 == 3:
                        for a in range(4):
                            mm = pe.matmul(PS[:, 6, g * NS:(g + 1) * NS],
                                           qblk[:, a, 4 * g:4 * g + 4, :, :].rearrange("p b h t -> p (b h t)"),
                                           knew[:, a, :], start=(a == 0), stop=(a == 3))
                        mm.then_inc(sb_psum, 1)
            for g in range(2):
                pe.wait_ge(p_ready, g + 1)
                pe.wait_ge(st_taken, NB)
                if g:
                    pe.wait_ge(ptk_ready, g)
                for k in range(NKT + 1):
                    if k < NKT:
                        t = pe.transpose(PS[:, 2 + k // 4, (k % 4) * P:(k % 4 + 1) * P], pb[g][:, k * P:(k + 1) * P], ident[:, :])
                    else:
                        t = pe.transpose(PS[0:NS, 7, 0:P], pb[g][:, k * P:NKEY], ident[:, :])
                t.then_inc(pk_psum, 1)
                pe.wait_ge(ptk_ready, g + 1)
                for b in range(4):
                    item_in(pe, NB + 4 * g + b)
                    v = cache[(NB + 4 * g + b) % NSLOT]
                    if g:
                        pe.wait_ge(ov_taken, b + 1)
                    o = PS[:, OV_BANK[b], :]
                    for k in range(NKT):
                        pe.matmul(o, ptk[:, k, :], v[:, k, :], start=(k == 0), stop=False)
                    pe.matmul(o, ptk[0:NS, NKT, :], vnew[0:NS, :], start=False, stop=True).then_inc(ov_psum, 1)
            for g in range(2):
                pe.wait_ge(ov_taken, 4 * (g + 1))
                for a in range(4):
                    t = pe.transpose(PS[:, 2 + g, a * P:(a + 1) * P], eout[g][:, a * P:(a + 1) * P], ident[:, :])
                t.then_inc(eo_psum, 1)

        OV_BANK = (0, 1, 4, 5)

        def take_kt(eng, copy, J):
            eng.wait_ge(kt_psum, J + 1)
            if J >= 2:
                eng.wait_ge(st_psum, J - 1)
            copy(ktile[J % 2], PS[:, J % 2, :].rearrange("p (a t) -> p a t", t=P)).then_inc(kt_taken[J % 2], 1)

        def phase_e_act(act):
            def exponent(g):
                act.wait_ge(e_min, g + 1)
                act.activation(pb[g], pb[g], ACT.Exp, bias=estat[:, g, 3:4], scale=-1.0,
                               accum_out=estat[:, g, 4:5]).then_inc(e_exp, 1)

            for J in range(0, NJ, 2):
                take_kt(act, lambda o, s: act.activation(o, s, ACT.Copy), J)
                if J == 4 * NKT + 6:
                    exponent(0)
            exponent(1)
            for n in range(NB):
                g, b = n // 4, n % 4
                pt = slice(32 * b, 32 * b + 32)
                act.wait_ge(ov_psum, n + 1)
                act.activation(eout[g][pt, :], PS[pt, OV_BANK[b], :], ACT.Copy).then_inc(ov_taken, 1)

        def phase_e_dve(dve):
            def scores(B):
                g, b = B // 4, B % 4
                pt = slice(32 * b, 32 * b + 32)
                dve.wait_ge(st_psum, NKT * (B + 1))
                for n, (at_, w) in enumerate(((0, NFT * P), (NFT * P, 4 * P))):
                    ins = dve.tensor_tensor_reduce(pb[g][pt, at_:at_ + w], PS[pt, score_banks(B) + n, 0:w], bkey[pt, at_:at_ + w],
                                                   -1.0, 3e38, ALU.add, ALU.min, estat[pt, g, n:n + 1])
                link("dve", dve, ins)
                dve.nop().then_inc(st_taken, 1)

            def minimum(g):
                dve.wait_ge(sb_psum, g + 1)
                link("dve", dve, dve.tensor_tensor_reduce(pb[g][:, NKEY - NS:], PS[:, 6, g * NS:(g + 1) * NS], bother[:, g, :],
                                                          -1.0, 3e38, ALU.add, ALU.min, estat[:, g, 2:3]))
                dve.tensor_reduce(estat[:, g, 3:4], estat[:, g, 0:3], AX.X, ALU.min).then_inc(e_min, 1)

            def normalise(g):
                dve.wait_ge(e_exp, g + 1)
                link("dve", dve, dve.reciprocal(estat[:, g, 5:6], estat[:, g, 4:5]))
                dve.tensor_scalar(pb[g], pb[g], estat[:, g, 5:6], None, ALU.mult).then_inc(p_ready, 1)

            def transposed(g):
                dve.wait_ge(pk_psum, g + 1)
                if g:
                    dve.wait_ge(ov_psum, 4)
                dve.tensor_copy(ptk[:, 0:4, :], PS[:, 2, :].rearrange("p (k q) -> p k q", q=P))
                dve.tensor_copy(ptk[:, 4:NKT, :], PS[:, 3, 0:(NKT - 4) * P].rearrange("p (k q) -> p k q", q=P))
                dve.tensor_copy(ptk[0:NS, NKT, :], PS[0:NS, 7, 0:P]).then_inc(ptk_ready, 1)

            dve.wait_ge(e_in, 48)
            dve.memset(ra[32:33, :], 1.0).then_inc(ra_ready, 1)
            link("dve", dve, dve.memset(rexp, 0.0))
            dve.wait_ge(ra_ready, 1)
            for t in range(NT):
                ins = dve.tensor_copy(rexp[:, t, :].rearrange("p (b h t) -> p b h t", b=4, h=H)[:, :, :, t],
                                      ra.unsqueeze(1).to_broadcast([33, 4, H]))
            ins.then_inc(rexp_ready, 1)
            dve.wait_ge(bkey_psum, 2)
            link("dve", dve, dve.tensor_copy(bkey.rearrange("p (a n) -> p a n", a=2), PS[:, 0:2, 0:NKEY // 2]))
            link("dve", dve, dve.tensor_tensor(bother, bother, bkey[:, NKEY - NS:].unsqueeze(1).to_broadcast([P, 2, NS]), ALU.add))
            dve.nop().then_inc(bkey_ready, 1)
            for J in range(NJ):
                if J % 2:
                    take_kt(dve, dve.tensor_copy, J)
                if J >= NKT and J % NKT == 1:
                    scores(J // NKT - 1)
                if J == 4 * NKT + 3:
                    minimum(0)
                if J == 4 * NKT + 7:
                    normalise(0)
            scores(NB - 1)
            transposed(0)
            minimum(1)
            normalise(1)
            transposed(1)
            for g in range(2):
                dve.wait_ge(eo_psum, g + 1)
                for h2 in range(2):
                    pt = slice(64 * h2, 64 * h2 + 64)
                    for a in range(4):
                        src = PS[pt, 2 + g, a * P:(a + 1) * P].rearrange("p (b h t) -> p b h t", b=4, t=NT)[:, :, 2 * a + h2, :]
                        dve.tensor_copy(atts[pt, a, 16 * g:16 * g + 16].rearrange("p (b t) -> p b t", t=NT), src)

        XH, XL = (view(x, 0, "", k=KD, t=NTOK) for x in (XH, XL))
        XHf = XH.bitcast(F32)
        x1 = view(R_x1, 0, "", i=NTILE, n=D)
        WOH = view(R_wo, 0, "", k=KD, n=D)

        def wo_low(k):
            return R_wo[:, 8192 + k * D:8192 + (k + 1) * D] if k < 4 else R_wo2[:, (k - 4) * D:(k - 3) * D]

        tmp4, tmp4b = ([view(r, at + n * 512, "", k=4, t=P) for n in range(2)] for r, at in ((R_x1, NCH * D), (R_row, 0)))

        FB = 256
        NF = FB // P
        NBLK = DFF // FB
        wup = i_["w_up"][0].rearrange("(c k p) n -> c p k n", k=4, p=P)
        wdn = i_["w_down"][0].rearrange("(f p) d -> f p d", p=P)
        def at(region, n):
            return region[:, n:n + 1024]

        CHUNKS = [(at(R_wo, k * D), wo_low(k), i_["w_out"][0, k * P:(k + 1) * P, :], at(R_x1, k * D))
                  for k in range(KD)]
        UP_CHUNKS, DOWN_CHUNKS = {}, {}
        for b in range(NBLK):
            UP_CHUNKS[b] = len(CHUNKS)
            for c in range(2):
                high = 2048 * c
                CHUNKS.append((at(R_up[b % 2], high), at(R_up[b % 2], high + 1024), wup[c, :, :, b * FB:(b + 1) * FB],
                               at(R_stage, len(CHUNKS) % 3 * 1024) if b else at(R_first, c * 1024)))
            DOWN_CHUNKS[b] = len(CHUNKS)
            for f in range(NF):
                high = 2048 * f
                CHUNKS.append((at(R_down, high), at(R_down, high + 1024), wdn[NF * b + f],
                               at(R_stage, len(CHUNKS) % 3 * 1024)))
        chunk_in = [sem(f"chunk_in{n}") for n in range(8)]
        NW = len(W_CHUNKS)

        def load_chunks(sp, first, last):
            for m in range(first, last):
                if m >= DOWN_CHUNKS[0]:
                    sp.wait_ge(chunk_split, NW + m - 2)
                src = CHUNKS[m][2]
                dst = CHUNKS[m][3] if len(src.shape) == 2 else CHUNKS[m][3].rearrange("p (k n) -> p k n", k=src.shape[1])
                sp.dma_start(dst, src).then_inc(chunk_in[m % 8], 16)

        def chunk_high_part(act, m):
            act.wait_ge(chunk_in[m % 8], 16 * (m // 8 + 1))
            act.activation(CHUNKS[m][0], CHUNKS[m][3], ACT.Copy).then_inc(chunk_high, 1)

        def chunk_low_part(dve, m):
            dve.wait_ge(chunk_high, NW + m + 1)
            dve.tensor_tensor(CHUNKS[m][1], CHUNKS[m][3], CHUNKS[m][0].bitcast(F32), ALU.subtract).then_inc(chunk_split, 1)

        head_ms, head_rms, f_scaled, f_psum = sem("head_ms"), sem("head_rms"), sem("f_scaled"), sem("f_psum")
        PARTS = ((slice(0, P), slice(0, NCH)), (slice(0, NS), slice(NCH, NTILE)))

        def phase_f1_sync(sp):
            load_chunks(sp, 0, KD)
            for i in range(NCH):
                sp.wait_ge(chunk_split, NW + i + 1)
                sp.dma_start(x1[:, i, :], i_["x_prompt"][0, i * P:(i + 1) * P, :]).then_inc(x1_in, 16)

        def phase_f1_act(act):
            for n, (pt, cs) in enumerate(PARTS):
                act.wait_ge(head_ms, n + 1)
                act.activation(hrstd[pt, :, cs, :], hstat[pt, :, cs, :], ACT.Sqrt).then_inc(head_rms, 1)
            for j in range(NTILE):
                for kk in range(2):
                    act.wait_ge(f_taken, 2 * NTILE + 2 * j + kk + 1)
                    ks, ts = half(j, kk)
                    act.activation(XH[:, ks, ts], tmp4[kk][:, :, 0:rows(j)], ACT.Copy).then_inc(f_high, 1)
                if j < KD:
                    chunk_high_part(act, j)

        def phase_f1_dve(dve):
            dve.memset(gout[:, 0:4], 1.0)
            for pt, cs in PARTS:
                dve.tensor_scalar(hstat[pt, :, cs, :], hstat[pt, :, cs, :], 1.0 / E, EPS, ALU.mult, ALU.add)\
                   .then_inc(head_ms, 1)
            for n, (pt, cs) in enumerate(PARTS):
                dve.wait_ge(head_rms, n + 1)
                link("dve", dve, dve.reciprocal(hrstd[pt, :, cs, :], hrstd[pt, :, cs, :]))

            def split_low(j, kk):
                ks, ts = half(j, kk)
                dve.wait_ge(f_high, 2 * NTILE + 2 * j + kk + 1)
                dve.tensor_tensor(XL[:, ks, ts], tmp4[kk][:, :, 0:rows(j)], XHf[:, ks, ts], ALU.subtract)\
                   .then_inc(f_split, 1)

            for i in range(NTILE + 2):
                if i < NTILE:
                    r = rows(i)
                    for w in range(2):
                        part = (mo, hg)[w][0:r, i, :].rearrange("p (h e) -> p h e", e=E)
                        ins = dve.tensor_tensor(part, part, hrstd[0:r, w, i, :].unsqueeze(2).to_broadcast([r, HM, E]), ALU.mult)
                    ins.then_inc(f_scaled, 1)
                if i >= 2:
                    j = i - 2
                    for kk in range(2):
                        if j:
                            dve.wait_ge(f_split, 2 * NTILE + 2 * j - 1 + kk)
                        ks, ts = half(j, kk)
                        if j == NCH and kk == 0:
                            dve.tensor_copy(tmp4[kk][:, :, 0:NS], atts[:, :, :]).then_inc(f_taken, 1)
                            continue
                        dve.wait_ge(f_psum, 2 * j + (kk if j < NCH else 0) + 1)
                        src = PS[:, 2 * (j % 2) + kk, :].rearrange("p (k t) -> p k t", t=P)[:, :, 0:rows(j)]
                        dve.tensor_tensor(tmp4[kk][:, :, 0:rows(j)], src,
                                          gout[:, 4 * kk:4 * kk + 4].unsqueeze(2).to_broadcast([P, 4, rows(j)]),
                                          ALU.mult).then_inc(f_taken, 1)
                    for kk in range(2):
                        split_low(j, kk)
                    if j < KD:
                        chunk_low_part(dve, j)

        def phase_f1_pe(pe):
            for i in range(NTILE):
                r = rows(i)
                pe.wait_ge(f_scaled, i + 1)
                if i >= 2:
                    pe.wait_ge(f_taken, 2 * NTILE + 2 * (i - 1))
                for k in range(KD) if i < NCH else range(4, KD):
                    src = mixa[:, i, k * P:(k + 1) * P] if k < 4 else (mo, hg)[k // 2 - 2][0:r, i, k % 2 * P:(k % 2 + 1) * P]
                    t = pe.transpose(PS[:, 2 * (i % 2) + k // 4, (k % 4) * P:(k % 4) * P + r], src, ident[0:r, 0:r])
                    if k % 4 == 3:
                        t.then_inc(f_psum, 1)

        xs2 = [R_xs2[:, n * D:(n + 1) * D] for n in range(2)]
        x1_in = sem("x1_in")
        op_psum, x1_ready, xs2_ready, xs2_T = sem("op_psum"), sem("x1_ready"), sem("xs2_ready"), sem("xs2_T")

        def phase_f2_sync(sp):
            sp.dma_start(x1[0:P - NS, NCH, :], i_["x_prompt"][0, S - (P - NS):S, :]).then_inc(x1_in, 16)
            sp.dma_start(x1[P - NS:P, NCH, :], i_["x_sample"].rearrange("b t d -> (b t) d")).then_inc(x1_in, 16)
            load_chunks(sp, UP_CHUNKS[0], UP_CHUNKS[0] + 2)

        def phase_f2_pe(pe):
            for i in range(NTILE + 2):
                if i < NTILE:
                    if i >= 2:
                        pe.wait_ge(x1_ready, 2 * (i - 1))
                    ts = last_tokens(i)
                    for n in range(2):
                        ns = slice(n * 512, (n + 1) * 512)
                        product(pe, PS[:, 4 + 2 * (i % 2) + n, :], lambda k: (XH[:, k, ts], XL[:, k, ts]),
                                lambda k: (WOH[:, k, ns], wo_low(k)[:, ns]), KD).then_inc(op_psum, 1)
                if i >= 2:
                    j = i - 2
                    pe.wait_ge(xs2_ready, j + 1)
                    if j >= 2:
                        pe.wait_ge(f_taken, 4 * NTILE + 2 * (j - 1))
                    for k in range(KD):
                        t = pe.transpose(PS[:, 2 * (j % 2) + k // 4, (k % 4) * P:(k % 4 + 1) * P],
                                         xs2[j % 2][:, k * P:(k + 1) * P], ident[:, :])
                        if k % 4 == 3:
                            t.then_inc(xs2_T, 1)

        def phase_f2_act(act):
            for i in range(NTILE + 2):
                if i < NTILE:
                    act.wait_ge(x1_ready, 2 * i + 2)
                    if i >= 2:
                        act.wait_ge(xs2_T, 2 * (i - 1))
                    act.activation(xs2[i % 2], x1[:, i, :], ACT.Square, accum_out=stat[:, 0, i:i + 1]).then_inc(sumsq_ready, 1)
                    act.wait_ge(meansq_ready, NTILE + i + 1)
                    act.activation(stat[:, 2, i:i + 1], stat[:, 1, i:i + 1], ACT.Sqrt).then_inc(rms_ready, 1)
                if i >= 2:
                    j = i - 2
                    act.wait_ge(op_psum, 2 * min(j + 2, NTILE))
                    for kk in range(2):
                        act.wait_ge(f_taken, 4 * NTILE + 2 * j + kk + 1)
                        ks, ts = half(j, kk)
                        act.activation(XH[:, ks, ts], tmp4b[kk][:, :, P - rows(j):], ACT.Copy).then_inc(f_high, 1)
                    if j in (2, 5):
                        chunk_high_part(act, UP_CHUNKS[0] + j // 3)

        def phase_f2_dve(dve):
            dve.wait_ge(x1_in, 16 * 10)
            for i in range(NTILE + 2):
                if i < NTILE:
                    for n in range(2):
                        dve.wait_ge(op_psum, 2 * i + n + 1)
                        part = x1[:, i, n * 512:(n + 1) * 512]
                        dve.tensor_tensor(part, part, PS[:, 4 + 2 * (i % 2) + n, :], ALU.add).then_inc(x1_ready, 1)
                    dve.wait_ge(sumsq_ready, NTILE + i + 1)
                    dve.tensor_scalar(stat[:, 1, i:i + 1], stat[:, 0, i:i + 1], 1.0 / D, EPS,
                                      ALU.mult, ALU.add).then_inc(meansq_ready, 1)
                    dve.wait_ge(rms_ready, NTILE + i + 1)
                    link("dve", dve, dve.reciprocal(stat[:, 3, i:i + 1], stat[:, 2, i:i + 1]))
                    dve.tensor_scalar(xs2[i % 2], x1[:, i, :], stat[:, 3, i:i + 1], None,
                                      ALU.mult).then_inc(xs2_ready, 1)
                if i >= 2:
                    j = i - 2
                    for kk in range(2):
                        dve.wait_ge(xs2_T, 2 * j + kk + 1)
                        if j:
                            dve.wait_ge(f_split, 4 * NTILE + 2 * j - 1 + kk)
                        src = PS[:, 2 * (j % 2) + kk, :].rearrange("p (k t) -> p k t", t=P)
                        dve.tensor_tensor(tmp4b[kk], src, gffn[:, 4 * kk:4 * kk + 4].unsqueeze(2).to_broadcast([P, 4, P]),
                                          ALU.mult).then_inc(f_taken, 1)
                    for kk in range(2):
                        dve.wait_ge(f_high, 4 * NTILE + 2 * j + kk + 1)
                        ks, ts = half(j, kk)
                        dve.tensor_tensor(XL[:, ks, ts], tmp4b[kk][:, :, P - rows(j):], XHf[:, ks, ts], ALU.subtract)\
                           .then_inc(f_split, 1)
                    if j in (2, 5):
                        chunk_low_part(dve, UP_CHUNKS[0] + j // 3)

        up_w = [view(r, 0, "", c=2, s=2, k=4, n=FB) for r in R_up]
        down_w = view(R_down, 0, "", f=NF, s=2, d=D)
        UH, UL = (view(R_u, n * NF * NTOK, "", f=NF, t=NTOK) for n in range(2))
        UHf = UH.bitcast(F32)
        u_pos = [R_upos[:, n * TG:(n + 1) * TG] for n in range(2)]
        u_sq = [R_usq[:, n * TG:(n + 1) * TG] for n in range(2)]
        grow, sqj3 = R_row, R_junk
        NU = 3 * NF
        ND = 2 * NTILE
        u_psum, u_relu, u_squared, u_high, u_split = (sem("u_psum"), sem("u_relu"), sem("u_squared"), sem("u_high"),
                                                      sem("u_split"))
        d_psum, d_taken = sem("d_psum"), sem("d_taken")
        g_row_in, y_ready, y_stored = sem("g_row_in"), sem("y_ready"), sem("y_stored")
        UP_AT, DOWN_AT = {0: 0, 2: 1}, {3: 0, 9: 1}

        def phase_g_sync(sp):
            sp.dma_start(grow, i_["g_final"].rearrange("(o d) -> o d", o=1).to_broadcast([P, D])).then_inc(g_row_in, 16)
            load_chunks(sp, DOWN_CHUNKS[0], len(CHUNKS))
            for i in range(NTILE):
                sp.wait_ge(y_ready, i + 1)
                if i < NCH:
                    sp.dma_start(o_["y_p"][0, i * P:(i + 1) * P, :], x1[:, i, :]).then_inc(y_stored, 16)
                else:
                    sp.dma_start(o_["y_s"].rearrange("b t d -> (b t) d"), x1[P - NS:P, i, :]).then_inc(y_stored, 16)
            sp.wait_ge(y_stored, 16 * NTILE)

        def phase_g_pe(pe):
            for b in range(NBLK):
                pe.wait_ge(chunk_split, NW + UP_CHUNKS[b] + 2)
                for u in range(NU):
                    f, g = u // 3, u % 3
                    U = b * NU + u
                    if U >= 4:
                        pe.wait_ge(u_relu, U - 3)
                    fs, ts = slice(f * P, (f + 1) * P), slice(g * TG, (g + 1) * TG)
                    product(pe, PS[:, U % 4, 0:TG], lambda k: (up_w[b % 2][:, k // 4, 0, k % 4, fs], up_w[b % 2][:, k // 4, 1, k % 4, fs]),
                            lambda k: (XH[:, k, ts], XL[:, k, ts]), KD).then_inc(u_psum, 1)
                pe.wait_ge(chunk_split, NW + DOWN_CHUNKS[b] + NF)
                for i in range(NTILE):
                    ts = last_tokens(i)
                    pe.wait_ge(u_split, (b + 1) * NU - 3 + (ts.stop - 1) // TG + 1)
                    for n in range(2):
                        j = b * ND + 2 * i + n
                        if j >= 4:
                            pe.wait_ge(d_taken, j - 3)
                        ns = slice(n * 512, (n + 1) * 512)
                        product(pe, PS[:, 4 + j % 4, :], lambda f: (UH[:, f, ts], UL[:, f, ts]),
                                lambda f: (down_w[:, f, 0, ns], down_w[:, f, 1, ns]), NF).then_inc(d_psum, 1)

        def phase_g_act(act):
            for b in range(NBLK):
                if b:
                    act.wait_ge(d_psum, ND * b)
                for u in range(NU):
                    f, g = u // 3, u % 3
                    U = b * NU + u
                    act.wait_ge(u_relu, U + 1)
                    if U >= 2:
                        act.wait_ge(u_split, U - 1)
                    act.activation(u_sq[U % 2], u_pos[U % 2], ACT.Square).then_inc(u_squared, 1)
                    act.wait_ge(u_squared, U + 1)
                    act.activation(UH[:, f, g * TG:(g + 1) * TG], u_sq[U % 2], ACT.Copy).then_inc(u_high, 1)
                    if u in UP_AT:
                        chunk_high_part(act, DOWN_CHUNKS[b] + UP_AT[u])
                if b + 1 < NBLK:
                    for c in range(2):
                        chunk_high_part(act, UP_CHUNKS[b + 1] + c)
            act.wait_ge(u_psum, NU * NBLK)
            for i in range(NTILE):
                act.wait_ge(d_taken, ((NBLK - 1) * NTILE + i) * 2 + 2)
                act.activation(sqj3, x1[:, i, :], ACT.Square, accum_out=stat[:, 0, i:i + 1]).then_inc(sumsq_ready, 1)
                act.wait_ge(meansq_ready, 2 * NTILE + i + 1)
                act.activation(stat[:, 2, i:i + 1], stat[:, 1, i:i + 1], ACT.Sqrt).then_inc(rms_ready, 1)

        def phase_g_dve(dve):
            def final(i):
                dve.wait_ge(sumsq_ready, 2 * NTILE + i + 1)
                dve.tensor_scalar(stat[:, 1, i:i + 1], stat[:, 0, i:i + 1], 1.0 / D, EPS,
                                  ALU.mult, ALU.add).then_inc(meansq_ready, 1)
                dve.wait_ge(rms_ready, 2 * NTILE + i + 1)
                link("dve", dve, dve.reciprocal(stat[:, 3, i:i + 1], stat[:, 2, i:i + 1]))
                dve.scalar_tensor_tensor(x1[:, i, :], x1[:, i, :], stat[:, 3, i:i + 1], grow,
                                         ALU.mult, ALU.mult).then_inc(y_ready, 1)

            def piece_low(U):
                f, g = U % NU // 3, U % 3
                dve.wait_ge(u_high, U + 1)
                dve.tensor_tensor(UL[:, f, g * TG:(g + 1) * TG], u_sq[U % 2], UHf[:, f, g * TG:(g + 1) * TG],
                                  ALU.subtract).then_inc(u_split, 1)

            dve.wait_ge(g_row_in, 16)
            for b in range(NBLK):
                for u in range(NU):
                    U = b * NU + u
                    dve.wait_ge(u_psum, U + 1)
                    if U >= 2:
                        dve.wait_ge(u_squared, U - 1)
                    dve.tensor_scalar(u_pos[U % 2], PS[:, U % 4, 0:TG], 0.0, None, ALU.max).then_inc(u_relu, 1)
                    if u:
                        piece_low(U - 1)
                    if u - 1 in UP_AT:
                        chunk_low_part(dve, DOWN_CHUNKS[b] + UP_AT[u - 1])
                piece_low(b * NU + NU - 1)
                for m in range(ND):
                    i, n = m // 2, m % 2
                    j = b * ND + m
                    dve.wait_ge(d_psum, j + 1)
                    part = x1[:, i, n * 512:(n + 1) * 512]
                    dve.tensor_tensor(part, part, PS[:, 4 + j % 4, :], ALU.add).then_inc(d_taken, 1)
                    if b + 1 < NBLK and m in DOWN_AT:
                        chunk_low_part(dve, UP_CHUNKS[b + 1] + DOWN_AT[m])
                    if b == NBLK - 1 and n and i:
                        final(i - 1)
            final(NTILE - 1)


        PHASES = {
            "sync": [phase_a_sync, phase_b1_sync, phase_d1_sync, phase_d2_sync, phase_b2_sync, phase_c_sync,
                     phase_e_sync, phase_f1_sync, phase_f2_sync, phase_g_sync],
            "gps": [phase_a_gps, phase_b1_gps, None, phase_d2_gps, phase_b2_gps, None, None, None, None, None],
            "act": [phase_a_act, phase_b1_act, phase_d1_act, phase_d2_act, phase_b2_act, phase_c_act,
                    phase_e_act, phase_f1_act, phase_f2_act, phase_g_act],
            "dve": [phase_a_dve, phase_b1_dve, phase_d1_dve, phase_d2_dve, phase_b2_dve, phase_c_dve,
                    phase_e_dve, phase_f1_dve, phase_f2_dve, phase_g_dve],
            "pe": [phase_a_pe, phase_b1_pe, phase_d1_pe, phase_d2_pe, phase_b2_pe, phase_c_pe,
                   phase_e_pe, phase_f1_pe, phase_f2_pe, phase_g_pe],
        }

        def run(eng, name):
            for f in PHASES[name][:upto]:
                if f is not None:
                    f(eng)
                barrier(eng, name)

        locals_ = dict(aqk=aqk, mqk=mqk, hqk=hqk, hb=hb, va=va, vm=vm, mo=mo[:, 0:8, :], hi=hi, hg=hg)
        tap_sem = y_stored

        @block.sync
        def _(sp):
            run(sp, "sync")
            if taps is not None:
                for n, (name, ap) in enumerate(taps(locals_).items()):
                    sp.dma_start(o_[name], ap).then_inc(tap_sem, 16)
                    sp.wait_ge(tap_sem, 16 * (n + 1))


        @block.gpsimd
        def _(pool):
            run(pool, "gps")

        @block.scalar
        def _(act):
            run(act, "act")

        @block.vector
        def _(dve):
            run(dve, "dve")

        @block.tensor
        def _(pe):
            run(pe, "pe")


OUTPUTS = {
    "y_p": (1, S, D), "y_s": (NB, NT, D), "p_k": (1, 1, S, H, E), "p_v": (1, 1, S, H, E), "p_conv": (1, 1, 3, 512),
    "p_C": (1, 1, HM, E, E), "p_n": (1, 1, HM, E), "p_m": (1, 1, HM), "p_S": (1, 1, HM, E, E),
    "s_k": (1, NB, NT, H, E), "s_v": (1, NB, NT, H, E), "s_conv": (1, NB, 3, 512), "s_C": (1, NB, HM, E, E),
    "s_n": (1, NB, HM, E), "s_m": (1, NB, HM), "s_S": (1, NB, HM, E, E),
}
INPUTS = ["x_prompt", "x_sample", "cache_attn_k", "cache_attn_v", "state_mlstm_conv", "state_mlstm_C", "state_mlstm_n",
          "state_mlstm_m", "state_hgrn_S", "rel_bias", "g_mix", "w_in", "mlstm_gate_b", "mlstm_conv_w", "mlstm_norm_g",
          "hgrn_lb_raw", "hgrn_norm_g", "w_out", "g_ffn", "w_up", "w_down", "g_final"]


def kernel(**inputs):
    import numpy as _np
    import concourse.bacc as _bacc
    from concourse import mybir as _mybir
    from concourse.bass_utils import run_bass_kernel_spmd as _run

    nc = _bacc.Bacc("TRN2", target_bir_lowering=False, num_devices=1)
    arrays = {f"in_{n}": _np.ascontiguousarray(inputs[n]) for n in INPUTS}
    arrays.update({f"in_{n}": a for n, a in constants().items()})
    i_ = {n[3:]: nc.dram_tensor(n, a.shape, _mybir.dt.from_np(a.dtype), kind="ExternalInput").ap()
          for n, a in arrays.items()}
    o_ = {n: nc.dram_tensor(f"out_{n}", shape, _mybir.dt.float32, kind="ExternalOutput").ap()
          for n, shape in OUTPUTS.items()}
    program(nc, i_, o_)
    r = _run(nc, [arrays], core_ids=[0])
    return tuple(r.results[0][f"out_{n}"] for n in OUTPUTS)
```

```python
from contextlib import ExitStack

import numpy as np
import concourse.bass as bass
from concourse import mybir

ALU = mybir.AluOpType
ACT = mybir.ActivationFunctionType
AX = mybir.AxisListType
F32 = mybir.dt.float32
F32R = mybir.dt.float32r

P = 128
D = 1024
KD = D // P
S = 1024
NB, NT = 8, 4
NS = NB * NT
NTOK = S + NS
TG = NTOK // 3
H, E = 8, 64
HM = 4
NCH = S // P
NTILE = NCH + 1
WB = 2048
FAR, NFAR = 1536, 96
DFF = 4096
EPS = 1e-6
NEG = -1e30
NLEV = 8
UW = 256
SLOTS = 3
TOE = S + P - 1
NKEY = 4 * NFAR + 4 * P + NS
FW = 1152

AQ, AK, AV = 0, 512, 1024
MQ, MK, MV, MO, MI, MF = 1536, 1792, 2048, 2304, 2560, 2564
HQ, HF, HI, HG = 2568, 2824, 3080, 3336


def rows(i):
    return P if i < NCH else NS


def tile_tokens(i):
    return slice(i * P, i * P + rows(i))


def _bucket(dist):
    n = np.asarray(dist).astype(np.int32)
    scaled = np.log(np.maximum(n, 1) / 16) / np.log(2048 / 16)
    large = np.minimum(16 + (scaled * 16).astype(np.int32), 31)
    return np.where(n < 16, n, large).astype(np.int32)


def _bias_rows(dist):
    d = np.asarray(dist)
    out = np.zeros((33,) + d.shape, np.float32)
    b = _bucket(np.clip(d, 0, None))
    for n in range(32):
        out[n] = b == n
    c = np.zeros(d.shape, np.int32)
    for window, dil in ((128, 1), (512, 4), (2048, 16)):
        c += (d >= 0) & (d <= window) & (d % dil == 0)
    out[32] = np.where(c > 0, np.log(np.maximum(c, 1).astype(np.float64)), NEG)
    return out


def constants():
    c = {}
    c["c_ident"] = np.eye(P, dtype=np.float32)
    toe = np.full(FW, 1 << 20, np.int64)
    toe[:TOE] = S - 1 - np.arange(TOE)
    c["c_bias_toe"] = _bias_rows(toe)
    idx = np.concatenate([
        16 * (np.arange(4 * NFAR) // 4) + np.arange(4 * NFAR) % 4,
        np.concatenate([FAR + 4 * np.arange(P) + k for k in range(4)]),
    ])
    dist = np.zeros((NT, NKEY), np.int64)
    for t in range(NT):
        dist[t, :NKEY - NS] = WB + t - idx
        dist[t, NKEY - NS:] = t - np.arange(NS) % NT
    c["c_bias_keys"] = np.ascontiguousarray(_bias_rows(dist))
    other = np.zeros((P, 2, NS), np.float32)
    for p in range(P):
        for g in range(2):
            other[p, g] = np.where(np.arange(NS) // NT == 4 * g + p // 32, 0.0, NEG)
    c["c_other_batch"] = other
    s, t = np.arange(P)[:, None], np.arange(P)[None]
    lev = np.zeros((P, NLEV, P), np.float32)
    for l in range(NLEV - 1):
        m = 64 >> l
        lev[:, l] = (s // (2 * m) == t // (2 * m)) & (s % (2 * m) < m) & (t % (2 * m) >= m)
    lev[:, NLEV - 1] = s == t
    c["c_levels"] = lev
    cm = np.zeros((P, P + NS), np.float32)
    cm[:, :P] = np.where(s <= t, 0.0, NEG)
    s4, t4 = np.arange(NS)[:, None], np.arange(NS)[None]
    cm[:NS, P:] = np.where((s4 // NT == t4 // NT) & (s4 <= t4), 0.0, NEG)
    c["c_causal"] = cm
    seg = np.ones((1, NTOK), np.float32)
    seg[0, 0:S:P] = 0.0
    seg[0, S::NT] = 0.0
    c["c_seg"] = seg
    sel = np.zeros((HM, HM + 2, P), np.float32)
    for h in range(HM):
        sel[h, h] = 1.0
        sel[h, HM + h // 2, 64 * (h % 2):64 * (h % 2) + 64] = 1.0
    c["c_sel"] = sel
    c["c_batch"] = (np.arange(NS)[:, None] // NT == np.arange(NB)[None]).astype(np.float32)
    return c


def program(nc, i_, o_):
    ctx = ExitStack()
    with ctx:
        def sb(name, shape):
            return ctx.enter_context(nc.sbuf_tensor(name, shape, F32))

        def sem(name):
            return ctx.enter_context(nc.semaphore(name))

        PS = ctx.enter_context(nc.psum_tensor("PS", [P, 8, 512], F32))

        def place(name, at, n, dtype=F32):
            with nc.sbuf_tensor(name + "_before", [P, max(at, 8)], F32):
                if at:
                    with nc.sbuf_tensor(name, [P, n], dtype) as t:
                        return t[:, :]
            with nc.sbuf_tensor(name, [P, n], dtype) as t:
                return t[:, :]

        XNH, XNL = place("xn_high", 0, KD * NTOK, F32R), place("xn_low", 8448, KD * NTOK, F32R)
        R_mo = place("R_mo", 16896, 2304)
        R_hg = place("R_hg", 19200, 2304)
        R_a = place("R_a", 21504, 14336)
        R_mqk = place("R_mqk", 21504, 4224)
        R_hqk = place("R_hqk", 25728, 4224)
        R_hb = place("R_hb", 29952, 2112)
        R_vm = place("R_vm", 32064, 2340)
        R_hi = place("R_hi", 34404, 2304)
        R_gs = [place("R_gs0", 16896, 4 * NTOK), place("R_gs1", 32064, 4 * NTOK)]
        R_wa = place("R_wa", 36708, 4096, F32R)
        R_wb = place("R_wb", 40804, 4096, F32R)
        R_wg = place("R_wg", 41828, 3072, F32R)
        R_conv = place("R_conv", 40804, 4278)
        R_wstage = place("R_wstage", 45082, 3072)
        R_d = place("R_d", 36708, 8320)
        R_as = place("R_as", 32064, 2 * P)
        R_x0 = place("R_x0", 45082, 2304)
        R_d2 = place("R_d2", 21504, 4224)
        R_aqk = place("R_aqk", 21504, 8448)
        R_va = place("R_va", 29952, 4680)
        R_wc = [place("R_wc0", 34632, 4096, F32R), place("R_wc1", 38728, 4096, F32R)]
        R_kstage = place("R_kstage", 42824, 1024)
        R_att = place("R_att", 0, 6144)
        R_mixa = place("R_mixa", 12800, 4096)
        R_cache = [place(f"R_cache{n}", at, 3584) for n, at in enumerate(
            (6144, 34632, 38728, 42824, 46920, 21504, 25600, 29952))]
        R_pb3 = place("R_pb3", 10240, S)
        R_ptk = place("R_ptk", 10240, 1024)
        R_eout = place("R_eout", 11264, 1024)
        R_keyrows = place("R_keyrows", 29952, NT * NKEY)
        R_atts = place("R_atts", 12416, 128)
        seg = place("seg", 48300, NTOK)
        bm = place("bm", 49356, NTOK)[0:HM, :]
        R_gcol = place("R_gcol", 50412, NTILE * P)
        sel = place("sel", 51564, (HM + 2) * P)[0:HM, :]
        XH, XL = (place(n, at, 8448, F32R) for n, at in (("x_high", 21504), ("x_low", 29952)))
        R_x1 = place("R_x1", 38400, 9216)
        R_wo = place("R_wo", 0, 12288, F32R)
        R_wo2 = place("R_wo2", 47616, 4096, F32R)
        R_up = [place("R_up0", 12288, 4096, F32R), place("R_up1", 16384, 4096, F32R)]
        R_down = place("R_down", 0, 4096, F32R)
        R_stage = place("R_stage", 4096, 3072)
        R_upos = place("R_upos", 7168, 704)
        R_usq = place("R_usq", 7872, 704)
        R_u = place("R_u", 47616, 4224, F32R)
        R_first = place("R_first", 16384, 2048)
        R_xs2 = place("R_xs2", 18432, 2048)
        R_row = place("R_row", 20480, 1024)
        R_junk = place("R_junk", 12288, 1024)
        sb("arena", [P, 52336])

        def view(region, at, **dims):
            n = int(np.prod(list(dims.values())))
            names = " ".join(dims)
            part = dict(list(dims.items())[1:])
            return region[:, at:at + n].rearrange(f"p ({names}) -> p {names}", **part)

        XNH, XNL = (view(x, 0, k=KD, t=NTOK) for x in (XNH, XNL))
        mixa = view(R_mixa, 0, a=4, s=S)
        atts = view(R_atts, 0, a=4, s=NS)
        aqk = view(R_aqk, 0, k=8, t=NTOK)
        mqk = view(R_mqk, 0, k=4, t=NTOK)
        hqk = view(R_hqk, 0, k=4, t=NTOK)
        hb = view(R_hb, 0, k=2, t=NTOK)
        va = view(R_va, 0, i=NTILE, h=H, e=E + 1)
        vm = view(R_vm, 0, i=NTILE, h=HM, e=E + 1)
        mo = view(R_mo, 0, i=NTILE, n=256)
        hi = view(R_hi, 0, i=NTILE, n=256)
        hg = view(R_hg, 0, i=NTILE, n=256)

        ident = sb("ident", [P, P])
        gmix = sb("gmix", [P, KD])
        gffn = sb("gffn", [P, KD])
        gout = sb("gout", [P, KD])
        convw = sb("convw", [P, 4, 4])
        lb3 = sb("lb3", [P, 6, 2])
        gateb = sb("gateb", [P, 1])
        m0 = sb("m0", [HM, NB])
        selv = sel[:, :].rearrange("h (a p) -> h a p", p=P)
        stat = sb("stat", [P, 4, 12])
        cstate = sb("cstate", [P, 4, 24])
        ctail = sb("ctail", [P, 4, 27])
        egl = sb("egl", [HM, 16])
        gcol = view(R_gcol, 0, i=NTILE, n=P)
        glc = sb("glc", [P, 2, 16])
        small = sb("small", [P, 64])

        def const(name):
            return i_[name]

        fdr = nc.dram_tensor("bias_by_distance", [H, FW], F32, kind="Internal").ap()
        frep = nc.dram_tensor("bias_by_distance_copies", [H, P, FW], F32, kind="Internal").ap()

        phase_end = sem("phase_end")
        phase = {}

        def barrier(eng, name):
            phase[name] = phase.get(name, 0) + 1
            eng.drain().then_inc(phase_end, 1)
            eng.wait_ge(phase_end, 5 * phase[name])

        consts_in = sem("consts_in")
        x_in = [sem(f"x_in{n}") for n in range(3)]
        sumsq_ready, meansq_ready, rms_ready = sem("sumsq_ready"), sem("meansq_ready"), sem("rms_ready")
        xs_ready, xs_transposed = sem("xs_ready"), sem("xs_transposed")
        f_taken, f_high, f_split = sem("half_taken"), sem("half_high"), sem("half_split")
        chunk_high, chunk_split = sem("chunk_high"), sem("chunk_split")
        dve_order, act_order, pe_order = sem("dve_order"), sem("act_order"), sem("pe_order")
        order = {"dve": 0, "act": 0, "pe": 0}

        def link(name, eng, ins):
            s = {"dve": dve_order, "act": act_order, "pe": pe_order}[name]
            order[name] += 1
            ins.then_inc(s, 1)
            eng.wait_ge(s, order[name])

        bias_in, bias_ready, bias_copied, bias_stored = sem("bias_in"), sem("bias_ready"), sem("bias_copied"), sem("bias_stored")
        wgate_zero, wgate_in = sem("wgate_zero"), sem("wgate_in")
        w_in_ready = [sem(f"w_in_ready{n}") for n in range(SLOTS)]
        gate_psum, gate_taken = sem("gate_psum"), sem("gate_taken")
        gate_abs, gate_soft, gate_args, gate_rows = sem("gate_abs"), sem("gate_soft"), sem("gate_args"), sem("gate_rows")
        gate_last, gate_cols, gcol_ready, glc_psum = sem("gate_last"), sem("gate_cols"), sem("gcol_ready"), sem("glc_psum")
        cstate_psum = sem("cstate_psum")
        t_psum, t_taken = sem("t_psum"), sem("t_taken")
        sig_ready, conv_in, conv_done, h_done = sem("sig_ready"), sem("conv_in"), sem("conv_done"), sem("h_done")
        lnf_ready, f_ready = sem("lnf_ready"), sem("f_ready")
        n_psum, n_taken = sem("n_psum"), sem("n_taken")
        tail_psum, tail_copied = sem("tail_psum"), sem("tail_copied")
        def half(j, kk):
            return slice(4 * kk, 4 * kk + 4), tile_tokens(j)

        def last_tokens(i):
            return slice(i * P, (i + 1) * P) if i < NCH else slice(NTOK - P, NTOK)

        def product(pe, out, lhs, rhs, n):
            for k in range(n):
                (lh, ll), (rh, rl_) = lhs(k), rhs(k)
                pe.matmul(out, ll, rh, start=(k == 0), stop=False)
                pe.matmul(out, lh, rl_, start=False, stop=False)
                mm = pe.matmul(out, lh, rh, start=False, stop=(k == n - 1))
            return mm

        block = ctx.enter_context(nc.Block())

        xt = [R_a[:, 3072 + n * D:3072 + (n + 1) * D] for n in range(NTILE)]
        sqj = R_a[:, 12288:12288 + D]
        tmpx = [[view(r, at + n * 512, k=4, t=P) for n in range(2)] for r, at in ((R_conv, 0), (R_a, 13312))]
        cst_nat = R_a[0:24, 0:512]
        toe_in = R_a[0:33, 512:512 + FW]
        raug = R_a[0:33, 1700:1708]
        F_sb = R_a[0:8, 1800:1800 + FW]

        def phase_a_sync(sp):
            def small_inputs():
                for n, (dst, src) in enumerate([
                    (seg[:, :], const("c_seg").to_broadcast([P, NTOK])),
                    (gmix[:, :], i_["g_mix"][0].rearrange("(k p) -> p k", p=P)),
                    (gffn[:, :], i_["g_ffn"][0].rearrange("(k p) -> p k", p=P)),
                    (gout[:, 4:6], i_["mlstm_norm_g"][0].rearrange("(k p) -> p k", p=P)),
                    (gout[:, 6:8], i_["hgrn_norm_g"][0].rearrange("(k p) -> p k", p=P)),
                    (lb3[:, 0, :], i_["hgrn_lb_raw"][0].rearrange("(k p) -> p k", p=P)),
                    (gateb[0:4, :], i_["mlstm_gate_b"][0, 0:1, :].rearrange("o h -> h o")),
                    (gateb[32:36, :], i_["mlstm_gate_b"][0, 1:2, :].rearrange("o h -> h o")),
                    (m0[:, :], i_["state_mlstm_m"][0].rearrange("b h -> h b")),
                    (selv, const("c_sel")),
                    (cst_nat, i_["state_mlstm_conv"][0].rearrange("b j n -> (b j) n")),
                ] + [(convw[:, k, :], i_["mlstm_conv_w"][0, :, k * P:(k + 1) * P].rearrange("j p -> p j"))
                     for k in range(4)]):
                    sp.dma_start(dst, src, allow_slow_non_contiguous=True).then_inc(consts_in, 16)

            sp.dma_start(ident[:, :], const("c_ident")).then_inc(bias_in, 16)
            sp.dma_start(toe_in, const("c_bias_toe")).then_inc(bias_in, 16)
            sp.dma_start(raug[0:32, :], i_["rel_bias"]).then_inc(bias_in, 16)
            for i in range(NTILE):
                if i >= 3:
                    sp.wait_ge(x_in[i % 3], 16 * (i // 3))
                src = i_["x_prompt"][0, i * P:(i + 1) * P, :] if i < NCH else i_["x_sample"].rearrange("b t d -> (b t) d")
                sp.dma_start(xt[i][0:rows(i), :], src).then_inc(x_in[i % 3], 16)
                if i == 2:
                    small_inputs()
                    first_w(sp)
            sp.wait_ge(bias_copied, 1)
            sp.dma_start(fdr, F_sb).then_inc(bias_stored, 16)
            sp.wait_ge(bias_stored, 16)
        NCONST = 15 * 16

        def phase_a_act(act):
            def high_part(j):
                for kk in range(2):
                    act.wait_ge(f_taken, 2 * j + kk + 1)
                    ks, ts = half(j, kk)
                    act.activation(XNH[:, ks, ts], tmpx[j % 2][kk][:, :, 0:rows(j)], ACT.Copy).then_inc(f_high, 1)

            def square(i):
                r = rows(i)
                act.wait_ge(x_in[i % 3], 16 * (i // 3 + 1))
                if i:
                    act.wait_ge(sumsq_ready, i)
                act.activation(sqj[0:r, :], xt[i][0:r, :], ACT.Square,
                               accum_out=stat[0:r, 0, i:i + 1]).then_inc(sumsq_ready, 1)

            def root(i):
                r = rows(i)
                act.wait_ge(meansq_ready, i + 1)
                act.activation(stat[0:r, 2, i:i + 1], stat[0:r, 1, i:i + 1], ACT.Sqrt).then_inc(rms_ready, 1)

            square(0)
            square(1)
            root(0)
            for i in range(NTILE):
                if i + 2 < NTILE:
                    square(i + 2)
                if i + 1 < NTILE:
                    root(i + 1)
                if i >= 1:
                    high_part(i - 1)
                if i in (3, 4, 5):
                    w_high_part(act, i - 3)
            high_part(NTILE - 1)
            act.wait_ge(lb_shifted, 1)
            act.activation(lb3[:, 2, :], lb3[:, 1, :], ACT.Exp).then_inc(lb_exp, 1)

        def phase_a_gps(pool):
            pool.memset(wst[0], 0.0).then_inc(wgate_zero, 1)
            for j in range(NTILE):
                for kk in range(2):
                    pool.wait_ge(f_high, 2 * j + kk + 1)
                    ks, ts = half(j, kk)
                    pool.tensor_tensor(XNL[:, ks, ts], tmpx[j % 2][kk][:, :, 0:rows(j)], XNH.bitcast(F32)[:, ks, ts],
                                       ALU.subtract).then_inc(f_split, 1)
                if j in (2, 3, 4):
                    w_low_parts(pool, j - 2, j - 1)

        def phase_a_dve(dve):
            dve.wait_ge(bias_in, 48)
            dve.memset(raug[32:33, :], 1.0).then_inc(bias_ready, 1)

            def mean_square(i):
                r = rows(i)
                dve.wait_ge(sumsq_ready, i + 1)
                dve.tensor_scalar(stat[0:r, 1, i:i + 1], stat[0:r, 0, i:i + 1], 1.0 / D, EPS,
                                  ALU.mult, ALU.add).then_inc(meansq_ready, 1)

            mean_square(0)
            for i in range(NTILE + 1):
                if i + 1 < NTILE:
                    mean_square(i + 1)
                if i < NTILE:
                    r = rows(i)
                    dve.wait_ge(rms_ready, i + 1)
                    link("dve", dve, dve.reciprocal(stat[0:r, 3, i:i + 1], stat[0:r, 2, i:i + 1]))
                    dve.tensor_scalar(xt[i][0:r, :], xt[i][0:r, :], stat[0:r, 3, i:i + 1], None,
                                      ALU.mult).then_inc(xs_ready, 1)
                if i == 1:
                    dve.wait_ge(consts_in, NCONST)
                    for kk in range(4):
                        dve.wait_ge(cstate_psum, 4)
                        last = dve.tensor_copy(cstate[:, kk, :], PS[:, 7, kk * 32:kk * 32 + 24])
                    link("dve", dve, last)
                    dve.wait_ge(bias_psum, 3)
                    dve.tensor_copy(F_sb.rearrange("h (a n) -> h a n", a=3), PS[0:8, 4:7, 0:384]).then_inc(bias_copied, 1)
                if i >= 1:
                    j = i - 1
                    for kk in range(2):
                        dve.wait_ge(xs_transposed, 2 * j + kk + 1)
                        src = PS[:, 2 * (j % 2) + kk, :].rearrange("p (k t) -> p k t", t=P)[:, :, 0:rows(j)]
                        if j >= 2:
                            dve.wait_ge(f_split, 2 * j - 3 + kk)
                        dve.tensor_tensor(tmpx[j % 2][kk][:, :, 0:rows(j)], src,
                                          gmix[:, 4 * kk:4 * kk + 4].unsqueeze(2).to_broadcast([P, 4, rows(j)]),
                                          ALU.mult).then_inc(f_taken, 1)
            dve.tensor_tensor(lb3[:, 1, :], lb3[:, 0, :], lb3[:, 0, :], ALU.subtract).then_inc(lb_shifted, 1)
            dve.wait_ge(lb_exp, 1)
            link("dve", dve, dve.reciprocal(lb3[:, 3, :], lb3[:, 2, :]))
            link("dve", dve, dve.tensor_tensor(lb3[:, 3, :], lb3[:, 2, :], lb3[:, 3, :], ALU.mult))
            link("dve", dve, dve.tensor_tensor(lb3[:, 4, :], lb3[:, 3, :], lb3[:, 3, :], ALU.subtract))
            link("dve", dve, dve.tensor_scalar(lb3[:, 5, :], lb3[:, 4, :], -1.0, 1.0, ALU.mult, ALU.add))

        bias_copies = sem("bias_copies")
        lb_exp, lb_shifted, bias_psum, silu_done = sem("lb_exp"), sem("lb_shifted"), sem("bias_psum"), sem("silu_done")

        def phase_a_pe(pe):
            def gates_product(g):
                pe.wait_ge(f_split, 6 * (g + 1))
                pe.wait_ge(bias_copied, 1)
                return column_tile(pe, 0, 4, (g,))

            pe.wait_ge(bias_in, 48)
            pe.wait_ge(bias_ready, 1)
            for a in range(3):
                pe.matmul(PS[0:8, 4 + a, 0:384], raug, toe_in[:, a * 384:(a + 1) * 384],
                          start=True, stop=True).then_inc(bias_psum, 1)
            for i in range(NTILE):
                r = rows(i)
                pe.wait_ge(xs_ready, i + 1)
                if i >= 2:
                    pe.wait_ge(f_taken, 2 * (i - 1))
                for k in range(KD):
                    t = pe.transpose(PS[:, 2 * (i % 2) + k // 4, (k % 4) * P:(k % 4) * P + r],
                                     xt[i][0:r, k * P:(k + 1) * P], ident[0:r, 0:r])
                    if k % 4 == 3:
                        t.then_inc(xs_transposed, 1)
                if i == 0:
                    pe.wait_ge(consts_in, NCONST)
                    for kk in range(4):
                        pe.transpose(PS[:, 7, kk * 32:kk * 32 + 24], cst_nat[:, kk * P:(kk + 1) * P],
                                     ident[0:24, 0:24]).then_inc(cstate_psum, 1)
                if i in (4, 7):
                    gates_product(i // 3 - 1)
            gates_product(2).then_inc(gate_psum, 1)

        W_CHUNKS = ([("g", None)] + [("t", c + n * P) for c in (HQ, HF, MQ, MK) for n in range(2)] +
                    [("n", c + n * P) for c in (MV, MO, HI, HG) for n in range(2)] +
                    [("t", c + n * P) for c in (AQ, AK) for n in range(4)] +
                    [("n", c + n * P) for c in (AV, AV + UW) for n in range(2)])
        NW1 = 17
        TB2, NB2 = 8, 4
        w_in = i_["w_in"][0].rearrange("(k p) n -> p k n", p=P)
        wst = [view(R_wstage, n * 1024, k=KD, n=P) for n in range(3)]

        def parts_at(m):
            if m == 0:
                r, half_ = R_wg, 0
            elif m < 9:
                r, half_ = R_wa, m % 2
            elif m < NW1:
                r, half_ = (R_wa, R_wb)[(m - 9) // 2 % 2], (m - 9) % 2
            else:
                r, half_ = R_wc[(m - NW1) // 2 % 2], (m - NW1) % 2
            return [r[:, 2048 * z + 1024 * half_:2048 * z + 1024 * half_ + 1024].rearrange("p (k n) -> p k n", k=KD)
                    for z in range(2)]

        def unit_parts(m):
            r = (R_wa, R_wb)[(m - 9) // 2 % 2] if m < NW1 else R_wc[(m - NW1) // 2 % 2]
            return [r[:, 2048 * z:2048 * (z + 1)].rearrange("p (c k n) -> p k c n", c=2, k=KD) for z in range(2)]

        def chunk_place_free(eng, m):
            if 3 <= m < 9:
                eng.wait_ge(t_psum, m - 2)
            elif m < 11 and m >= 9:
                eng.wait_ge(t_psum, TB2)
            elif m in (11, 12):
                eng.wait_ge(silu_done, 4)
            elif m in (13, 14, 15, 16):
                eng.wait_ge(n_psum, NTILE * ((m - 11) // 2))
            elif 21 <= m:
                eng.wait_ge(t_psum, TB2 + (m - 20 if m < 25 else 6 if m < 27 else 8))

        def w_high_part(act, m):
            if m:
                act.wait_ge(w_in_ready[m % 3], 16 * ((m + 2) // 3))
            else:
                act.wait_ge(wgate_in, 32)
            chunk_place_free(act, m)
            act.activation(parts_at(m)[0], wst[m % 3], ACT.Copy).then_inc(chunk_high, 1)

        def w_low_parts(pool, first, last):
            for m in range(first, last):
                pool.wait_ge(chunk_high, m + 1)
                pool.tensor_tensor(parts_at(m)[1], wst[m % 3], parts_at(m)[0].bitcast(F32), ALU.subtract)\
                    .then_inc(chunk_split, 1)

        def load_w(sp, first, last):
            for m in range(first, last):
                if m >= 3:
                    sp.wait_ge(chunk_split, m - 2)
                kind, col = W_CHUNKS[m]
                sp.dma_start(wst[m % 3], w_in[:, :, col:col + P]).then_inc(w_in_ready[m % 3], 16)

        CW = 3 + S + 7 * NB
        cst = [R_conv[:, n * 1083:n * 1083 + CW] for n in range(2)]
        scr = [R_conv[:, 2166 + n * NTOK:2166 + (n + 1) * NTOK] for n in range(2)]
        gs = [R_gs[n // 4][0:4, n % 4 * NTOK:(n % 4 + 1) * NTOK] for n in range(7)]
        gr = R_gs[1][:, 3 * NTOK:4 * NTOK]
        tailnat = R_hi[0:27, 0:512]

        def three(ap):
            return ap.rearrange("p (a t) -> p a t", a=3)

        def prompt(ap):
            return ap[:, 0:S].rearrange("p (c t) -> p c t", t=P)

        def sample(ap):
            return ap[:, S:NTOK].rearrange("p (b t) -> p b t", t=NT)

        def first_w(sp):
            sp.wait_ge(wgate_zero, 1)
            for col, at in ((MI, 0), (MF, 32)):
                sp.dma_start(wst[0][:, :, at:at + 4], w_in[:, :, col:col + 4],
                             allow_slow_non_contiguous=True).then_inc(wgate_in, 16)
            load_w(sp, 1, 3)

        def phase_b1_sync(sp):
            load_w(sp, 3, 9)
            sp.wait_ge(gate_args, 1)
            sp.dma_start(o_["p_m"][0].rearrange("b h -> h b"), gs[6][:, S - 1:S],
                         allow_slow_non_contiguous=True).then_inc(gate_stored, 16)
            sp.dma_start(o_["s_m"][0].rearrange("b h -> h b"), gs[6][:, S + 3::NT],
                         allow_slow_non_contiguous=True).then_inc(gate_stored, 16)
            load_w(sp, 9, 13)
            sp.wait_ge(tail_copied, 1)
            sp.dma_start(o_["p_conv"][0, 0], tailnat[0:3, :]).then_inc(gate_stored, 16)
            sp.dma_start(o_["s_conv"][0].rearrange("b j n -> (b j) n"), tailnat[3:27, :]).then_inc(gate_stored, 16)
            load_w(sp, 13, NW1)
            sp.wait_ge(gate_stored, 64)

        def phase_b2_sync(sp):
            load_w(sp, NW1 + 3, len(W_CHUNKS))
            for i in range(NTILE):
                sp.wait_ge(k_taken, i + 1)
                sp.dma_start(by_token("k", i), kstage[i % 2][0:rows(i), :].rearrange("p (h e) -> p h e", e=E))\
                  .then_inc(k_stored[i % 2], 16)
            sp.wait_ge(k_stored[0], 16 * 5)
            sp.wait_ge(k_stored[1], 16 * 4)

        gate_stored = sem("gate_stored")
        k_psum, k_taken, k_stored = sem("k_psum"), sem("k_taken"), [sem(f"k_stored{n}") for n in range(2)]
        kstage = [R_kstage[:, n * 512:(n + 1) * 512] for n in range(2)]

        def by_token(what, i):
            if i < NCH:
                return o_["p_" + what][0, 0, i * P:(i + 1) * P]
            return o_["s_" + what][0].rearrange("b t h e -> (b t) h e")

        def phase_b1_gps(pool):
            pool.dma_start(frep, fdr.unsqueeze(1).to_broadcast([H, P, FW])).then_inc(bias_copies, 16)
            w_low_parts(pool, 3, NW1)

        def phase_b2_gps(pool):
            w_low_parts(pool, NW1, len(W_CHUNKS))

        def tile_taken(eng, tj):
            if tj < 2:
                eng.wait_ge(h_done, tj + 1)
            elif tj < 4:
                eng.wait_ge(sig_ready, tj + 1)
            else:
                eng.wait_ge(t_taken, tj - 3)

        def tile_banks(tj):
            return 3 * (tj % 2)

        def column_tile(pe, m, bank, groups_=(0, 1, 2)):
            pe.wait_ge(chunk_split, m + 1)
            wh, wl = parts_at(m)
            for g in groups_:
                ts = slice(g * TG, (g + 1) * TG)
                mm = product(pe, PS[:, bank + g, 0:TG], lambda k: (wh[:, k, :], wl[:, k, :]),
                             lambda k: (XNH[:, k, ts], XNL[:, k, ts]), KD)
            return mm

        def natural_tile(pe, m, i, q):
            if q >= 2:
                pe.wait_ge(n_taken, q - 1)
            wh, wl = unit_parts(m)
            ts = last_tokens(i)
            product(pe, PS[:, 6 + q % 2, 0:UW].rearrange("p (c n) -> p c n", c=2),
                    lambda k: (XNH[:, k, ts], XNL[:, k, ts]), lambda k: (wh[:, k], wl[:, k]), KD).then_inc(n_psum, 1)

        def phase_b1_pe(pe):
            for tj in range(TB2):
                if tj == 1:
                    pe.wait_ge(gate_taken, 1)
                if tj >= 2:
                    tile_taken(pe, tj - 2)
                column_tile(pe, 1 + tj, tile_banks(tj)).then_inc(t_psum, 1)
                if tj == 3:
                    pe.wait_ge(gate_rows, 4)
                    for c in range(NTILE):
                        r = rows(c)
                        pe.transpose(PS[0:r, 6, (c % 4) * P:(c % 4 + 1) * P], gr[:, tile_tokens(c)], ident[:, :])\
                            .then_inc(gate_cols, 1)
                        if c % 4 == 3 or c == NTILE - 1:
                            pe.wait_ge(gcol_ready, c // 4 + 1)
                    pe.wait_ge(gate_last, 1)
                    for pr in range(2):
                        mm = pe.matmul(PS[:, 7, pr * 16:(pr + 1) * 16], selv[:, HM + pr, :], egl[:, :],
                                       start=True, stop=True)
                    mm.then_inc(glc_psum, 1)
            for nu in range(NB2):
                m = 9 + 2 * nu
                if nu == 1:
                    pe.wait_ge(conv_done, 4)
                    for kk in range(4):
                        t = pe.transpose(PS[0:27, 0, kk * P:(kk + 1) * P], ctail[:, kk, :], ident[:, :])
                    t.then_inc(tail_psum, 1)
                pe.wait_ge(chunk_split, m + 2)
                for i in range(NTILE):
                    natural_tile(pe, m, i, nu * NTILE + i)

        def phase_b2_pe(pe):
            for tj in range(TB2, 2 * TB2):
                if tj >= TB2 + 2:
                    tile_taken(pe, tj - 2)
                column_tile(pe, NW1 + tj - TB2, tile_banks(tj)).then_inc(t_psum, 1)
            pe.wait_ge(t_taken, 12)
            for nu in range(NB2, NB2 + 2):
                m = NW1 + TB2 + 2 * (nu - NB2)
                pe.wait_ge(chunk_split, m + 2)
                for i in range(NTILE):
                    natural_tile(pe, m, i, nu * NTILE + i)
                    if nu == NB2:
                        if i >= 2:
                            pe.wait_ge(k_taken, i - 1)
                        for k in range(4):
                            t = pe.transpose(PS[0:rows(i), i % 2, k * P:(k + 1) * P], aqk[:, 4 + k, tile_tokens(i)],
                                             ident[:, :])
                        t.then_inc(k_psum, 1)

        def natural_out(act, q):
            act.wait_ge(n_psum, q + 1)
            return PS[0:P, 6 + q % 2, 0:UW] if q % NTILE < NCH else PS[P - NS:P, 6 + q % 2, 0:UW]

        def phase_b1_act(act):
            act.wait_ge(gate_abs, 1)
            link("act", act, act.activation(gs[2], gs[2], ACT.Exp, scale=-1.0))
            act.activation(gs[2], gs[2], ACT.Ln, bias=1.0).then_inc(gate_soft, 1)
            for tj in range(TB2):
                bank = tile_banks(tj)
                src = PS[:, bank:bank + 3, 0:TG]
                act.wait_ge(t_psum, tj + 1)
                if tj < 4:
                    if tj >= 2:
                        act.wait_ge(h_done, tj - 1)
                    act.activation(three(scr[tj % 2]), src, ACT.Sigmoid).then_inc(sig_ready, 1)
                else:
                    n = tj - 4
                    c = cst[n % 2]
                    if n >= 2:
                        act.wait_ge(conv_done, n - 1)
                    c2 = c[:, 3 + S:].rearrange("p (b j) -> p b j", j=7)
                    act.activation(c[:, 3:3 + 2 * TG].rearrange("p (a t) -> p a t", a=2),
                                   PS[:, bank:bank + 2, 0:TG], ACT.Copy).then_inc(conv_in, 1)
                    act.activation(c[:, 3 + 2 * TG:3 + S], PS[:, bank + 2, 0:S - 2 * TG], ACT.Copy).then_inc(conv_in, 1)
                    act.activation(c2[:, :, 0:3], cstate[:, n, :].rearrange("p (b j) -> p b j", j=3), ACT.Copy)\
                        .then_inc(conv_in, 1)
                    act.activation(c2[:, :, 3:7], PS[:, bank + 2, S - 2 * TG:TG].rearrange("p (b j) -> p b j", j=4),
                                   ACT.Copy).then_inc(t_taken, 1)
                if tj + 3 < 9:
                    w_high_part(act, tj + 3)
                if tj == 7:
                    w_high_part(act, 9)
                    w_high_part(act, 10)
                if tj == 0:
                    act.wait_ge(gate_args, 1)
                    act.activation(gr[0:4, :], gs[3], ACT.Exp).then_inc(gate_rows, 1)
                    act.activation(gr[32:36, :], gs[6], ACT.Exp, scale=-1.0).then_inc(gate_rows, 1)
                    act.activation(gr[64:68, :], gs[4], ACT.Exp).then_inc(gate_rows, 1)
                    act.activation(gr[96:100, :], gs[1], ACT.Copy).then_inc(gate_rows, 1)
                if tj >= 5:
                    conv_sigmoid(act, tj - 5)
            conv_sigmoid(act, 3)
            act.wait_ge(gate_stored, 32)
            act.wait_ge(gcol_ready, 3)
            for nu in range(NB2):
                for i in range(NTILE):
                    q = nu * NTILE + i
                    r = rows(i)
                    src = natural_out(act, q)
                    if nu == 0:
                        act.activation(vm[0:r, i, :, 0:E], src.rearrange("p (h e) -> p h e", e=E), ACT.Copy)\
                            .then_inc(n_taken, 1)
                    elif nu in (1, 3):
                        act.activation((mo if nu == 1 else hg)[0:r, i, :], src, ACT.Sigmoid).then_inc(n_taken, 1)
                    else:
                        if i == 0:
                            act.wait_ge(gate_stored, 64)
                        act.activation(hi[0:r, i, :], src, ACT.Copy).then_inc(n_taken, 1)
                    if i == 1 and nu + 1 < NB2:
                        w_high_part(act, 11 + 2 * nu)
                        w_high_part(act, 12 + 2 * nu)
                if nu == 0:
                    act.wait_ge(f_ready, 2)
                    for p in range(2):
                        act.activation(hb[:, p, :], hb[:, p, :], ACT.Ln).then_inc(lnf_ready, 1)

        def phase_b2_act(act):
            for m in range(NW1, NW1 + 4):
                w_high_part(act, m)
            for k in range(8):
                bank = tile_banks(TB2 + k)
                act.wait_ge(t_psum, TB2 + k + 1)
                act.activation(three(aqk[:, k, :]), PS[:, bank:bank + 3, 0:TG], ACT.Copy, scale=0.125 if k < 4 else 1.0)\
                    .then_inc(t_taken, 1)
                if k < 4:
                    w_high_part(act, NW1 + 4 + k)
                elif k in (5, 7):
                    w_high_part(act, NW1 + 3 + k)
                    w_high_part(act, NW1 + 4 + k)
            for nu in range(2):
                for i in range(NTILE):
                    q = (NB2 + nu) * NTILE + i
                    r = rows(i)
                    act.activation(va[0:r, i, 4 * nu:4 * nu + 4, 0:E],
                                   natural_out(act, q).rearrange("p (h e) -> p h e", e=E), ACT.Copy).then_inc(n_taken, 1)
                    if nu == 0:
                        act.wait_ge(k_psum, i + 1)
                        if i >= 2:
                            act.wait_ge(k_stored[i % 2], 16 * (i // 2))
                        act.activation(kstage[i % 2][0:r, :], PS[0:r, i % 2, :], ACT.Copy).then_inc(k_taken, 1)

        def conv_sigmoid(act, n):
            act.wait_ge(conv_done, n + 1)
            if n >= 2:
                act.wait_ge(silu_done, n - 1)
            else:
                act.wait_ge(h_done, 4)
            act.activation(scr[n % 2], mqk[:, n, :], ACT.Sigmoid).then_inc(sig_ready, 1)

        def phase_b1_dve(dve):
            dve.wait_ge(gate_psum, 1)
            link("dve", dve, dve.tensor_scalar(three(gs[0]), PS[0:4, 4:7, 0:TG], gateb[0:4, :], None, ALU.add))
            link("dve", dve, dve.tensor_scalar(three(gs[1]), PS[32:36, 4:7, 0:TG], gateb[32:36, :], None, ALU.add))
            dve.nop().then_inc(gate_taken, 1)
            dve.scalar_tensor_tensor(gs[2], gs[1], -1.0, gs[1], ALU.mult, ALU.max).then_inc(gate_abs, 1)
            link("dve", dve, dve.tensor_scalar(gs[1], gs[1], 0.0, None, ALU.min))
            link("dve", dve, dve.memset(gr[:, :], 0.0))
            dve.wait_ge(gate_soft, 1)
            link("dve", dve, dve.tensor_tensor(gs[3], gs[1], gs[2], ALU.subtract))
            link("dve", dve, dve.tensor_tensor_scan(gs[4], seg[0:4, :], gs[3], 0.0, ALU.mult, ALU.add))
            link("dve", dve, dve.tensor_tensor(small[0:4, 0:NB], gs[3][:, S::NT], m0[:, :], ALU.add))
            link("dve", dve, dve.tensor_copy(gs[5], gs[0]))
            link("dve", dve, dve.tensor_tensor(gs[5][:, S::NT], small[0:4, 0:NB], gs[0][:, S::NT], ALU.max))
            link("dve", dve, dve.memset(gs[3][:, S::NT], NEG))
            link("dve", dve, dve.tensor_tensor_scan(gs[6], gs[3], gs[5], 0.0, ALU.add, ALU.max))
            link("dve", dve, dve.tensor_tensor(bm[:, :], gs[4], gs[6], ALU.subtract))
            link("dve", dve, dve.tensor_tensor(gs[1], gs[0], gs[4], ALU.subtract))
            dve.tensor_copy(gs[3][:, 0:P], bm[:, 0:P])
            prev = gs[6][:, P - 1:S - 1:P].unsqueeze(2).to_broadcast([HM, NCH - 1, P])
            dve.tensor_tensor(prompt(gs[3])[:, 1:], prompt(bm[:, :])[:, 1:], prev, ALU.add)
            dve.tensor_tensor(sample(gs[3]), sample(bm[:, :]), m0[:, :].unsqueeze(2).to_broadcast([HM, NB, NT]), ALU.add)
            dve.tensor_tensor(prompt(gs[4]), prompt(gs[1]),
                              bm[:, P - 1:S:P].unsqueeze(2).to_broadcast([HM, NCH, P]), ALU.add)
            dve.tensor_tensor(sample(gs[4]), sample(gs[1]),
                              bm[:, S + NT - 1::NT].unsqueeze(2).to_broadcast([HM, NB, NT]), ALU.add).then_inc(gate_args, 1)
            dve.wait_ge(gate_rows, 4)
            link("dve", dve, dve.tensor_copy(egl[:, 0:8], gr[0:4, P - 1:S:P]))
            link("dve", dve, dve.tensor_copy(egl[:, 8:16], gr[0:4, S + NT - 1::NT]))
            dve.nop().then_inc(gate_last, 1)
            for tj in range(8):
                if tj == 4:
                    for c4 in range(3):
                        n = 4 if c4 < 2 else 1
                        r = rows(4 * c4)
                        dve.wait_ge(gate_cols, 4 * c4 + n)
                        dve.tensor_copy(gcol[0:r, 4 * c4:4 * c4 + n, :],
                                        PS[0:r, 6, 0:n * P].rearrange("p (c t) -> p c t", t=P)).then_inc(gcol_ready, 1)
                    dve.wait_ge(glc_psum, 1)
                    link("dve", dve, dve.tensor_copy(glc[:, :, :], PS[:, 7, 0:32].rearrange("p (a n) -> p a n", a=2)))
                kind, p = tj // 2, tj % 2
                bank = tile_banks(tj)
                src = PS[:, bank:bank + 3, 0:TG]
                if kind == 0:
                    dve.wait_ge(sig_ready, tj + 1)
                    dve.tensor_tensor(three(hqk[:, p, :]), src, three(scr[tj % 2]), ALU.mult).then_inc(h_done, 1)
                elif kind == 1:
                    dve.wait_ge(sig_ready, tj + 1)
                    dve.tensor_scalar(hb[:, p, :], scr[tj % 2], lb3[:, 5, p:p + 1], lb3[:, 4, p:p + 1],
                                      ALU.mult, ALU.add).then_inc(f_ready, 1)
                    dve.wait_ge(f_ready, p + 1)
                    dve.tensor_scalar(hqk[:, 2 + p, :], hb[:, p, :], -1.0, 1.0, ALU.mult, ALU.add).then_inc(h_done, 1)
                else:
                    n = tj - 4
                    c = cst[n % 2]
                    if n < 2:
                        link("dve", dve, dve.memset(c[:, 0:3], 0.0))
                    dve.wait_ge(conv_in, 3 * n + 3)
                    dve.wait_ge(t_taken, n + 1)
                    dst = mqk[:, n, :]
                    c2 = c[:, 3 + S:].rearrange("p (b j) -> p b j", j=7)
                    for j in range(4):
                        w = convw[:, n, j:j + 1]
                        for out, src in ((dst[:, 0:S], c[:, j:j + S]), (sample(dst), c2[:, :, j:j + NT])):
                            if j == 0:
                                ins = dve.tensor_scalar(out, src, w, None, ALU.mult)
                            else:
                                ins = dve.scalar_tensor_tensor(out, src, w, out, ALU.mult, ALU.add)
                        link("dve", dve, ins)
                    dve.tensor_copy(ctail[:, n, 0:3], c[:, S:S + 3])
                    dve.tensor_copy(ctail[:, n, 3:27].rearrange("p (b j) -> p b j", j=3), c2[:, :, 4:7])\
                        .then_inc(conv_done, 1)
                    if n >= 1:
                        conv_silu(dve, n - 1)
                    if n == 3:
                        conv_silu(dve, 3)
            dve.wait_ge(tail_psum, 1)
            dve.tensor_copy(tailnat[:, :], PS[0:27, 0, :]).then_inc(tail_copied, 1)
            dve.memset(vm[:, :, :, E:E + 1], 1.0)
            for p in range(2):
                dve.wait_ge(lnf_ready, p + 1)
                link("dve", dve, dve.tensor_tensor_scan(hb[:, p, :], seg[:, :], hb[:, p, :], 0.0, ALU.mult, ALU.add))

        def phase_b2_dve(dve):
            dve.memset(va[:, :, :, E:E + 1], 1.0)

        def conv_silu(dve, n):
            dve.wait_ge(sig_ready, 4 + n + 1)
            dve.scalar_tensor_tensor(mqk[:, n, :], mqk[:, n, :], 1.0 if n < 2 else 0.125, scr[n % 2],
                                     ALU.mult, ALU.mult).then_inc(silu_done, 1)

        G = [R_att[:, n * S:(n + 1) * S] for n in range(2)]
        PB = [R_att[:, 2 * S:3 * S], R_att[:, 3 * S:4 * S], R_pb3]
        PT = [view(R_att, (4 + n) * S, k=NCH, q=P) for n in range(2)]
        g_in = [sem(f"g_in{n}") for n in range(2)]
        s_psum, biased, exped = sem("s_psum"), sem("biased"), sem("exped")
        pT_psum = sem("pT_psum")
        pT_taken = [sem("pT_taken_act"), sem("pT_taken_dve")]
        o_psum, o_taken, v_stored, p_scaled = sem("o_psum"), sem("o_taken"), sem("v_stored"), sem("p_scaled")
        negm = sb("negm", [P, 3])
        psum_ = sb("psum_of_exp", [P, 3])
        rl = sb("rl", [P, 3])
        STEPS = [(h, i) for h in range(H) for i in range(NCH)]
        groups, gsum = [], [0]
        for n_, (h_, i_n) in enumerate(STEPS):
            groups.append([(k0, min(i_n + 1, k0 + 4)) for k0 in range(0, i_n + 1, 4)])
            gsum.append(gsum[-1] + len(groups[-1]))

        def taken_through(eng, gid):
            if (gid + 1) // 2:
                eng.wait_ge(pT_taken[0], (gid + 1) // 2)
            if gid // 2:
                eng.wait_ge(pT_taken[1], gid // 2)

        def phase_c_sync(sp):
            sp.wait_ge(bias_copies, 16)
            for h in range(H):
                if h >= 2:
                    sp.wait_ge(biased, NCH * (h - 1))
                src = bass.AP(frep.tensor, h * P * FW + P - 1, [[FW - 1, P], [1, S]])
                sp.dma_start(G[h % 2], src).then_inc(g_in[h % 2], 16)
                if h == 1:
                    load_caches(sp, 0, NAHEAD)
                    for i in range(NTILE):
                        sp.dma_start(by_token("v", i), va[0:rows(i), i, :, 0:E]).then_inc(v_stored, 16)
            sp.wait_ge(v_stored, 16 * NTILE)

        def phase_c_pe(pe):
            for n in range(len(STEPS) + 3):
                if n < len(STEPS):
                    h, i = STEPS[n]
                    if n >= 2:
                        pe.wait_ge(biased, n - 1)
                    part = slice(64 * (h % 2), 64 * (h % 2) + 64)
                    nk = (i + 1) * P
                    for c in range(0, nk, 512):
                        mm = pe.matmul(PS[:, 2 * (n % 2) + c // 512, 0:min(512, nk - c)],
                                       aqk[part, h // 2, i * P:(i + 1) * P], aqk[part, 4 + h // 2, c:min(c + 512, nk)],
                                       start=True, stop=True)
                    mm.then_inc(s_psum, 1)
                if 2 <= n <= len(STEPS) + 1:
                    m = n - 2
                    pe.wait_ge(p_scaled, m + 1)
                    for j, (k0, k1) in enumerate(groups[m]):
                        gid = gsum[m] + j
                        if gid >= 2:
                            taken_through(pe, gid - 1)
                        for k in range(k0, k1):
                            t = pe.transpose(PS[:, 4 + gid % 2, (k - k0) * P:(k - k0 + 1) * P],
                                             PB[m % 3][:, k * P:(k + 1) * P], ident[:, :])
                        t.then_inc(pT_psum, 1)
                if n >= 3:
                    m = n - 3
                    h, i = STEPS[m]
                    taken_through(pe, gsum[m + 1])
                    if m >= 2:
                        pe.wait_ge(o_taken, m - 1)
                    for k in range(i + 1):
                        mm = pe.matmul(PS[0:E, 6 + m % 2, 0:P], va[:, k, h, 0:E], PT[m % 2][:, k, :],
                                       start=(k == 0), stop=(k == i))
                    mm.then_inc(o_psum, 1)

        def copy_groups(eng, copy, m, parity):
            for j, (k0, k1) in enumerate(groups[m]):
                gid = gsum[m] + j
                if gid % 2 == parity:
                    eng.wait_ge(pT_psum, gid + 1)
                    if m >= 2:
                        eng.wait_ge(o_psum, m - 1)
                    copy(PT[m % 2][:, k0:k1, :],
                         PS[:, 4 + gid % 2, 0:(k1 - k0) * P].rearrange("p (k q) -> p k q", q=P))\
                        .then_inc(pT_taken[parity], 1)

        def phase_c_act(act):
            for n in range(len(STEPS) + 3):
                if n < len(STEPS):
                    h, i = STEPS[n]
                    nk = (i + 1) * P
                    act.wait_ge(biased, n + 1)
                    act.activation(PB[n % 3][:, 0:nk], PB[n % 3][:, 0:nk], ACT.Exp, bias=negm[:, n % 3:n % 3 + 1],
                                   scale=-1.0, accum_out=psum_[:, n % 3:n % 3 + 1]).then_inc(exped, 1)
                if 2 <= n <= len(STEPS) + 1:
                    copy_groups(act, lambda o, s: act.activation(o, s, ACT.Copy), n - 2, 0)
                if n >= 3:
                    m = n - 3
                    h, i = STEPS[m]
                    act.wait_ge(o_psum, m + 1)
                    act.activation(mixa[64 * (h % 2):64 * (h % 2) + 64, h // 2, i * P:(i + 1) * P],
                                   PS[0:E, 6 + m % 2, 0:P], ACT.Copy).then_inc(o_taken, 1)

        def phase_c_dve(dve):
            for n in range(len(STEPS) + 2):
                if n < len(STEPS):
                    h, i = STEPS[n]
                    nk = (i + 1) * P
                    if i == 0:
                        dve.wait_ge(g_in[h % 2], 16 * (h // 2 + 1))
                    if n >= 3:
                        dve.wait_ge(pT_psum, gsum[n - 2])
                    dve.wait_ge(s_psum, n + 1)
                    scores = PS[:, 2 * (n % 2):2 * (n % 2) + 2, :].rearrange("p a n -> p (a n)")[:, 0:nk]
                    dve.tensor_tensor_reduce(PB[n % 3][:, 0:nk], scores, G[h % 2][:, S - nk:S], -1.0, 3e38,
                                             ALU.add, ALU.min, negm[:, n % 3:n % 3 + 1]).then_inc(biased, 1)
                if 1 <= n <= len(STEPS):
                    m = n - 1
                    nk = (STEPS[m][1] + 1) * P
                    dve.wait_ge(exped, m + 1)
                    link("dve", dve, dve.reciprocal(rl[:, m % 3:m % 3 + 1], psum_[:, m % 3:m % 3 + 1]))
                    dve.tensor_scalar(PB[m % 3][:, 0:nk], PB[m % 3][:, 0:nk], rl[:, m % 3:m % 3 + 1], None,
                                      ALU.mult).then_inc(p_scaled, 1)
                if n >= 2:
                    copy_groups(dve, dve.tensor_copy, n - 2, 1)
            link("dve", dve, dve.memset(qblk[:, :, :, :, :], 0.0))
            for hp in range(4):
                for h2 in range(2):
                    pt = slice(64 * h2, 64 * h2 + 64)
                    ins = dve.tensor_copy(qblk[pt, hp, :, 2 * hp + h2, :], sample(aqk[pt, hp, :]))
            link("dve", dve, ins)
            link("dve", dve, dve.tensor_copy(knew[:, :, :], aqk[:, 4:8, S:NTOK]))
            link("dve", dve, dve.tensor_copy(vnew[0:NS, :].rearrange("p (h e) -> p h e", e=E), va[0:NS, 8, :, 0:E]))

        qblk = R_att[:, 0:1024].rearrange("p (hp b h t) -> p hp b h t", hp=4, b=NB, h=H)
        knew = R_att[:, 1024:1152].rearrange("p (k t) -> p k t", k=4)
        vnew = R_att[:, 1152:1664]

        A_ = R_d
        Dm = [view(A_, n * 512, h=HM, t=P) for n in range(2)]
        Wm = [view(A_, 1024 + n * 512, h=HM, t=P) for n in range(2)]
        kd = [view(A_, 2048 + n * 256, h=HM, e=E) for n in range(2)]
        tmpN = view(A_, 2560, h=HM, e=E + 1)
        nd = view(A_, 2820, h=HM, e=E + 1)
        hh = view(A_, 3080, h=HM, e=E)
        sq = view(A_, 3336, h=HM, e=E)
        Cst = view(A_, 3592, a=2, e=E + 1)
        Css = view(A_, 3722, b=NB, a=2, e=E + 1)
        qm_flat = [A_[:, 4762 + n * 288:4762 + (n + 1) * 288] for n in range(2)]
        kdm = view(A_, 5338, b=NB, h=HM, e=E)
        cmask = A_[:, 7386:7386 + P + NS]
        bmask = A_[0:NS, 7546:7554]
        tmpC = view(A_, 7554, b=NB, e=E + 1)
        hstat = sb("hstat", [P, 2, NTILE, HM])
        hrstd = sb("hrstd", [P, 2, NTILE, HM])
        adn = sb("adn", [P, HM])
        d_in, d_zero = sem("d_in"), sem("d_zero")
        g1, g2 = sem("mlstm_scores"), sem("mlstm_sums")
        m_biased, m_exp, m_w, m_kd = sem("m_biased"), sem("m_exp"), sem("m_w"), sem("m_kd")
        m_state, m_taken, m_masked, m_upd, m_updt = (sem("m_state"), sem("m_taken"), sem("m_masked"), sem("m_upd"),
                                                     sem("m_updt"))
        st_out = sem("state_stored")

        def masked_q(flat):
            return (flat[:, 0:256].rearrange("p (b t) -> p b t", b=NB),
                    flat.rearrange("p (b s) -> p b s", s=36)[:, :, 0:NT])

        def halves():
            return [(a, h2, slice(64 * h2, 64 * h2 + 64)) for a in range(2) for h2 in range(2)]

        def phase_d1_sync(sp):
            sp.dma_start(cmask, const("c_causal")).then_inc(d_in, 16)
            sp.dma_start(bmask, const("c_batch")).then_inc(d_in, 16)
            for a, h2, pt in halves():
                sp.dma_start(Css[pt, :, a, 0:E], i_["state_mlstm_C"][0, :, 2 * a + h2].rearrange("b k v -> k b v"))\
                  .then_inc(d_in, 16)
                sp.dma_start(Css[pt, :, a, E:E + 1], i_["state_mlstm_n"][0, :, 2 * a + h2:2 * a + h2 + 1].rearrange(
                    "b o k -> k b o"), allow_slow_non_contiguous=True).then_inc(d_in, 16)
            sp.wait_ge(m_state, NCH)
            for a, h2, pt in halves():
                h = 2 * a + h2
                sp.dma_start(o_["p_C"][0, 0, h], Cst[pt, a, 0:E]).then_inc(st_out, 16)
                sp.dma_start(o_["p_n"][0, 0, h:h + 1].rearrange("o k -> k o"), Cst[pt, a, E:E + 1],
                             allow_slow_non_contiguous=True).then_inc(st_out, 16)
            sp.wait_ge(m_upd, 4)
            for a, h2, pt in halves():
                h = 2 * a + h2
                sp.dma_start(o_["s_C"][0, :, h].rearrange("b k v -> k b v"), Css[pt, :, a, 0:E]).then_inc(st_out, 16)
                sp.dma_start(o_["s_n"][0, :, h:h + 1].rearrange("b o k -> k b o"), Css[pt, :, a, E:E + 1],
                             allow_slow_non_contiguous=True).then_inc(st_out, 16)

        def phase_d1_pe(pe):
            def scores(c):
                r, tt = rows(c), tile_tokens(c)
                if c >= 2:
                    pe.wait_ge(m_w, c - 1)
                    pe.wait_ge(m_kd, c - 1)
                for h in (0, 2, 1, 3):
                    pt = slice(64 * (h % 2), 64 * (h % 2) + 64)
                    mm = pe.matmul(PS[0:r, c % 2, h * P:h * P + r], mqk[pt, 2 + h // 2, tt], mqk[pt, h // 2, tt],
                                   start=True, stop=True)
                    if h == 2:
                        link("pe", pe, mm)
                if c:
                    pe.wait_ge(m_biased, c)
                for h in range(HM):
                    pe.matmul(PS[0:r, 2, h * P:h * P + r], selv[:, h, 0:r], bm[:, tt], start=True, stop=True)
                for a in range(2):
                    t = pe.transpose(PS[0:r, 3 + c % 2, a * P:(a + 1) * P], mqk[:, 2 + a, tt], ident[:, :])
                t.then_inc(g1, 1)

            def sums(c):
                r, tt = rows(c), tile_tokens(c)
                pe.wait_ge(m_kd, c + 1)
                pe.wait_ge(m_w, c + 1)
                pe.wait_ge(d_zero, 1)
                if c >= 1:
                    pe.wait_ge(m_state, c)
                    pe.wait_ge(m_taken, c)
                if c == NCH:
                    pe.wait_ge(m_masked, 1)
                for h in (0, 2, 1, 3):
                    pt = slice(64 * (h % 2), 64 * (h % 2) + 64)
                    o = PS[0:r, 5, h * (E + 1):(h + 1) * (E + 1)]
                    if c < NCH:
                        mm = pe.matmul(o, mqk[pt, h // 2, tt], Cst[pt, h // 2, :], start=True, stop=True)
                    else:
                        for b in range(NB):
                            mm = pe.matmul(o, masked_q(qm_flat[h // 2])[0][pt, b, :], Css[pt, b, h // 2, :],
                                           start=(b == 0), stop=(b == NB - 1))
                    if h == 2:
                        link("pe", pe, mm)
                for h in range(HM):
                    mm = pe.matmul(PS[0:r, 6, h * (E + 1):(h + 1) * (E + 1)], Wm[c % 2][0:r, h, 0:r], vm[0:r, c, h, :],
                                   start=True, stop=True)
                if c < NCH:
                    for a in range(2):
                        mm = pe.matmul(PS[:, 7, a * 130:(a + 1) * 130],
                                       kd[c % 2][0:r, 2 * a:2 * a + 2, :].rearrange("p h e -> p (h e)"),
                                       vm[0:r, c, 2 * a:2 * a + 2, :].rearrange("p h e -> p (h e)"), start=True, stop=True)
                mm.then_inc(g2, 1)

            pe.wait_ge(d_in, 160)
            scores(0)
            scores(1)
            for c in range(NTILE):
                sums(c)
                if c + 2 < NTILE:
                    scores(c + 2)
            for a in range(2):
                if a:
                    pe.wait_ge(m_upd, 2)
                for b in range(NB):
                    mm = pe.matmul(PS[:, b // 2, (b % 2) * 130:(b % 2 + 1) * 130],
                                   kdm[0:NS, b, 2 * a:2 * a + 2, :].rearrange("p h e -> p (h e)"),
                                   vm[0:NS, NCH, 2 * a:2 * a + 2, :].rearrange("p h e -> p (h e)"), start=True, stop=True)
                mm.then_inc(m_updt, 1)

        def phase_d1_act(act):
            for c in range(NTILE):
                r = rows(c)
                act.wait_ge(m_biased, c + 1)
                for h in range(HM):
                    e = act.activation(Dm[c % 2][0:r, h, 0:r], Dm[c % 2][0:r, h, 0:r], ACT.Exp,
                                       bias=gcol[0:r, c, 96 + h:97 + h])
                e.then_inc(m_exp, 1)
            decays(act, 0)

        def phase_d1_dve(dve):
            def biased_(c):
                r = rows(c)
                dve.wait_ge(g1, c + 1)
                m = cmask[0:r, 0:P] if c < NCH else cmask[0:r, P:P + NS]
                dve.tensor_tensor(Dm[c % 2][0:r, :, 0:r],
                                  PS[0:r, 2, :].rearrange("p (h t) -> p h t", t=P)[:, :, 0:r],
                                  m.unsqueeze(1).to_broadcast([r, HM, r]), ALU.add).then_inc(m_biased, 1)

            def col(c, at, n):
                return gcol[0:rows(c), c, at:at + HM].unsqueeze(2).to_broadcast([rows(c), HM, n])

            dve.wait_ge(d_in, 160)
            dve.memset(Cst[:, :, :], 0.0).then_inc(d_zero, 1)
            for a in range(2):
                link("dve", dve, dve.memset(qm_flat[a], 0.0))
                dve.tensor_copy(masked_q(qm_flat[a])[1], sample(mqk[:, a, :]))

            def weighted(c):
                r = rows(c)
                dve.wait_ge(m_exp, c + 1)
                dve.tensor_tensor(Wm[c % 2][0:r, :, 0:r], Dm[c % 2][0:r, :, 0:r],
                                  PS[0:r, c % 2, :].rearrange("p (h t) -> p h t", t=P)[:, :, 0:r], ALU.mult)\
                   .then_inc(m_w, 1)
                if c == NCH:
                    dve.wait_ge(m_kd, c + 1)
                    for h in range(HM):
                        ins = dve.tensor_tensor(kdm[0:NS, :, h, :], kd[c % 2][0:NS, h, :].unsqueeze(1).to_broadcast([NS, NB, E]),
                                                bmask.unsqueeze(2).to_broadcast([NS, NB, E]), ALU.mult)
                    ins.then_inc(m_masked, 1)

            def keys_and_bias(c):
                r = rows(c)
                dve.wait_ge(g1, c + 1)
                if c >= 2:
                    dve.wait_ge(g2, c - 1)
                dve.tensor_tensor(kd[c % 2][0:r], PS[0:r, 3 + c % 2, 0:256].rearrange("p (h e) -> p h e", e=E),
                                  col(c, 64, E), ALU.mult).then_inc(m_kd, 1)
                biased_(c)

            def update(a):
                dve.wait_ge(m_updt, a + 1)
                for h2 in range(2):
                    pt = slice(64 * h2, 64 * h2 + 64)
                    link("dve", dve, dve.tensor_tensor(tmpC[pt], Css[pt, :, a, :],
                                                       glc[pt, a, 8:16].unsqueeze(2).to_broadcast([64, NB, E + 1]), ALU.mult))
                    upd = PS[pt, 0:4, 0:260].rearrange("p a (b e) -> p a b e", b=2)[:, :, :, h2 * 65:h2 * 65 + 65]
                    dve.tensor_tensor(Css[pt, :, a, :].rearrange("p (x y) e -> p x y e", y=2),
                                      tmpC[pt].rearrange("p (x y) e -> p x y e", y=2), upd, ALU.add).then_inc(m_upd, 1)

            keys_and_bias(0)
            weighted(0)
            for c in range(NTILE):
                r = rows(c)
                if c + 1 < NTILE:
                    keys_and_bias(c + 1)
                dve.wait_ge(g2, c + 1)
                if c < NCH:
                    for a, h2, pt in halves():
                        ins = dve.scalar_tensor_tensor(Cst[pt, a, :], Cst[pt, a, :], glc[pt, a, c:c + 1],
                                                       PS[pt, 7, a * 130 + h2 * 65:a * 130 + h2 * 65 + 65],
                                                       ALU.mult, ALU.add)
                    ins.then_inc(m_state, 1)
                heads4 = lambda bank: PS[0:r, bank, 0:4 * (E + 1)].rearrange("p (h e) -> p h e", e=E + 1)
                link("dve", dve, dve.tensor_tensor(tmpN[0:r], heads4(5), col(c, 0, E + 1), ALU.mult))
                dve.tensor_tensor(nd[0:r], heads4(6), tmpN[0:r], ALU.add).then_inc(m_taken, 1)
                dve.wait_ge(m_taken, c + 1)
                if c + 1 < NTILE:
                    weighted(c + 1)
                else:
                    update(0)
                den = nd[0:r, :, E]
                link("dve", dve, dve.scalar_tensor_tensor(adn[0:r, :], den, -1.0, den, ALU.mult, ALU.max))
                link("dve", dve, dve.tensor_tensor(adn[0:r, :], adn[0:r, :], gcol[0:r, c, 32:36], ALU.max))
                link("dve", dve, dve.reciprocal(adn[0:r, :], adn[0:r, :]))
                link("dve", dve, dve.tensor_tensor(hh[0:r], nd[0:r, :, 0:E],
                                                   adn[0:r, :].unsqueeze(2).to_broadcast([r, HM, E]), ALU.mult))
                gated_head(dve, c, hh[0:r], mo)
                link("dve", dve, dve.tensor_tensor(sq[0:r], hh[0:r], hh[0:r], ALU.mult))
                link("dve", dve, dve.tensor_reduce(hstat[0:r, 0, c, :], sq[0:r], AX.X, ALU.add))
            update(1)

        def gated_head(eng, c, h, gate):
            r = rows(c)
            g = gate[0:r, c, :].rearrange("p (h e) -> p h e", e=E)
            eng.tensor_tensor(g, h, g, ALU.mult)

        NX = NLEV + 1
        X = [view(R_x0, 0, l=NX, a=2, t=P)] + [view(R_d, n * 2304, l=NX, a=2, t=P) for n in range(2)]
        AM = [view(R_d, 4608 + n * 1024, l=NLEV, t=P) for n in range(2)]
        AS = [R_as[:, n * P:(n + 1) * P] for n in range(2)]
        Sst = view(R_d, 6656, a=2, e=E)
        Sss = view(R_d, 6784, b=NB, a=2, e=E)
        kl = [R_d[:, 7808 + n * 256:8064 + n * 256] for n in range(2)]
        lev = view(R_d2, 0, l=NLEV, t=P)
        hqm_flat = [R_d2[:, 1024 + n * 288:1024 + (n + 1) * 288] for n in range(2)]
        klm = view(R_d2, 1600, b=NB, n=256)
        osb = view(R_d2, 3648, h=HM, e=E)
        osq = view(R_d2, 3904, h=HM, e=E)
        tmpS = view(R_d, 0, b=NB, e=E)
        bmask2 = R_d2[0:NS, 4160:4168]
        eb = sb("eb", [P, 2, 2])
        ebs = sb("ebs", [P, 2, NB])
        h_in, h_zero, h_arg, h_exp, h_prod = sem("h_in"), sem("h_zero"), sem("h_arg"), sem("h_exp"), sem("h_prod")
        a_psum, a_masked, kl_psum, kl_taken = sem("a_psum"), sem("a_masked"), sem("kl_psum"), sem("kl_taken")
        ho_psum, ho_copied, ho_taken, h_state = sem("ho_psum"), sem("ho_copied"), sem("ho_taken"), sem("h_state")
        h_masked, hu_psum, h_upd = sem("h_masked"), sem("hu_psum"), sem("h_upd")

        def split(ap, m):
            return ap.rearrange("p a (n z m) -> p a n z m", z=2, m=m)

        def levels_of(c):
            return range(NLEV - 1) if c < NCH else range(NLEV - 3, NLEV - 1)

        def phase_d2_sync(sp):
            sp.dma_start(lev, const("c_levels")).then_inc(h_in, 16)
            sp.dma_start(bmask2, const("c_batch")).then_inc(h_in, 16)
            for a, h2, pt in halves():
                sp.dma_start(Sss[pt, :, a, :], i_["state_hgrn_S"][0, :, 2 * a + h2].rearrange("b k v -> k b v"))\
                  .then_inc(h_in, 16)
            sp.wait_ge(h_state, NCH)
            for a, h2, pt in halves():
                sp.dma_start(o_["p_S"][0, 0, 2 * a + h2], Sst[pt, a, :]).then_inc(st_out, 16)
            sp.wait_ge(ho_psum, NTILE)
            load_w(sp, NW1, NW1 + 3)
            sp.wait_ge(h_upd, 4)
            for a, h2, pt in halves():
                sp.dma_start(o_["s_S"][0, :, 2 * a + h2].rearrange("b k v -> k b v"), Sss[pt, :, a, :]).then_inc(st_out, 16)
            sp.wait_ge(st_out, 16 * 24)

        def operands(pool, first, last):
            for c in range(first, last):
                r, tt = rows(c), tile_tokens(c)
                x = X[c % 3]
                if c >= 3:
                    pool.wait_ge(ho_psum, c - 2)
                b = hb[:, :, tt]
                for l in levels_of(c):
                    m = 64 >> l
                    bb, xx = split(b, m), split(x[:, l, :, 0:r], m)
                    mid = bb[:, :, :, 0, m - 1:m].to_broadcast([P, 2, r // (2 * m), m])
                    pool.tensor_tensor(xx[:, :, :, 1, :], bb[:, :, :, 1, :], mid, ALU.subtract)
                    pool.tensor_tensor(xx[:, :, :, 0, :], mid, bb[:, :, :, 0, :], ALU.subtract)
                pool.tensor_copy(x[:, NLEV - 1, :, 0:r], b)
                seglen = P if c < NCH else NT
                bs = b.rearrange("p a (n s) -> p a n s", s=seglen)
                last = bs[:, :, :, seglen - 1:seglen].to_broadcast([P, 2, r // seglen, seglen])
                pool.tensor_tensor(x[:, NLEV, :, 0:r].rearrange("p a (n s) -> p a n s", s=seglen), last, bs,
                                   ALU.subtract).then_inc(h_arg, 1)
                pool.wait_ge(h_exp, c + 1)
                q, k = hqk[:, 0:2, tt], hqk[:, 2:4, tt]
                for l in levels_of(c):
                    m = 64 >> l
                    xx = split(x[:, l, :, 0:r], m)
                    pool.tensor_tensor(xx[:, :, :, 1, :], xx[:, :, :, 1, :], split(q, m)[:, :, :, 1, :], ALU.mult)
                    pool.tensor_tensor(xx[:, :, :, 0, :], xx[:, :, :, 0, :], split(k, m)[:, :, :, 0, :], ALU.mult)
                pool.tensor_tensor(x[:, NLEV - 1, :, 0:r], x[:, NLEV - 1, :, 0:r], q, ALU.mult)
                pool.tensor_tensor(x[:, NLEV, :, 0:r], x[:, NLEV, :, 0:r], k, ALU.mult).then_inc(h_prod, 1)

        def phase_d1_gps(pool):
            operands(pool, 0, 1)

        def phase_d2_gps(pool):
            operands(pool, 1, 2)
            pool.wait_ge(st_out, 16 * 16)
            operands(pool, 2, NTILE)
            pool.wait_ge(h_prod, NTILE)
            pool.wait_ge(h_zero, 1)
            for a in range(2):
                ins = pool.tensor_copy(masked_q(hqm_flat[a])[1], X[NCH % 3][:, NLEV - 1, a, 0:NS].rearrange("p (b t) -> p b t", t=NT))
            ins.then_inc(h_zero, 1)

        def decays(act, c):
                r = rows(c)
                x = X[c % 3]
                act.wait_ge(h_arg, c + 1)
                l0 = 0 if c < NCH else NLEV - 3
                if c >= 2:
                    act.wait_ge(h_state, c - 1)
                if c < NCH:
                    act.activation(eb[:, :, c % 2:c % 2 + 1], hb[:, :, (c + 1) * P - 1:(c + 1) * P], ACT.Exp)
                else:
                    act.activation(ebs[:, :, :], hb[:, :, S + NT - 1::NT], ACT.Exp)
                act.activation(x[:, l0:, :, 0:r], x[:, l0:, :, 0:r], ACT.Exp).then_inc(h_exp, 1)

        def phase_d2_act(act):
            for c in range(1, NTILE):
                decays(act, c)
                out_copy(act, c - 1)
            out_copy(act, NTILE - 1)

        def out_copy(act, c):
            r = rows(c)
            act.wait_ge(ho_psum, c + 1)
            if c >= 1:
                act.wait_ge(ho_taken, c)
            src = PS[0:r, 4 + c % 2, 0:256].rearrange("p (h e) -> p h e", e=E)
            act.activation(osq[0:r], src, ACT.Square).then_inc(ho_copied, 1)

        def phase_d2_dve(dve):
            dve.wait_ge(h_in, 96)
            for a in range(2):
                link("dve", dve, dve.memset(hqm_flat[a], 0.0))
            link("dve", dve, dve.memset(Sst[:, :, :], 0.0))
            dve.nop().then_inc(h_zero, 1)


            def decayed_scores(c, h):
                r = rows(c)
                j = c * HM + h
                dve.wait_ge(a_psum, j + 1)
                if j >= 2:
                    dve.wait_ge(am_used, j - 1)
                l0 = 0 if c < NCH else NLEV - 3
                src = PS[0:r, 2 * (j % 2):2 * (j % 2) + 2, :].rearrange("p b (l t) -> p (b l) t", t=P)
                link("dve", dve, dve.tensor_tensor(AM[j % 2][0:r, l0:, 0:r], src[:, l0:, 0:r], lev[0:r, l0:, 0:r], ALU.mult))
                dve.tensor_reduce(AS[j % 2][0:r, 0:r], AM[j % 2][0:r, l0:, 0:r].rearrange("p l t -> p t l"), AX.X, ALU.add)\
                   .then_inc(a_masked, 1)

            def state_and_gate(c):
                r = rows(c)
                dve.wait_ge(ho_psum, c + 1)
                if c < NCH:
                    for a, h2, pt in halves():
                        ins = dve.scalar_tensor_tensor(Sst[pt, a, :], Sst[pt, a, :], eb[pt, a, c % 2:c % 2 + 1],
                                                       PS[pt, 7, a * P + h2 * 64:a * P + h2 * 64 + 64], ALU.mult, ALU.add)
                    ins.then_inc(h_state, 1)
                dve.wait_ge(ho_copied, c + 1)
                gated_head(dve, c, PS[0:r, 4 + c % 2, 0:256].rearrange("p (h e) -> p h e", e=E), hg)
                dve.tensor_reduce(hstat[0:r, 1, c, :], osq[0:r], AX.X, ALU.add).then_inc(ho_taken, 1)

            dve.wait_ge(st_out, 16 * 16)
            for c in range(NTILE):
                r = rows(c)
                decayed_scores(c, 0)
                if c:
                    state_and_gate(c - 1)
                decayed_scores(c, 1)
                dve.wait_ge(kl_psum, c + 1)
                dve.tensor_copy(kl[c % 2][0:r, :], PS[0:r, 6, 0:256]).then_inc(kl_taken, 1)
                decayed_scores(c, 2)
                decayed_scores(c, 3)
            dve.wait_ge(kl_taken, NTILE)
            link("dve", dve, dve.tensor_tensor(klm[0:NS], kl[NCH % 2][0:NS, :].unsqueeze(1).to_broadcast([NS, NB, 256]),
                                               bmask2.unsqueeze(2).to_broadcast([NS, NB, 256]), ALU.mult))
            dve.nop().then_inc(h_masked, 1)
            state_and_gate(NTILE - 1)
            for a in range(2):
                if a:
                    dve.wait_ge(hu_psum, 1)
                for h2 in range(2):
                    pt = slice(64 * h2, 64 * h2 + 64)
                    link("dve", dve, dve.tensor_tensor(tmpS[pt], Sss[pt, :, a, :],
                                                       ebs[pt, a, :].unsqueeze(2).to_broadcast([64, NB, E]), ALU.mult))
                    upd = PS[pt, 0:2, :].rearrange("p x (b e) -> p x b e", b=4)[:, :, :, h2 * 64:h2 * 64 + 64]
                    dve.tensor_tensor(Sss[pt, :, a, :].rearrange("p (x y) e -> p x y e", y=4),
                                      tmpS[pt].rearrange("p (x y) e -> p x y e", y=4), upd, ALU.add).then_inc(h_upd, 1)

        am_used, inter_done = sem("am_used"), sem("inter_done")

        def phase_d2_pe(pe):
            def level_scores(c, h):
                r, tt = rows(c), tile_tokens(c)
                j = c * HM + h
                if h == 0:
                    pe.wait_ge(h_prod, c + 1)
                if j >= 2:
                    pe.wait_ge(a_masked, j - 1)
                pt, a = slice(64 * (h % 2), 64 * (h % 2) + 64), h // 2
                x = X[c % 3]
                for l in levels_of(c):
                    pe.matmul(PS[0:r, 2 * (j % 2) + l // 4, (l % 4) * P:(l % 4) * P + r], x[pt, l, a, 0:r], x[pt, l, a, 0:r],
                              start=True, stop=True)
                pe.matmul(PS[0:r, 2 * (j % 2) + 1, 3 * P:3 * P + r], hqk[pt, 2 + a, tt], hqk[pt, a, tt],
                          start=True, stop=True).then_inc(a_psum, 1)

            def apply(c, h):
                r = rows(c)
                j = c * HM + h
                pt, a = slice(64 * (h % 2), 64 * (h % 2) + 64), h // 2
                pe.wait_ge(a_masked, j + 1)
                if h == 0:
                    if c >= 2:
                        pe.wait_ge(ho_taken, c - 1)
                    pe.wait_ge(h_zero, 1)
                    if c >= 1:
                        pe.wait_ge(h_state, c)
                o = PS[0:r, 4 + c % 2, h * E:(h + 1) * E]
                pe.matmul(o, AS[j % 2][0:r, 0:r], hi[0:r, c, h * E:(h + 1) * E], start=True, stop=False).then_inc(am_used, 1)
                if j >= 1:
                    pe.wait_ge(inter_done, j)
                if c < NCH:
                    mm = pe.matmul(o, X[c % 3][pt, NLEV - 1, a, 0:r], Sst[pt, a, :], start=False, stop=True)
                else:
                    pe.wait_ge(h_zero, 2)
                    for b in range(NB):
                        mm = pe.matmul(o, masked_q(hqm_flat[a])[0][pt, b, :], Sss[pt, b, a, :], start=False, stop=(b == NB - 1))
                mm.then_inc(inter_done, 1)

            def keys(c):
                r = rows(c)
                if c >= 1:
                    pe.wait_ge(kl_taken, c)
                for a in range(2):
                    t = pe.transpose(PS[0:r, 6, a * P:(a + 1) * P], X[c % 3][:, NLEV, a, 0:r], ident[:, :])
                t.then_inc(kl_psum, 1)

            pe.wait_ge(h_in, 96)
            level_scores(0, 0)
            for c in range(NTILE):
                r = rows(c)
                level_scores(c, 1)
                keys(c)
                apply(c, 0)
                level_scores(c, 2)
                apply(c, 1)
                level_scores(c, 3)
                apply(c, 2)
                if c + 1 < NTILE:
                    level_scores(c + 1, 0)
                apply(c, 3)
                pe.wait_ge(kl_taken, c + 1)
                if c < NCH:
                    for a in range(2):
                        mm = pe.matmul(PS[:, 7, a * P:(a + 1) * P], kl[c % 2][:, a * P:(a + 1) * P],
                                       hi[:, c, a * P:(a + 1) * P], start=True, stop=True)
                    mm.then_inc(ho_psum, 1)
                else:
                    pe.wait_ge(h_masked, 1)
                    for a in range(2):
                        if a:
                            pe.wait_ge(h_upd, 2)
                        for b in range(NB):
                            mm = pe.matmul(PS[:, b // 4, (b % 4) * P:(b % 4 + 1) * P], klm[0:NS, b, a * P:(a + 1) * P],
                                           hi[0:NS, c, a * P:(a + 1) * P], start=True, stop=True)
                        mm.then_inc(hu_psum if a else ho_psum, 1)

        NFT = 4 * NFAR // P
        NKT = NFT + 4
        NSLOT = 8
        NAHEAD = 5
        cache = [view(r, 0, k=NKT, n=512) for r in R_cache]
        ktile = [view(R_att, 1664 + n * 512, a=4, s=P) for n in range(2)]
        pb = [R_att[:, at:at + NKEY] for at in (2688, 3712)]
        bkey = R_att[:, 4640:4640 + NKEY]
        bother = view(R_att, 5568, g=2, n=NS)
        rexp = R_att[0:33, 5632:6144].rearrange("p (t c) -> p t c", t=NT)
        ptk = view(R_ptk, 0, k=NKT + 1, q=P)
        eout = [R_eout[:, n * 512:(n + 1) * 512] for n in range(2)]
        keyrows = R_keyrows[0:33, :].rearrange("p (t n) -> p t n", t=NT)
        ra = small[0:33, 0:H]
        estat = sb("estat", [P, 2, 8])
        e_in, ra_ready, rexp_ready, bkey_psum, bkey_ready = (sem("e_in"), sem("ra_ready"), sem("rexp_ready"),
                                                             sem("bkey_psum"), sem("bkey_ready"))
        cache_in = [sem(f"cache_in{n}") for n in range(NSLOT)]
        kt_psum, st_psum, sb_psum = sem("kt_psum"), sem("st_psum"), sem("sb_psum")
        kt_taken = [sem("kt_taken_act"), sem("kt_taken_dve")]
        st_taken, e_min, e_exp, p_ready = sem("st_taken"), sem("e_min"), sem("e_exp"), sem("p_ready")
        pk_psum, ptk_ready, ov_psum, ov_taken = sem("pk_psum"), sem("ptk_ready"), sem("ov_psum"), sem("ov_taken")
        eo_psum = sem("eo_psum")
        ITEMS = [("cache_attn_" + kv, b) for kv in "kv" for b in range(NB)]
        NJ = NB * NKT

        def score_banks(B):
            return 2 + 2 * (B % 2)

        def key_bank(B, k):
            return (score_banks(B), k * P) if k < NFT else (score_banks(B) + 1, (k - NFT) * P)

        def item_in(eng, m):
            eng.wait_ge(cache_in[m % NSLOT], 64 * (m // NSLOT + 1))

        def phase_e_sync(sp):
            sp.dma_start(keyrows, const("c_bias_keys")).then_inc(e_in, 16)
            sp.dma_start(ra[0:32, :], i_["rel_bias"]).then_inc(e_in, 16)
            sp.dma_start(bother, const("c_other_batch")).then_inc(e_in, 16)
            load_caches(sp, NAHEAD, NSLOT - 1)
            sp.wait_ge(bkey_psum, 2)
            load_caches(sp, NSLOT - 1, len(ITEMS))
            sp.wait_ge(ov_psum, 4)
            load_chunks(sp, 0, KD)

        def load_caches(sp, first, last):
            for m in range(first, last):
                name, b = ITEMS[m]
                if m >= NSLOT:
                    sp.wait_ge(kt_psum, NKT * (m - NSLOT + 1))
                rows_ = i_[name][0, b].rearrange("s h e -> s (h e)")
                far = rows_[0:FAR, :].rearrange("(c m s) n -> c m s n", s=16, m=P // 4)
                near = rows_[FAR:WB, :].rearrange("(p k) n -> p k n", k=4)
                for c in range(NFT):
                    sp.dma_start(cache[m % NSLOT][:, c, :], far[c, :, 0:4, :]).then_inc(cache_in[m % NSLOT], 16)
                sp.dma_start(cache[m % NSLOT][:, NFT:, :], near).then_inc(cache_in[m % NSLOT], 16)

        def phase_e_pe(pe):
            pe.wait_ge(e_in, 48)
            pe.wait_ge(rexp_ready, 1)
            for n in range(2):
                for t in range(NT):
                    mm = pe.matmul(PS[:, n, 0:NKEY // 2], rexp[:, t, :],
                                   keyrows[:, t, n * (NKEY // 2):(n + 1) * (NKEY // 2)],
                                   start=(t == 0), stop=(t == NT - 1))
                mm.then_inc(bkey_psum, 1)
            pe.wait_ge(bkey_ready, 1)
            for J in range(NJ + 1):
                if J < NJ:
                    B, k = J // NKT, J % NKT
                    if k == 0:
                        item_in(pe, B)
                    if J >= 2:
                        pe.wait_ge(kt_taken[J % 2], J // 2)
                    for a in range(4):
                        t = pe.transpose(PS[:, J % 2, a * P:(a + 1) * P], cache[B % NSLOT][:, k, a * P:(a + 1) * P],
                                         ident[:, :])
                    t.then_inc(kt_psum, 1)
                if J >= 1:
                    B, k = (J - 1) // NKT, (J - 1) % NKT
                    g = B // 4
                    pe.wait_ge(kt_taken[(J - 1) % 2], (J - 1) // 2 + 1)
                    if k == 0 and B >= 2:
                        pe.wait_ge(st_taken, B - 1)
                    bank, at_ = key_bank(B, k)
                    for a in range(4):
                        mm = pe.matmul(PS[:, bank, at_:at_ + P], qblk[:, a, 4 * g:4 * g + 4, :, :].rearrange("p b h t -> p (b h t)"),
                                       ktile[(J - 1) % 2][:, a, :], start=(a == 0), stop=(a == 3))
                    mm.then_inc(st_psum, 1)
                    if k == NKT - 1 and B % 4 == 3:
                        for a in range(4):
                            mm = pe.matmul(PS[:, 6, g * NS:(g + 1) * NS],
                                           qblk[:, a, 4 * g:4 * g + 4, :, :].rearrange("p b h t -> p (b h t)"),
                                           knew[:, a, :], start=(a == 0), stop=(a == 3))
                        mm.then_inc(sb_psum, 1)
            for g in range(2):
                pe.wait_ge(p_ready, g + 1)
                pe.wait_ge(st_taken, NB)
                if g:
                    pe.wait_ge(ptk_ready, g)
                for k in range(NKT + 1):
                    if k < NKT:
                        t = pe.transpose(PS[:, 2 + k // 4, (k % 4) * P:(k % 4 + 1) * P], pb[g][:, k * P:(k + 1) * P], ident[:, :])
                    else:
                        t = pe.transpose(PS[0:NS, 7, 0:P], pb[g][:, k * P:NKEY], ident[:, :])
                t.then_inc(pk_psum, 1)
                pe.wait_ge(ptk_ready, g + 1)
                for b in range(4):
                    item_in(pe, NB + 4 * g + b)
                    v = cache[(NB + 4 * g + b) % NSLOT]
                    if g:
                        pe.wait_ge(ov_taken, b + 1)
                    o = PS[:, OV_BANK[b], :]
                    for k in range(NKT):
                        pe.matmul(o, ptk[:, k, :], v[:, k, :], start=(k == 0), stop=False)
                    pe.matmul(o, ptk[0:NS, NKT, :], vnew[0:NS, :], start=False, stop=True).then_inc(ov_psum, 1)
            for g in range(2):
                pe.wait_ge(ov_taken, 4 * (g + 1))
                for a in range(4):
                    t = pe.transpose(PS[:, 2 + g, a * P:(a + 1) * P], eout[g][:, a * P:(a + 1) * P], ident[:, :])
                t.then_inc(eo_psum, 1)

        OV_BANK = (0, 1, 4, 5)

        def take_kt(eng, copy, J):
            eng.wait_ge(kt_psum, J + 1)
            if J >= 2:
                eng.wait_ge(st_psum, J - 1)
            copy(ktile[J % 2], PS[:, J % 2, :].rearrange("p (a t) -> p a t", t=P)).then_inc(kt_taken[J % 2], 1)

        def phase_e_act(act):
            def exponent(g):
                act.wait_ge(e_min, g + 1)
                act.activation(pb[g], pb[g], ACT.Exp, bias=estat[:, g, 3:4], scale=-1.0,
                               accum_out=estat[:, g, 4:5]).then_inc(e_exp, 1)

            for J in range(0, NJ, 2):
                take_kt(act, lambda o, s: act.activation(o, s, ACT.Copy), J)
                if J == 4 * NKT + 6:
                    exponent(0)
            exponent(1)
            for n in range(NB):
                g, b = n // 4, n % 4
                pt = slice(32 * b, 32 * b + 32)
                act.wait_ge(ov_psum, n + 1)
                act.activation(eout[g][pt, :], PS[pt, OV_BANK[b], :], ACT.Copy).then_inc(ov_taken, 1)

        def phase_e_dve(dve):
            def scores(B):
                g, b = B // 4, B % 4
                pt = slice(32 * b, 32 * b + 32)
                dve.wait_ge(st_psum, NKT * (B + 1))
                for n, (at_, w) in enumerate(((0, NFT * P), (NFT * P, 4 * P))):
                    ins = dve.tensor_tensor_reduce(pb[g][pt, at_:at_ + w], PS[pt, score_banks(B) + n, 0:w], bkey[pt, at_:at_ + w],
                                                   -1.0, 3e38, ALU.add, ALU.min, estat[pt, g, n:n + 1])
                link("dve", dve, ins)
                dve.nop().then_inc(st_taken, 1)

            def minimum(g):
                dve.wait_ge(sb_psum, g + 1)
                link("dve", dve, dve.tensor_tensor_reduce(pb[g][:, NKEY - NS:], PS[:, 6, g * NS:(g + 1) * NS], bother[:, g, :],
                                                          -1.0, 3e38, ALU.add, ALU.min, estat[:, g, 2:3]))
                dve.tensor_reduce(estat[:, g, 3:4], estat[:, g, 0:3], AX.X, ALU.min).then_inc(e_min, 1)

            def normalise(g):
                dve.wait_ge(e_exp, g + 1)
                link("dve", dve, dve.reciprocal(estat[:, g, 5:6], estat[:, g, 4:5]))
                dve.tensor_scalar(pb[g], pb[g], estat[:, g, 5:6], None, ALU.mult).then_inc(p_ready, 1)

            def transposed(g):
                dve.wait_ge(pk_psum, g + 1)
                if g:
                    dve.wait_ge(ov_psum, 4)
                dve.tensor_copy(ptk[:, 0:4, :], PS[:, 2, :].rearrange("p (k q) -> p k q", q=P))
                dve.tensor_copy(ptk[:, 4:NKT, :], PS[:, 3, 0:(NKT - 4) * P].rearrange("p (k q) -> p k q", q=P))
                dve.tensor_copy(ptk[0:NS, NKT, :], PS[0:NS, 7, 0:P]).then_inc(ptk_ready, 1)

            dve.wait_ge(e_in, 48)
            dve.memset(ra[32:33, :], 1.0).then_inc(ra_ready, 1)
            link("dve", dve, dve.memset(rexp, 0.0))
            dve.wait_ge(ra_ready, 1)
            for t in range(NT):
                ins = dve.tensor_copy(rexp[:, t, :].rearrange("p (b h t) -> p b h t", b=4, h=H)[:, :, :, t],
                                      ra.unsqueeze(1).to_broadcast([33, 4, H]))
            ins.then_inc(rexp_ready, 1)
            dve.wait_ge(bkey_psum, 2)
            link("dve", dve, dve.tensor_copy(bkey.rearrange("p (a n) -> p a n", a=2), PS[:, 0:2, 0:NKEY // 2]))
            link("dve", dve, dve.tensor_tensor(bother, bother, bkey[:, NKEY - NS:].unsqueeze(1).to_broadcast([P, 2, NS]), ALU.add))
            dve.nop().then_inc(bkey_ready, 1)
            for J in range(NJ):
                if J % 2:
                    take_kt(dve, dve.tensor_copy, J)
                if J >= NKT and J % NKT == 1:
                    scores(J // NKT - 1)
                if J == 4 * NKT + 3:
                    minimum(0)
                if J == 4 * NKT + 7:
                    normalise(0)
            scores(NB - 1)
            transposed(0)
            minimum(1)
            normalise(1)
            transposed(1)
            for g in range(2):
                dve.wait_ge(eo_psum, g + 1)
                for h2 in range(2):
                    pt = slice(64 * h2, 64 * h2 + 64)
                    for a in range(4):
                        src = PS[pt, 2 + g, a * P:(a + 1) * P].rearrange("p (b h t) -> p b h t", b=4, t=NT)[:, :, 2 * a + h2, :]
                        dve.tensor_copy(atts[pt, a, 16 * g:16 * g + 16].rearrange("p (b t) -> p b t", t=NT), src)

        XH, XL = (view(x, 0, k=KD, t=NTOK) for x in (XH, XL))
        XHf = XH.bitcast(F32)
        x1 = view(R_x1, 0, i=NTILE, n=D)
        WOH = view(R_wo, 0, k=KD, n=D)

        def wo_low(k):
            return R_wo[:, 8192 + k * D:8192 + (k + 1) * D] if k < 4 else R_wo2[:, (k - 4) * D:(k - 3) * D]

        tmp4, tmp4b = ([view(r, at + n * 512, k=4, t=P) for n in range(2)] for r, at in ((R_x1, NCH * D), (R_row, 0)))

        FB = 256
        NF = FB // P
        NBLK = DFF // FB
        wup = i_["w_up"][0].rearrange("(c k p) n -> c p k n", k=4, p=P)
        wdn = i_["w_down"][0].rearrange("(f p) d -> f p d", p=P)
        def at(region, n):
            return region[:, n:n + 1024]

        CHUNKS = [(at(R_wo, k * D), wo_low(k), i_["w_out"][0, k * P:(k + 1) * P, :], at(R_x1, k * D))
                  for k in range(KD)]
        UP_CHUNKS, DOWN_CHUNKS = {}, {}
        for b in range(NBLK):
            UP_CHUNKS[b] = len(CHUNKS)
            for c in range(2):
                high = 2048 * c
                CHUNKS.append((at(R_up[b % 2], high), at(R_up[b % 2], high + 1024), wup[c, :, :, b * FB:(b + 1) * FB],
                               at(R_stage, len(CHUNKS) % 3 * 1024) if b else at(R_first, c * 1024)))
            DOWN_CHUNKS[b] = len(CHUNKS)
            for f in range(NF):
                high = 2048 * f
                CHUNKS.append((at(R_down, high), at(R_down, high + 1024), wdn[NF * b + f],
                               at(R_stage, len(CHUNKS) % 3 * 1024)))
        chunk_in = [sem(f"chunk_in{n}") for n in range(8)]
        NW = len(W_CHUNKS)

        def load_chunks(sp, first, last):
            for m in range(first, last):
                if m >= DOWN_CHUNKS[0]:
                    sp.wait_ge(chunk_split, NW + m - 2)
                src = CHUNKS[m][2]
                dst = CHUNKS[m][3] if len(src.shape) == 2 else CHUNKS[m][3].rearrange("p (k n) -> p k n", k=src.shape[1])
                sp.dma_start(dst, src).then_inc(chunk_in[m % 8], 16)

        def chunk_high_part(act, m):
            act.wait_ge(chunk_in[m % 8], 16 * (m // 8 + 1))
            act.activation(CHUNKS[m][0], CHUNKS[m][3], ACT.Copy).then_inc(chunk_high, 1)

        def chunk_low_part(dve, m):
            dve.wait_ge(chunk_high, NW + m + 1)
            dve.tensor_tensor(CHUNKS[m][1], CHUNKS[m][3], CHUNKS[m][0].bitcast(F32), ALU.subtract).then_inc(chunk_split, 1)

        head_ms, head_rms, f_scaled, f_psum = sem("head_ms"), sem("head_rms"), sem("f_scaled"), sem("f_psum")
        PARTS = ((slice(0, P), slice(0, NCH)), (slice(0, NS), slice(NCH, NTILE)))

        def phase_f1_sync(sp):
            for i in range(NCH):
                sp.wait_ge(chunk_split, NW + i + 1)
                sp.dma_start(x1[:, i, :], i_["x_prompt"][0, i * P:(i + 1) * P, :]).then_inc(x1_in, 16)

        def attended(j):
            return mixa[:, :, tile_tokens(j)] if j < NCH else atts

        def phase_f1_act(act):
            for n, (pt, cs) in enumerate(PARTS):
                act.wait_ge(head_ms, n + 1)
                act.activation(hrstd[pt, :, cs, :], hstat[pt, :, cs, :], ACT.Sqrt).then_inc(head_rms, 1)
            for j in range(NTILE):
                if j < KD:
                    chunk_high_part(act, j)
                ks, ts = half(j, 0)
                act.activation(XH[:, ks, ts], attended(j), ACT.Copy).then_inc(f_high, 1)
            for j in range(NTILE):
                ks, ts = half(j, 1)
                act.wait_ge(f_taken, 2 * NTILE + j + 1)
                act.activation(XH[:, ks, ts], tmp4[j % 2][:, :, 0:rows(j)], ACT.Copy).then_inc(f_high, 1)

        def phase_f1_gps(pool):
            for j in range(NTILE):
                ks, ts = half(j, 0)
                pool.wait_ge(f_high, 2 * NTILE + j + 1)
                pool.tensor_tensor(XL[:, ks, ts], attended(j), XHf[:, ks, ts], ALU.subtract)
            for j in range(NTILE):
                ks, ts = half(j, 1)
                pool.wait_ge(f_high, 3 * NTILE + j + 1)
                pool.tensor_tensor(XL[:, ks, ts], tmp4[j % 2][:, :, 0:rows(j)], XHf[:, ks, ts], ALU.subtract)\
                    .then_inc(f_split, 1)

        def phase_f1_dve(dve):
            for pt, cs in PARTS:
                dve.tensor_scalar(hstat[pt, :, cs, :], hstat[pt, :, cs, :], 1.0 / E, EPS, ALU.mult, ALU.add)\
                   .then_inc(head_ms, 1)
            for n, (pt, cs) in enumerate(PARTS):
                dve.wait_ge(head_rms, n + 1)
                link("dve", dve, dve.reciprocal(hrstd[pt, :, cs, :], hrstd[pt, :, cs, :]))
            for i in range(NTILE + 2):
                if i < NTILE:
                    r = rows(i)
                    for w in range(2):
                        part = (mo, hg)[w][0:r, i, :].rearrange("p (h e) -> p h e", e=E)
                        ins = dve.tensor_tensor(part, part, hrstd[0:r, w, i, :].unsqueeze(2).to_broadcast([r, HM, E]), ALU.mult)
                    ins.then_inc(f_scaled, 1)
                if i == 1:
                    for m in range(KD):
                        chunk_low_part(dve, m)
                if i >= 2:
                    j = i - 2
                    dve.wait_ge(f_psum, j + 1)
                    if j >= 2:
                        dve.wait_ge(f_split, 2 * NTILE + j - 1)
                    dve.tensor_tensor(tmp4[j % 2][:, :, 0:rows(j)], PS[:, j % 2, :].rearrange("p (k t) -> p k t", t=P)[:, :, 0:rows(j)],
                                      gout[:, 4:8].unsqueeze(2).to_broadcast([P, 4, rows(j)]), ALU.mult).then_inc(f_taken, 1)

        def phase_f1_pe(pe):
            for i in range(NTILE):
                r = rows(i)
                pe.wait_ge(f_scaled, i + 1)
                if i >= 2:
                    pe.wait_ge(f_taken, 2 * NTILE + i - 1)
                for k in range(4):
                    t = pe.transpose(PS[:, i % 2, k * P:k * P + r], (mo, hg)[k // 2][0:r, i, k % 2 * P:(k % 2 + 1) * P],
                                     ident[0:r, 0:r])
                t.then_inc(f_psum, 1)
                if i in (3, 6):
                    output_projection(pe, i // 3 - 1)

        def output_projection(pe, i):
            pe.wait_ge(chunk_split, NW + KD)
            pe.wait_ge(f_split, 2 * NTILE + i + 1)
            ts = last_tokens(i)
            for n in range(2):
                ns = slice(n * 512, (n + 1) * 512)
                product(pe, PS[:, 4 + 2 * (i % 2) + n, :], lambda k: (XH[:, k, ts], XL[:, k, ts]),
                        lambda k: (WOH[:, k, ns], wo_low(k)[:, ns]), KD).then_inc(op_psum, 1)

        xs2 = [R_xs2[:, n * D:(n + 1) * D] for n in range(2)]
        x1_in = sem("x1_in")
        op_psum, x1_ready, xs2_ready, xs2_T = sem("op_psum"), sem("x1_ready"), sem("xs2_ready"), sem("xs2_T")

        def phase_f2_sync(sp):
            sp.wait_ge(x1_in, 16 * NCH)
            sp.wait_ge(op_psum, 6)
            sp.dma_start(x1[0:P - NS, NCH, :], i_["x_prompt"][0, S - (P - NS):S, :]).then_inc(x1_in, 16)
            sp.dma_start(x1[P - NS:P, NCH, :], i_["x_sample"].rearrange("b t d -> (b t) d")).then_inc(x1_in, 16)
            load_chunks(sp, UP_CHUNKS[0], UP_CHUNKS[0] + 2)

        def phase_f2_pe(pe):
            pe.wait_ge(f_taken, 3 * NTILE)
            pe.wait_ge(f_split, 3 * NTILE)
            for i in range(2, NTILE + 2):
                if i < NTILE:
                    pe.wait_ge(x1_ready, 2 * (i - 1))
                    output_projection(pe, i)
                if i >= 2:
                    j = i - 2
                    pe.wait_ge(xs2_ready, j + 1)
                    if j >= 2:
                        pe.wait_ge(f_taken, 3 * NTILE + 2 * (j - 1))
                    for k in range(KD):
                        t = pe.transpose(PS[:, 2 * (j % 2) + k // 4, (k % 4) * P:(k % 4 + 1) * P],
                                         xs2[j % 2][:, k * P:(k + 1) * P], ident[:, :])
                        if k % 4 == 3:
                            t.then_inc(xs2_T, 1)

        def phase_f2_act(act):
            for i in range(NTILE + 2):
                if i < NTILE:
                    act.wait_ge(x1_ready, 2 * i + 2)
                    if i >= 2:
                        act.wait_ge(xs2_T, 2 * (i - 1))
                    act.activation(xs2[i % 2], x1[:, i, :], ACT.Square, accum_out=stat[:, 0, i:i + 1]).then_inc(sumsq_ready, 1)
                    act.wait_ge(meansq_ready, NTILE + i + 1)
                    act.activation(stat[:, 2, i:i + 1], stat[:, 1, i:i + 1], ACT.Sqrt).then_inc(rms_ready, 1)
                if i >= 2:
                    j = i - 2
                    act.wait_ge(op_psum, 2 * min(j + 2, NTILE))
                    for kk in range(2):
                        act.wait_ge(f_taken, 3 * NTILE + 2 * j + kk + 1)
                        ks, ts = half(j, kk)
                        act.activation(XH[:, ks, ts], tmp4b[kk][:, :, P - rows(j):], ACT.Copy).then_inc(f_high, 1)
                    if j in (2, 5):
                        chunk_high_part(act, UP_CHUNKS[0] + j // 3)

        def phase_f2_dve(dve):
            dve.wait_ge(x1_in, 16 * NCH)
            for i in range(NTILE + 2):
                if i == NCH:
                    dve.wait_ge(x1_in, 16 * 10)
                if i < NTILE:
                    for n in range(2):
                        dve.wait_ge(op_psum, 2 * i + n + 1)
                        part = x1[:, i, n * 512:(n + 1) * 512]
                        dve.tensor_tensor(part, part, PS[:, 4 + 2 * (i % 2) + n, :], ALU.add).then_inc(x1_ready, 1)
                    dve.wait_ge(sumsq_ready, NTILE + i + 1)
                    dve.tensor_scalar(stat[:, 1, i:i + 1], stat[:, 0, i:i + 1], 1.0 / D, EPS,
                                      ALU.mult, ALU.add).then_inc(meansq_ready, 1)
                    dve.wait_ge(rms_ready, NTILE + i + 1)
                    link("dve", dve, dve.reciprocal(stat[:, 3, i:i + 1], stat[:, 2, i:i + 1]))
                    dve.tensor_scalar(xs2[i % 2], x1[:, i, :], stat[:, 3, i:i + 1], None,
                                      ALU.mult).then_inc(xs2_ready, 1)
                if i >= 2:
                    j = i - 2
                    for kk in range(2):
                        dve.wait_ge(xs2_T, 2 * j + kk + 1)
                        if j:
                            dve.wait_ge(f_split, 3 * NTILE + 2 * j - 1 + kk)
                        src = PS[:, 2 * (j % 2) + kk, :].rearrange("p (k t) -> p k t", t=P)
                        dve.tensor_tensor(tmp4b[kk], src, gffn[:, 4 * kk:4 * kk + 4].unsqueeze(2).to_broadcast([P, 4, P]),
                                          ALU.mult).then_inc(f_taken, 1)
                    for kk in range(2):
                        dve.wait_ge(f_high, 4 * NTILE + 2 * j + kk + 1)
                        ks, ts = half(j, kk)
                        dve.tensor_tensor(XL[:, ks, ts], tmp4b[kk][:, :, P - rows(j):], XHf[:, ks, ts], ALU.subtract)\
                           .then_inc(f_split, 1)
                    if j in (2, 5):
                        chunk_low_part(dve, UP_CHUNKS[0] + j // 3)

        up_w = [view(r, 0, c=2, s=2, k=4, n=FB) for r in R_up]
        down_w = view(R_down, 0, f=NF, s=2, d=D)
        UH, UL = (view(R_u, n * NF * NTOK, f=NF, t=NTOK) for n in range(2))
        UHf = UH.bitcast(F32)
        u_pos = [R_upos[:, n * TG:(n + 1) * TG] for n in range(2)]
        u_sq = [R_usq[:, n * TG:(n + 1) * TG] for n in range(2)]
        grow, sqj3 = R_row, R_junk
        NU = 3 * NF
        ND = 2 * NTILE
        u_psum, u_relu, u_squared, u_high, u_split = (sem("u_psum"), sem("u_relu"), sem("u_squared"), sem("u_high"),
                                                      sem("u_split"))
        d_psum, d_taken = sem("d_psum"), sem("d_taken")
        y_ready, y_stored = sem("y_ready"), sem("y_stored")
        UP_AT, DOWN_AT = {0: 0, 2: 1}, {3: 0, 9: 1}

        def phase_g_sync(sp):
            sp.dma_start(grow, i_["g_final"].rearrange("(o d) -> o d", o=1).to_broadcast([P, D])).then_inc(x1_in, 16)
            load_chunks(sp, DOWN_CHUNKS[0], len(CHUNKS))
            for i in range(NTILE):
                sp.wait_ge(y_ready, i + 1)
                if i < NCH:
                    sp.dma_start(o_["y_p"][0, i * P:(i + 1) * P, :], x1[:, i, :]).then_inc(y_stored, 16)
                else:
                    sp.dma_start(o_["y_s"].rearrange("b t d -> (b t) d"), x1[P - NS:P, i, :]).then_inc(y_stored, 16)
            sp.wait_ge(y_stored, 16 * NTILE)

        def phase_g_pe(pe):
            for b in range(NBLK):
                pe.wait_ge(chunk_split, NW + UP_CHUNKS[b] + 2)
                for u in range(NU):
                    f, g = u // 3, u % 3
                    U = b * NU + u
                    if U >= 4:
                        pe.wait_ge(u_relu, U - 3)
                    fs, ts = slice(f * P, (f + 1) * P), slice(g * TG, (g + 1) * TG)
                    product(pe, PS[:, U % 4, 0:TG], lambda k: (up_w[b % 2][:, k // 4, 0, k % 4, fs], up_w[b % 2][:, k // 4, 1, k % 4, fs]),
                            lambda k: (XH[:, k, ts], XL[:, k, ts]), KD).then_inc(u_psum, 1)
                pe.wait_ge(chunk_split, NW + DOWN_CHUNKS[b] + NF)
                for i in range(NTILE):
                    ts = last_tokens(i)
                    pe.wait_ge(u_split, (b + 1) * NU - 3 + (ts.stop - 1) // TG + 1)
                    for n in range(2):
                        j = b * ND + 2 * i + n
                        if j >= 4:
                            pe.wait_ge(d_taken, j - 3)
                        ns = slice(n * 512, (n + 1) * 512)
                        product(pe, PS[:, 4 + j % 4, :], lambda f: (UH[:, f, ts], UL[:, f, ts]),
                                lambda f: (down_w[:, f, 0, ns], down_w[:, f, 1, ns]), NF).then_inc(d_psum, 1)

        def phase_g_act(act):
            for b in range(NBLK):
                if b:
                    act.wait_ge(d_psum, ND * b)
                for u in range(NU):
                    f, g = u // 3, u % 3
                    U = b * NU + u
                    act.wait_ge(u_relu, U + 1)
                    if U >= 2:
                        act.wait_ge(u_split, U - 1)
                    act.activation(u_sq[U % 2], u_pos[U % 2], ACT.Square).then_inc(u_squared, 1)
                    act.wait_ge(u_squared, U + 1)
                    act.activation(UH[:, f, g * TG:(g + 1) * TG], u_sq[U % 2], ACT.Copy).then_inc(u_high, 1)
                    if u in UP_AT:
                        chunk_high_part(act, DOWN_CHUNKS[b] + UP_AT[u])
                if b + 1 < NBLK:
                    for c in range(2):
                        chunk_high_part(act, UP_CHUNKS[b + 1] + c)
            act.wait_ge(u_psum, NU * NBLK)
            for i in range(NTILE):
                act.wait_ge(d_taken, ((NBLK - 1) * NTILE + i) * 2 + 2)
                act.activation(sqj3, x1[:, i, :], ACT.Square, accum_out=stat[:, 0, i:i + 1]).then_inc(sumsq_ready, 1)
                act.wait_ge(meansq_ready, 2 * NTILE + i + 1)
                act.activation(stat[:, 2, i:i + 1], stat[:, 1, i:i + 1], ACT.Sqrt).then_inc(rms_ready, 1)

        def phase_g_dve(dve):
            def final(i):
                dve.wait_ge(sumsq_ready, 2 * NTILE + i + 1)
                dve.tensor_scalar(stat[:, 1, i:i + 1], stat[:, 0, i:i + 1], 1.0 / D, EPS,
                                  ALU.mult, ALU.add).then_inc(meansq_ready, 1)
                dve.wait_ge(rms_ready, 2 * NTILE + i + 1)
                link("dve", dve, dve.reciprocal(stat[:, 3, i:i + 1], stat[:, 2, i:i + 1]))
                dve.scalar_tensor_tensor(x1[:, i, :], x1[:, i, :], stat[:, 3, i:i + 1], grow,
                                         ALU.mult, ALU.mult).then_inc(y_ready, 1)

            def piece_low(U):
                f, g = U % NU // 3, U % 3
                dve.wait_ge(u_high, U + 1)
                dve.tensor_tensor(UL[:, f, g * TG:(g + 1) * TG], u_sq[U % 2], UHf[:, f, g * TG:(g + 1) * TG],
                                  ALU.subtract).then_inc(u_split, 1)

            dve.wait_ge(x1_in, 16 * 11)
            for b in range(NBLK):
                for u in range(NU):
                    U = b * NU + u
                    dve.wait_ge(u_psum, U + 1)
                    if U >= 2:
                        dve.wait_ge(u_squared, U - 1)
                    dve.tensor_scalar(u_pos[U % 2], PS[:, U % 4, 0:TG], 0.0, None, ALU.max).then_inc(u_relu, 1)
                    if u:
                        piece_low(U - 1)
                    if u - 1 in UP_AT:
                        chunk_low_part(dve, DOWN_CHUNKS[b] + UP_AT[u - 1])
                piece_low(b * NU + NU - 1)
                for m in range(ND):
                    i, n = m // 2, m % 2
                    j = b * ND + m
                    dve.wait_ge(d_psum, j + 1)
                    part = x1[:, i, n * 512:(n + 1) * 512]
                    dve.tensor_tensor(part, part, PS[:, 4 + j % 4, :], ALU.add).then_inc(d_taken, 1)
                    if b + 1 < NBLK and m in DOWN_AT:
                        chunk_low_part(dve, UP_CHUNKS[b + 1] + DOWN_AT[m])
                    if b == NBLK - 1 and n and i:
                        final(i - 1)
            final(NTILE - 1)


        PHASES = {
            "sync": [phase_a_sync, phase_b1_sync, phase_d1_sync, phase_d2_sync, phase_b2_sync, phase_c_sync,
                     phase_e_sync, phase_f1_sync, phase_f2_sync, phase_g_sync],
            "gps": [phase_a_gps, phase_b1_gps, phase_d1_gps, phase_d2_gps, phase_b2_gps, None, None, phase_f1_gps, None, None],
            "act": [phase_a_act, phase_b1_act, phase_d1_act, phase_d2_act, phase_b2_act, phase_c_act,
                    phase_e_act, phase_f1_act, phase_f2_act, phase_g_act],
            "dve": [phase_a_dve, phase_b1_dve, phase_d1_dve, phase_d2_dve, phase_b2_dve, phase_c_dve,
                    phase_e_dve, phase_f1_dve, phase_f2_dve, phase_g_dve],
            "pe": [phase_a_pe, phase_b1_pe, phase_d1_pe, phase_d2_pe, phase_b2_pe, phase_c_pe,
                   phase_e_pe, phase_f1_pe, phase_f2_pe, phase_g_pe],
        }

        def run(eng, name):
            for n, f in enumerate(PHASES[name]):
                if f is not None:
                    f(eng)
                if n != 7:
                    barrier(eng, name)

        @block.sync
        def _(sp):
            run(sp, "sync")

        @block.gpsimd
        def _(pool):
            run(pool, "gps")

        @block.scalar
        def _(act):
            run(act, "act")

        @block.vector
        def _(dve):
            run(dve, "dve")

        @block.tensor
        def _(pe):
            run(pe, "pe")


OUTPUTS = {
    "y_p": (1, S, D), "y_s": (NB, NT, D), "p_k": (1, 1, S, H, E), "p_v": (1, 1, S, H, E), "p_conv": (1, 1, 3, 512),
    "p_C": (1, 1, HM, E, E), "p_n": (1, 1, HM, E), "p_m": (1, 1, HM), "p_S": (1, 1, HM, E, E),
    "s_k": (1, NB, NT, H, E), "s_v": (1, NB, NT, H, E), "s_conv": (1, NB, 3, 512), "s_C": (1, NB, HM, E, E),
    "s_n": (1, NB, HM, E), "s_m": (1, NB, HM), "s_S": (1, NB, HM, E, E),
}
INPUTS = ["x_prompt", "x_sample", "cache_attn_k", "cache_attn_v", "state_mlstm_conv", "state_mlstm_C", "state_mlstm_n",
          "state_mlstm_m", "state_hgrn_S", "rel_bias", "g_mix", "w_in", "mlstm_gate_b", "mlstm_conv_w", "mlstm_norm_g",
          "hgrn_lb_raw", "hgrn_norm_g", "w_out", "g_ffn", "w_up", "w_down", "g_final"]


def kernel(**inputs):
    import numpy as _np
    import concourse.bacc as _bacc
    from concourse import mybir as _mybir
    from concourse.bass_utils import run_bass_kernel_spmd as _run

    nc = _bacc.Bacc("TRN2", target_bir_lowering=False, num_devices=1)
    arrays = {f"in_{n}": _np.ascontiguousarray(inputs[n]) for n in INPUTS}
    arrays.update({f"in_{n}": a for n, a in constants().items()})
    i_ = {n[3:]: nc.dram_tensor(n, a.shape, _mybir.dt.from_np(a.dtype), kind="ExternalInput").ap()
          for n, a in arrays.items()}
    o_ = {n: nc.dram_tensor(f"out_{n}", shape, _mybir.dt.float32, kind="ExternalOutput").ap()
          for n, shape in OUTPUTS.items()}
    program(nc, i_, o_)
    r = _run(nc, [arrays], core_ids=[0])
    return tuple(r.results[0][f"out_{n}"] for n in OUTPUTS)
```
